# Optimizing a Trainium2 kernel written in Bass

```python
import jax, jax.numpy as jnp
from jax import lax
import numpy as np
import math

D_MODEL = 1024
BATCH = 1
SEQ = 256
DEPTH = 2

CTX_LEN = 256
GRID_W = 64
N_MIXERS = 2
EXPAND = 2
D_INNER = EXPAND * D_MODEL
MLSTM_HEADS = 4
MLSTM_HEAD_DIM = D_INNER // MLSTM_HEADS
CHUNK = 64
CONV_K = 3
FOURIER_GROUPS = 8
FOURIER_GROUP_DIM = D_INNER // FOURIER_GROUPS
N_MLSTM_LAYERS = (DEPTH + 1) // 2
N_FOURIER_LAYERS = DEPTH // 2
LAST_MLSTM = ((DEPTH - 1) // N_MIXERS) * N_MIXERS
EPS = 1e-6


H = MLSTM_HEADS
DH = MLSTM_HEAD_DIM

def rmsnorm(x, g):
    xf = x.astype(jnp.float32)
    y = xf * lax.rsqrt(jnp.mean(xf * xf, axis=-1, keepdims=True) + EPS)
    return (y * g.astype(jnp.float32)).astype(x.dtype)

def mlstm_chunk_scan(q, k, v, li, lf, state, emit):
    b, h, n, d = q.shape
    nc = n // CHUNK

    def to_chunks(a):
        a = a.reshape(b, h, nc, CHUNK, *a.shape[3:])
        return jnp.moveaxis(a, 2, 0)

    lower = jnp.tril(jnp.ones((CHUNK, CHUNK), dtype=bool))

    def step(carry, inp):
        C, nv, m = carry
        qc, kc, vc, lic, lfc = inp
        bcum = jnp.cumsum(lfc, axis=-1)
        logw = bcum[..., :, None] - bcum[..., None, :] + lic[..., None, :]
        logw = jnp.where(lower, logw, -jnp.inf)
        log_prev = bcum + m[..., None]
        m_new = jnp.maximum(log_prev, jnp.max(logw, axis=-1))
        w_intra = jnp.exp(logw - m_new[..., None])
        w_prev = jnp.exp(log_prev - m_new)
        out = None
        if emit:
            scores = jnp.einsum('bhjd,bhsd->bhjs', qc, kc) * w_intra
            num = jnp.einsum('bhjs,bhsd->bhjd', scores, vc) + \
                w_prev[..., None] * jnp.einsum('bhvk,bhjk->bhjv', C, qc)
            den = jnp.sum(scores, axis=-1) + w_prev * jnp.einsum('bhk,bhjk->bhj', nv, qc)
            out = num / jnp.maximum(jnp.abs(den), jnp.exp(-m_new))[..., None]
        m_end = m_new[..., -1]
        w_src = jnp.exp(bcum[..., -1:] - bcum + lic - m_end[..., None])
        decay = jnp.exp(bcum[..., -1] + m - m_end)
        C_new = decay[..., None, None] * C + jnp.einsum('bhsv,bhsk->bhvk', w_src[..., None] * vc, kc)
        n_new = decay[..., None] * nv + jnp.einsum('bhs,bhsk->bhk', w_src, kc)
        return (C_new, n_new, m_end), out

    state, hs = lax.scan(step, state, tuple(to_chunks(a) for a in (q, k, v, li, lf)))
    if emit:
        hs = jnp.moveaxis(hs, 0, 2).reshape(b, h, n, d)
    return hs, state

def mlstm_inputs(hmod, grid_rows, grid_cols, w_in, conv_w, conv_b, w_q, w_k, w_if, b_i, b_f):
    b, n, _ = hmod.shape
    xm, o_pre, z = jnp.split(hmod @ w_in, 3, axis=-1)
    xg = xm.reshape(b, grid_rows, grid_cols, D_INNER)
    xconv = lax.conv_general_dilated(xg, conv_w, (1, 1), 'SAME',
                                     dimension_numbers=('NHWC', 'HWIO', 'NHWC'),
                                     feature_group_count=D_INNER)
    xconv = jax.nn.silu(xconv.reshape(b, n, D_INNER) + conv_b)
    xh = xconv.reshape(b, n, H, DH)
    q = jnp.einsum('bnhd,hde->bhne', xh, w_q).astype(jnp.float32)
    k = (jnp.einsum('bnhd,hde->bhne', xh, w_k) * (DH ** -0.5)).astype(jnp.float32)
    v = xm.reshape(b, n, H, DH).transpose(0, 2, 1, 3).astype(jnp.float32)
    wq_g = w_if[:, 0].reshape(2, H, DH, 2 * H).astype(jnp.float32)
    wk_g = w_if[:, 1].reshape(2, H, DH, 2 * H).astype(jnp.float32)
    wv_g = w_if[:, 2].reshape(2, H, DH, 2 * H).astype(jnp.float32)
    gates = (jnp.einsum('bhne,rheg->rbng', q, wq_g) + jnp.einsum('bhne,rheg->rbng', k, wk_g)
             + jnp.einsum('bhne,rheg->rbng', v, wv_g))
    li = gates[..., :H] + b_i.astype(jnp.float32)[:, None, None, :]
    lf = jax.nn.log_sigmoid(gates[..., H:] + b_f.astype(jnp.float32)[:, None, None, :])
    li = jnp.moveaxis(li, -1, 2)
    lf = jnp.moveaxis(lf, -1, 2)
    return (q, k, v, li, lf), o_pre, z, xconv

def mlstm_output(hsum, o_pre, z, xconv, ln_w, skip, w_out, dtype):
    b, _, n, _ = hsum.shape
    hh = hsum.transpose(0, 2, 1, 3)
    mu = jnp.mean(hh, axis=-1, keepdims=True)
    var = jnp.mean(jnp.square(hh - mu), axis=-1, keepdims=True)
    hn = ((hh - mu) * lax.rsqrt(var + EPS)).reshape(b, n, D_INNER) * ln_w.astype(jnp.float32)
    hn = jax.nn.sigmoid(o_pre.astype(jnp.float32)) * hn
    y = (hn.astype(dtype) + skip * xconv) * jax.nn.silu(z)
    return y @ w_out

def mlstm_branch(h_lat, h_ctx, rows, emit_ctx, w_in, conv_w, conv_b, w_q, w_k, w_if,
                 b_i, b_f, ln_w, skip, w_out):
    lat, o_l, z_l, xc_l = mlstm_inputs(h_lat, rows, GRID_W, w_in, conv_w, conv_b, w_q, w_k, w_if, b_i, b_f)
    ctx, o_c, z_c, xc_c = mlstm_inputs(h_ctx, 1, h_ctx.shape[1], w_in, conv_w, conv_b, w_q, w_k, w_if, b_i, b_f)
    b = h_lat.shape[0]
    zero = (jnp.zeros((b, H, DH, DH), jnp.float32), jnp.zeros((b, H, DH), jnp.float32),
            jnp.zeros((b, H), jnp.float32))
    h_lat_sum = 0.0
    h_ctx_sum = 0.0
    for r, rev in ((0, False), (1, True)):
        fl = (lambda a: jnp.flip(a, 2)) if rev else (lambda a: a)
        qc, kc, vc, lic, lfc = ctx
        ql, kl, vl, lil, lfl = lat
        hc, st = mlstm_chunk_scan(fl(qc), fl(kc), fl(vc), fl(lic[r]), fl(lfc[r]), zero, emit_ctx)
        hl, _ = mlstm_chunk_scan(fl(ql), fl(kl), fl(vl), fl(lil[r]), fl(lfl[r]), st, True)
        h_lat_sum = h_lat_sum + fl(hl)
        if emit_ctx:
            h_ctx_sum = h_ctx_sum + fl(hc)
    y_lat = mlstm_output(h_lat_sum, o_l, z_l, xc_l, ln_w, skip, w_out, h_lat.dtype)
    y_ctx = mlstm_output(h_ctx_sum, o_c, z_c, xc_c, ln_w, skip, w_out, h_ctx.dtype) if emit_ctx else None
    return y_lat, y_ctx

def fourier_branch(hmod, w_in, w_out):
    b, n, _ = hmod.shape
    u, z = jnp.split(hmod @ w_in, 2, axis=-1)
    ug = u.astype(jnp.float32).reshape(b, n, FOURIER_GROUPS, FOURIER_GROUP_DIM)
    f = jnp.fft.fft2(ug, axes=(1, 3), norm='ortho').real
    y = f.reshape(b, n, D_INNER).astype(hmod.dtype) * jax.nn.silu(z)
    return y @ w_out

def first_inputs(seed: int = 0) -> dict:
    key = jax.random.key(seed)
    ks = jax.random.split(key, 24)
    nA, nB, E = N_MLSTM_LAYERS, N_FOURIER_LAYERS, D_INNER
    nrm = jax.random.normal
    return {
        "x": nrm(ks[0], (BATCH, SEQ, D_MODEL), jnp.float32),
        "c": nrm(ks[1], (BATCH, D_MODEL), jnp.float32),
        "ctx": nrm(ks[2], (BATCH, CTX_LEN, D_MODEL), jnp.float32),
        "c_ctx": nrm(ks[3], (D_MODEL,), jnp.float32),
        "norm_g": 1.0 + 0.1 * nrm(ks[4], (DEPTH, D_MODEL), jnp.float32),
        "w_ada": nrm(ks[5], (DEPTH, D_MODEL, 3 * D_MODEL), jnp.float32) * D_MODEL ** -0.5,
        "b_ada": 0.02 * nrm(ks[6], (DEPTH, 3 * D_MODEL), jnp.float32),
        "m_w_in": nrm(ks[7], (nA, D_MODEL, 3 * E), jnp.float32) * D_MODEL ** -0.5,
        "m_conv_w": nrm(ks[8], (nA, CONV_K, CONV_K, 1, E), jnp.float32) / CONV_K,
        "m_conv_b": 0.02 * nrm(ks[9], (nA, E), jnp.float32),
        "m_w_q": nrm(ks[10], (nA, H, DH, DH), jnp.float32) * DH ** -0.5,
        "m_w_k": nrm(ks[11], (nA, H, DH, DH), jnp.float32) * DH ** -0.5,
        "m_w_if": nrm(ks[12], (nA, 2, 3, E, 2 * H), jnp.float32) * (3 * E) ** -0.5,
        "m_b_i": 0.1 * nrm(ks[13], (nA, 2, H), jnp.float32),
        "m_b_f": jnp.linspace(3.0, 6.0, H, dtype=jnp.float32) + 0.1 * nrm(ks[14], (nA, 2, H), jnp.float32),
        "m_ln_w": 1.0 + 0.1 * nrm(ks[15], (nA, E), jnp.float32),
        "m_skip": 1.0 + 0.1 * nrm(ks[16], (nA, E), jnp.float32),
        "m_w_out": nrm(ks[17], (nA, E, D_MODEL), jnp.float32) * E ** -0.5,
        "f_w_in": nrm(ks[18], (nB, D_MODEL, 2 * E), jnp.float32) * D_MODEL ** -0.5,
        "f_w_out": nrm(ks[19], (nB, E, D_MODEL), jnp.float32) * E ** -0.5,
        "norm_f": 1.0 + 0.1 * nrm(ks[20], (D_MODEL,), jnp.float32),
    }

def first_block(x, c, ctx, c_ctx, norm_g, w_ada, b_ada, m_w_in, m_conv_w, m_conv_b, m_w_q, m_w_k,
              m_w_if, m_b_i, m_b_f, m_ln_w, m_skip, m_w_out, f_w_in, f_w_out, norm_f):
    rows = x.shape[1] // GRID_W
    xc = ctx
    sc_lat = jax.nn.silu(c)
    sc_ctx = jax.nn.silu(c_ctx)
    for i in range(DEPTH):
        j = i // N_MIXERS
        update_ctx = i < LAST_MLSTM
        sh, sc, g = jnp.split(sc_lat @ w_ada[i] + b_ada[i], 3, axis=-1)
        h = rmsnorm(x, norm_g[i]) * (1.0 + sc[:, None, :]) + sh[:, None, :]
        need_ctx_in = update_ctx or (i % N_MIXERS == 0)
        if need_ctx_in:
            shc, scc, gc = jnp.split(sc_ctx @ w_ada[i] + b_ada[i], 3, axis=-1)
            hc = rmsnorm(xc, norm_g[i]) * (1.0 + scc) + shc
        if i % N_MIXERS == 0:
            y, yc = mlstm_branch(h, hc, rows, update_ctx, m_w_in[j], m_conv_w[j], m_conv_b[j],
                                 m_w_q[j], m_w_k[j], m_w_if[j], m_b_i[j], m_b_f[j],
                                 m_ln_w[j], m_skip[j], m_w_out[j])
        else:
            y = fourier_branch(h, f_w_in[j], f_w_out[j])
            yc = fourier_branch(hc, f_w_in[j], f_w_out[j]) if update_ctx else None
        x = x + g[:, None, :] * y
        if update_ctx:
            xc = xc + gc * yc
    return rmsnorm(x, norm_f)


N_EVEN = (DEPTH + 1) // 2
N_ODD = DEPTH // 2

D_A = D_MODEL // 2
A_CONV = 3
D_B = D_MODEL // 2
POOL_WINDOWS = (2, 4, 8, 16)
POOL_GROUPS = len(POOL_WINDOWS)
POOL_GC = D_B // POOL_GROUPS
EV_IN = 3 * D_A + D_B
EV_MIX = D_A + D_B

D_C = D_MODEL // 2
HEAD_DIM = 64
H_C = D_C // HEAD_DIM
Q_BLOCK = 128
D_D = D_MODEL // 2
D_CONV = 31
OD_IN = 3 * D_C + H_C + 2 * D_D
OD_MIX = D_C + D_D

D_FF = int(math.ceil((8 * D_MODEL / 3) / 256) * 256)

ALPHA = (2.0 * DEPTH) ** 0.25
BETA = (8.0 * DEPTH) ** -0.25
LN_EPS = 1e-5


def layer_norm(x, g, b):
    x32 = x.astype(jnp.float32)
    mu = jnp.mean(x32, axis=-1, keepdims=True)
    var = jnp.mean(jnp.square(x32 - mu), axis=-1, keepdims=True)
    y = (x32 - mu) * lax.rsqrt(var + LN_EPS)
    return (y * g.astype(jnp.float32) + b.astype(jnp.float32)).astype(x.dtype)

def causal_dwconv(x, w):
    k = w.shape[0]
    return lax.conv_general_dilated(
        x, w[:, None, :].astype(x.dtype), window_strides=(1,), padding=[(k - 1, 0)],
        dimension_numbers=("NWC", "WIO", "NWC"), feature_group_count=x.shape[-1])

def short_gated_conv(p_a, conv_w):
    b_gate = p_a[..., :D_A]
    c_gate = p_a[..., D_A:2 * D_A]
    val = p_a[..., 2 * D_A:]
    return b_gate * causal_dwconv(c_gate * val, conv_w)

def multiscale_pool(u, w_grp, scale):
    bsz, s, _ = u.shape
    u32 = u.astype(jnp.float32).reshape(bsz, s, POOL_GROUPS, POOL_GC)
    cs = jnp.cumsum(u32, axis=1)
    pos = jnp.arange(s)
    pooled = []
    for g, win in enumerate(POOL_WINDOWS):
        c = cs[:, :, g]
        lagged = jnp.pad(c, ((0, 0), (win, 0), (0, 0)))[:, :s]
        cnt = jnp.minimum(pos + 1, win).astype(jnp.float32)[None, :, None]
        pooled.append((c - lagged) / cnt)
    pooled = (jnp.stack(pooled, axis=2) - u32).astype(u.dtype)
    y = jnp.einsum("bsgc,gcd->bsgd", pooled, w_grp).reshape(bsz, s, D_B)
    return y * scale

def forgetting_attention(q, k, v, log_f):
    s_len = q.shape[1]
    cum = jnp.cumsum(log_f.astype(jnp.float32), axis=1).transpose(0, 2, 1)
    scale = 1.0 / math.sqrt(HEAD_DIM)
    outs = []
    for blk in range(s_len // Q_BLOCK):
        q0, q1 = blk * Q_BLOCK, (blk + 1) * Q_BLOCK
        logits = jnp.einsum("bqhd,bkhd->bhqk", q[:, q0:q1], k[:, :q1]).astype(jnp.float32) * scale
        logits = logits + cum[:, :, q0:q1, None] - cum[:, :, None, :q1]
        mask = jnp.arange(q0, q1)[:, None] >= jnp.arange(q1)[None, :]
        logits = jnp.where(mask[None, None], logits, -1e30)
        probs = jax.nn.softmax(logits, axis=-1).astype(v.dtype)
        outs.append(jnp.einsum("bhqk,bkhd->bqhd", probs, v[:, :q1]))
    return jnp.concatenate(outs, axis=1)

def conformer_conv(p_d, dw_w, dw_b, cn_g, cn_b):
    h = p_d[..., :D_D] * jax.nn.sigmoid(p_d[..., D_D:])
    h = causal_dwconv(h, dw_w) + dw_b
    h = layer_norm(h, cn_g, cn_b)
    return jax.nn.silu(h)

def even_mixer(x, w_in, conv_w, pool_w, pool_scale, w_out):
    p = x @ w_in
    y_a = short_gated_conv(p[..., :3 * D_A], conv_w)
    y_b = multiscale_pool(p[..., 3 * D_A:], pool_w, pool_scale)
    return jnp.concatenate([y_a, y_b], axis=-1) @ w_out

def odd_mixer(x, w_in, forget_b, dw_w, dw_b, cn_g, cn_b, w_out):
    bsz, s, _ = x.shape
    p = x @ w_in
    q = p[..., :D_C].reshape(bsz, s, H_C, HEAD_DIM)
    k = p[..., D_C:2 * D_C].reshape(bsz, s, H_C, HEAD_DIM)
    v = p[..., 2 * D_C:3 * D_C].reshape(bsz, s, H_C, HEAD_DIM)
    log_f = jax.nn.log_sigmoid((p[..., 3 * D_C:3 * D_C + H_C] + forget_b).astype(jnp.float32))
    y_c = forgetting_attention(q, k, v, log_f).reshape(bsz, s, D_C)
    y_d = conformer_conv(p[..., 3 * D_C + H_C:], dw_w, dw_b, cn_g, cn_b)
    return jnp.concatenate([y_c, y_d], axis=-1) @ w_out

def swiglu(x, w_in, w_out):
    h = x @ w_in
    return (jax.nn.silu(h[..., :D_FF]) * h[..., D_FF:]) @ w_out

def second_inputs(seed: int = 0) -> dict:
    key = jax.random.key(seed)
    ks = jax.random.split(key, 24)
    f32 = jnp.float32
    nrm = lambda k, shape, s: jax.random.normal(k, shape, f32) * s
    x = jax.random.normal(ks[0], (BATCH, SEQ, D_MODEL), f32)
    ev_w_in = nrm(ks[1], (N_EVEN, D_MODEL, EV_IN), D_MODEL ** -0.5)
    ev_conv_w = nrm(ks[2], (N_EVEN, A_CONV, D_A), A_CONV ** -0.5)
    ev_pool_w = nrm(ks[3], (N_EVEN, POOL_GROUPS, POOL_GC, POOL_GC), POOL_GC ** -0.5)
    ev_pool_scale = 1.0 + nrm(ks[4], (N_EVEN, D_B), 0.1)
    ev_w_out = nrm(ks[5], (N_EVEN, EV_MIX, D_MODEL), EV_MIX ** -0.5 * BETA)
    col_scale = jnp.ones((OD_IN,), f32).at[2 * D_C:3 * D_C].set(BETA)
    od_w_in = nrm(ks[6], (N_ODD, D_MODEL, OD_IN), D_MODEL ** -0.5) * col_scale
    od_forget_b = jax.random.uniform(ks[7], (N_ODD, H_C), f32, 1.0, 4.0)
    od_dw_w = nrm(ks[8], (N_ODD, D_CONV, D_D), D_CONV ** -0.5)
    od_dw_b = nrm(ks[9], (N_ODD, D_D), 0.02)
    od_cn_g = 1.0 + nrm(ks[10], (N_ODD, D_D), 0.05)
    od_cn_b = nrm(ks[11], (N_ODD, D_D), 0.02)
    od_w_out = nrm(ks[12], (N_ODD, OD_MIX, D_MODEL), OD_MIX ** -0.5 * BETA)
    ln_mix_g = 1.0 + nrm(ks[13], (DEPTH, D_MODEL), 0.05)
    ln_mix_b = nrm(ks[14], (DEPTH, D_MODEL), 0.02)
    ln_ffn_g = 1.0 + nrm(ks[15], (DEPTH, D_MODEL), 0.05)
    ln_ffn_b = nrm(ks[16], (DEPTH, D_MODEL), 0.02)
    ffn_w_in = nrm(ks[17], (DEPTH, D_MODEL, 2 * D_FF), D_MODEL ** -0.5)
    ffn_w_out = nrm(ks[18], (DEPTH, D_FF, D_MODEL), D_FF ** -0.5 * BETA)
    return {"x": x, "ev_w_in": ev_w_in, "ev_conv_w": ev_conv_w, "ev_pool_w": ev_pool_w,
            "ev_pool_scale": ev_pool_scale, "ev_w_out": ev_w_out, "od_w_in": od_w_in,
            "od_forget_b": od_forget_b, "od_dw_w": od_dw_w, "od_dw_b": od_dw_b,
            "od_cn_g": od_cn_g, "od_cn_b": od_cn_b, "od_w_out": od_w_out,
            "ln_mix_g": ln_mix_g, "ln_mix_b": ln_mix_b, "ln_ffn_g": ln_ffn_g,
            "ln_ffn_b": ln_ffn_b, "ffn_w_in": ffn_w_in, "ffn_w_out": ffn_w_out}

def second_block(x, ev_w_in, ev_conv_w, ev_pool_w, ev_pool_scale, ev_w_out, od_w_in,
              od_forget_b, od_dw_w, od_dw_b, od_cn_g, od_cn_b, od_w_out,
              ln_mix_g, ln_mix_b, ln_ffn_g, ln_ffn_b, ffn_w_in, ffn_w_out):
    for layer in range(DEPTH):
        i = layer // 2
        if layer % 2 == 0:
            mix = even_mixer(x, ev_w_in[i], ev_conv_w[i], ev_pool_w[i], ev_pool_scale[i], ev_w_out[i])
        else:
            mix = odd_mixer(x, od_w_in[i], od_forget_b[i], od_dw_w[i], od_dw_b[i],
                            od_cn_g[i], od_cn_b[i], od_w_out[i])
        x = layer_norm(ALPHA * x + mix, ln_mix_g[layer], ln_mix_b[layer])
        x = layer_norm(ALPHA * x + swiglu(x, ffn_w_in[layer], ffn_w_out[layer]),
                       ln_ffn_g[layer], ln_ffn_b[layer])
    return x


def setup_inputs(seed=0):
    out = dict(first_inputs(seed))
    for name, value in second_inputs(seed + 1).items():
        if name != "x":
            out[name + "_2"] = value
    return out


def reference(
    x, c, ctx, c_ctx, norm_g, w_ada, b_ada, m_w_in, m_conv_w, m_conv_b, m_w_q, m_w_k, m_w_if,
    m_b_i, m_b_f, m_ln_w, m_skip, m_w_out, f_w_in, f_w_out, norm_f, ev_w_in_2, ev_conv_w_2,
    ev_pool_w_2, ev_pool_scale_2, ev_w_out_2, od_w_in_2, od_forget_b_2, od_dw_w_2, od_dw_b_2,
    od_cn_g_2, od_cn_b_2, od_w_out_2, ln_mix_g_2, ln_mix_b_2, ln_ffn_g_2, ln_ffn_b_2,
    ffn_w_in_2, ffn_w_out_2,
):
    x = first_block(
        x, c, ctx, c_ctx, norm_g, w_ada, b_ada, m_w_in, m_conv_w, m_conv_b, m_w_q, m_w_k,
        m_w_if, m_b_i, m_b_f, m_ln_w, m_skip, m_w_out, f_w_in, f_w_out, norm_f,
    )
    return second_block(
        x, ev_w_in_2, ev_conv_w_2, ev_pool_w_2, ev_pool_scale_2, ev_w_out_2, od_w_in_2,
        od_forget_b_2, od_dw_w_2, od_dw_b_2, od_cn_g_2, od_cn_b_2, od_w_out_2, ln_mix_g_2,
        ln_mix_b_2, ln_ffn_g_2, ln_ffn_b_2, ffn_w_in_2, ffn_w_out_2,
    )


_drawn_inputs = setup_inputs


def setup_inputs(seed=0):
    import zlib

    import numpy as np

    out = dict(_drawn_inputs(seed))
    spreads = {}
    factors = {'m_conv_b': 2.893,
     'm_b_i': 21.848,
     'od_forget_b_2': 39.488,
     'od_dw_b_2': 8.0,
     'od_cn_g_2': 6.015,
     'od_cn_b_2': 21.749}
    for name, (base, spread) in spreads.items():
        noise = np.random.default_rng([zlib.crc32(name.encode()), seed]).standard_normal(out[name].shape)
        drawn = base * np.exp(spread * noise) if base else spread * noise
        out[name] = __import__('jax').numpy.asarray(drawn.astype(out[name].dtype))
    for name, factor in factors.items():
        out[name] = (out[name] * factor).astype(out[name].dtype)
    return out
```

```python
from contextlib import ExitStack

import numpy as np

import concourse.bass as bass
from concourse import mybir

F32 = mybir.dt.float32
ALU = mybir.AluOpType
ACT = mybir.ActivationFunctionType
AX = mybir.AxisListType

P = 128
D = 1024
KD = D // P
SEQ = 256
CTX = 256
TOK = CTX + SEQ
E = 2048
KE = E // P
HEADS = 4
DH = E // HEADS
HC = DH // P
GRID = 64
ROWS = SEQ // GRID
GROUPS = 8
GD = E // GROUPS
FF = 2816
KF = FF // P
HALF = 512
KH = HALF // P
FH = 8
FD = 64
TAPS = 31
WINDOWS = (2, 4, 8, 16)
ALPHA = 4.0 ** 0.25
RMS_EPS = 1e-6
LN_EPS = 1e-5
NEG = -1e30
RING = 4
SLOT = 2048

N_ADA0, N_XM, N_QK, N_OZ, N_MOUT = 8, 8, 8, 16, 8
N_FIN, N_FOUT, N_EVIN, N_EVOUT = 16, 8, 8, 4
N_FFI, N_FFO, N_ODIN, N_ODOUT = KF, KF // 2, 10, 4
N_MIX = 3 * N_XM
STARTS = {}
_at = 0
for _name, _n in (("ada0", N_ADA0), ("mix", N_MIX), ("qk", N_QK), ("oz", N_OZ), ("mout", N_MOUT),
                  ("fin", N_FIN), ("fout", N_FOUT), ("evin", N_EVIN), ("evout", N_EVOUT),
                  ("ffi0", N_FFI), ("ffo0", N_FFO), ("odin", N_ODIN), ("odout", N_ODOUT),
                  ("ffi1", N_FFI), ("ffo1", N_FFO)):
    STARTS[_name] = _at
    _at += _n
SLOTS = _at

VEC = {}
_at = 0
for _name, _n in (("c", 2 * KD), ("norm_g0", KD), ("norm_g1", KD), ("norm_f", KD), ("b_ada", 6 * KD),
                  ("conv_w", 9 * KE), ("conv_b", KE), ("ln_w", KE), ("skip", KE),
                  ("gate_w", 3 * KE * 16), ("ev_conv", 3 * KH), ("pool_s", KH), ("pool_w", KH * P),
                  ("dw_w", TAPS * KH), ("dw_b", KH), ("cn_g", KH), ("cn_b", KH), ("forget_w", KD * FH),
                  ("mix_g0", KD), ("mix_b0", KD), ("ffn_g0", KD), ("ffn_b0", KD),
                  ("mix_g1", KD), ("mix_b1", KD), ("ffn_g1", KD), ("ffn_b1", KD)):
    VEC[_name] = (_at, _n)
    _at += _n
VECS = _at

CST = {}
_at = 0
for _name, _n in (("ident", P), ("mask_f", P), ("mask_b", P), ("count", 4 * 16), ("select", FH * P)):
    CST[_name] = (_at, _n)
    _at += _n
CSTS = _at


class Chain:

    def __init__(self, eng, sem):
        self.eng, self.sem, self.base, self.n = eng, sem, 0, 0

    def step(self, ins):
        ins.then_inc(self.sem, 1)
        self.n += 1

    def join(self, back=0):
        self.eng.wait_ge(self.sem, self.base + self.n - back)

    def enter(self, i, per):
        self.start, self.per = self.n, per
        self.base, self.n = i * per + self.start, 0

    def leave(self, rounds):
        assert self.n == self.per, (self.n, self.per)
        self.base, self.n = 0, self.start + rounds * self.per


def program(nc, w_in, x_in, ctx_in, vec_in, cst_in, dft_in, row_in, out):
    with ExitStack() as ctx:
        sems = {}

        def S(name):
            if name not in sems:
                sems[name] = ctx.enter_context(nc.semaphore(name))
            return sems[name]

        def tensors(stack):
            return lambda name, shape: stack.enter_context(nc.sbuf_tensor(name, [shape[0], *shape[1:]], F32))

        sb = tensors(ctx)
        ring = sb("ring", (P, RING, SLOT))
        X = sb("X", (P, KD, SEQ))
        vec = sb("vec", (P, VECS))
        cst = sb("cst", (P, CSTS))
        rows = sb("rows", (FH, 8))
        ones_d = sb("ones_d", (P, P))
        ones_h = sb("ones_h", (P, P))
        ones = sb("ones", (P, P))
        modl = sb("modl", (P, 6 * KD, 2))
        scl = sb("scl", (P, 3 * KD))
        eps = sb("eps", (P, 2))
        rstd = sb("rstd", (P, TOK))

        first = ExitStack()
        sa = tensors(first)
        h = sa("h", (P, KD, TOK))
        V = sa("V", (P, HC + KE, TOK))
        xconv = sa("xconv", (P, KE, TOK))
        scores = sa("scores", (P, HEADS, 4, SEQ))
        qk = sa("qk", (P, 2 * HC, TOK))
        o_sb = sa("o_sb", (P, KE, SEQ))
        ones_row = sa("ones_row", (HEADS, CTX))
        em = sa("em", (P, 2, SEQ))
        rden = sa("rden", (P, 2, SEQ))
        diag = sa("diag", (P, 4, P))
        gcol = sa("gcol", (P, 2, 4, HEADS))
        gtok = sa("gtok", (P, 4, 16))
        silc = sa("silc", (P, KD, 2))
        wexp = [h[:, 4 * b:4 * b + 4, :].rearrange("p a b -> p (a b)").rearrange("p (d s j) -> p d s j", d=2, s=4)
                for b in range(2)]
        z_sb = qk[:, :, :].rearrange("p a b -> p (a b)").rearrange("p (c j) -> p c j", j=SEQ)
        def work(n):
            return xconv[:, 4 * n:4 * n + 4, 0:CTX]

        def grow(a, n=1, half=slice(0, 2)):
            v = xconv[0:HEADS, :, 0:CTX].rearrange("p (r t) j -> p r t j", t=2)
            return v[:, a:a + n, half, :]

        first.close()

        second = ExitStack()
        sc = tensors(second)
        h2 = sc("h2", (P, KD, SEQ))
        U = sc("U", (P, KE, SEQ))
        G = sc("G", (P, KF, SEQ))
        dft = sc("dft", (P, 2, 3 * SEQ))
        pq = sc("pq", (P, 2, 2, 512))
        sq = sc("sq", (P, KD, SEQ))
        gate = sc("gate", (P, 2, SEQ))
        pad_a = sc("pad_a", (P, KH, 32 + SEQ))
        pad_b = sc("pad_b", (P, KH, 32 + SEQ))
        pad_c = sc("pad_c", (P, KH, 32 + SEQ))
        pad_d = sc("pad_d", (P, KH, 32 + SEQ))
        acc31 = sc("acc31", (P, KH, SEQ))
        logit = sc("logit", (P, FH, 2, SEQ))
        probT = sc("probT", (P, 2, 2, SEQ))
        vtok = sc("vtok", (P, 2, HALF))
        frow = sc("frow", (FH, 6, SEQ))
        stat = sc("stat", (P, 3, 2 * FH))
        second.close()

        ps = ctx.enter_context(nc.psum_tensor("ps", [P, 8, 512], F32))

        def vcol(name, k=0, n=1):
            a = VEC[name][0] + k
            return vec[:, bass.ds(a, n)]

        def cc(name, a=0, b=None):
            o, n = CST[name]
            return cst[:, o + a:o + (n if b is None else b)]

        ident = cc("ident")
        gate_w = vcol("gate_w", 0, 48 * 16).rearrange("p (c g) -> p c g", g=16)
        forget_w = vcol("forget_w", 0, KD * FH).rearrange("p (k f) -> p k f", f=FH)
        pool_w = vcol("pool_w", 0, KH * P).rearrange("p (g d) -> p g d", d=P)
        tile8 = ring[:, :, :].rearrange("p s (k n) -> p s k n", k=8)
        tile4 = ring[:, :, :].rearrange("p s (k n) -> p s k n", k=4)
        tile2 = ring[:, :, :].rearrange("p s (k n) -> p s k n", k=2)
        acc = ps[:, 4:8, :].rearrange("p b n -> p (b n)").rearrange("p (m t) -> p m t", t=SEQ)
        acc_flat = ps[:, 4:8, :].rearrange("p b n -> p (b n)")
        mean_ps = ps[:, 0, 0:SEQ]
        var_ps = ps[:, 1, 0:SEQ]

        def wide(a, n):
            return a.rearrange("p (o t) -> p o t", o=1).to_broadcast([P, n, a.shape[1]])

        loaded = [S(f"weights_loaded_{s}") for s in range(RING)]
        block = ctx.enter_context(nc.Block())

        @block.sync
        def _(sp):
            for s in range(RING):
                sp.dma_start(ring[:, s, :], w_in[s]).then_inc(loaded[s], 16)
            with sp.Fori(1, SLOTS // RING) as i:
                for s in range(RING):
                    sp.wait_ge(S("slot_done"), (i - 1) * RING + s + 1)
                    sp.dma_start(ring[:, s, :], w_in[i * RING + s]).then_inc(loaded[s], 16)
            sp.wait_ge(S("out_ffn1"), KD)
            sp.dma_start(out, X[:, :, :]).then_inc(S("result_stored"), 16)
            sp.wait_ge(S("result_stored"), 16)

        @block.tensor
        def _(pe):
            mm = nc.tensor.matmul

            def weights(g, i=0):
                pe.wait_ge(loaded[g % RING], i * 16 + (g // RING + 1) * 16)
                return g % RING

            def walk(n, start, body):
                rounds = n // RING
                for t in range(min(n, RING)):
                    body(t, t % RING, weights(start + t))
                at = RING
                if rounds > 2:
                    with pe.Fori(1, rounds) as i:
                        for u in range(RING):
                            body(i * RING + u, u, weights(start + u, i))
                    at = rounds * RING
                for t in range(at, n):
                    body(t, t % RING, weights(start + t))

            def project(n, start, rhs, moved, ready=None):
                def body(t, u, s):
                    if not isinstance(t, int) or t >= 4:
                        pe.wait_ge(moved, t - 3)
                    for b in range(2):
                        for k in range(KD):
                            if ready is not None and isinstance(t, int) and t == 0 and b == 0:
                                pe.wait_ge(ready, k + 1)
                            last = mm(ps[:, u, b * SEQ:(b + 1) * SEQ], tile8[:, s, k, b * P:(b + 1) * P],
                                      rhs(k), start=(k == 0), stop=(k == KD - 1))
                    last.then_inc(S("slot_done"), 1)
                walk(n, start, body)

            def accumulate(n, start, rhs, wait):
                def body(t, u, s):
                    for k in range(2):
                        wait(t, k)
                        for m in range(KD):
                            last = mm(acc[:, m, :], tile2[:, s, k, m * P:(m + 1) * P], rhs(t, k),
                                      start=(isinstance(t, int) and t == 0 and k == 0 and m % 2 == 0),
                                      stop=(k == 1), skip_group_check=True)
                    last.then_inc(S("slot_done"), 1)
                walk(n, start, body)

            def column_sum(dst, weight, src, n, ready, done):
                for k in range(n):
                    if ready is not None:
                        pe.wait_ge(ready, k + 1)
                    last = mm(dst, weight, src(k), start=(k == 0), stop=(k == n - 1))
                last.then_inc(done, 1)

            pe.wait_ge(S("silc_ready"), 1)

            def ada(s, bank, col):
                for b in range(2):
                    for k in range(KD):
                        last = mm(ps[:, bank, bass.ds(col + 2 * b, 2)], tile8[:, s, k, b * P:(b + 1) * P],
                                  silc[:, k, :], start=(k == 0), stop=(k == KD - 1))
                last.then_inc(S("slot_done"), 1)

            pe.wait_ge(S("ones_ready"), 3)
            column_sum(ps[:, 6, :], ones_d[:, :], lambda k: V[:, k, :], KD, S("squares_0"), S("meansq_0"))
            walk(N_ADA0, STARTS["ada0"], lambda t, u, s: ada(s, 4, t * 4))

            def mix(t, u, s, i):
                if u % 3 == 0:
                    for b in range(2):
                        unit = 2 * (u // 3) + b
                        if not isinstance(i, int) or i * 8 + unit >= 4:
                            pe.wait_ge(S("xm_moved"), i * 8 + unit - 3)
                        for k in range(KD):
                            if isinstance(i, int) and i == 0 and u == 0 and b == 0:
                                pe.wait_ge(S("h_ready"), 2 * k + 2)
                            last = mm(ps[:, unit % 4, :], tile8[:, s, k, b * P:(b + 1) * P], h[:, k, :],
                                      start=(k == 0), stop=(k == KD - 1))
                        last.then_inc(S("slot_done") if b else S("xm_half"), 1)
                else:
                    ada(s, 5, i * 32 + 4 * (u - u // 3 - 1))

            for u in range(12):
                mix(u, u, weights(STARTS["mix"] + u), 0)
            with pe.Fori(1, 2) as i:
                for u in range(12):
                    mix(i * 12 + u, u, weights(STARTS["mix"] + u, i * 3), i)

            pe.wait_ge(S("xm_moved"), KE)
            pe.wait_ge(S("ident_ready"), 16)
            for hd in range(HEADS):
                for part in range(2):
                    s = weights(STARTS["qk"] + 2 * hd + part)
                    for e in range(HC):
                        unit = 12 * hd + 4 * part + e
                        if unit >= 4:
                            pe.wait_ge(S("qkv_moved"), unit - 3)
                        for k in range(HC):
                            pe.wait_ge(S("xconv_ready"), 4 * hd + k + 1)
                            last = mm(ps[:, e, :], tile4[:, s, k, e * P:(e + 1) * P],
                                      xconv[:, HC * hd + k, :], start=(k == 0), stop=(k == HC - 1))
                        last.then_inc(S("qk_done") if e < HC - 1 else S("slot_done"), 1)
                xm = [V[:, HC + HC * hd + e, :] for e in range(HC)]
                for t in range(4):
                    pe.wait_ge(S("qkv_moved"), 12 * hd + 8 + t - 3)
                    for e in range(HC):
                        last = nc.tensor.transpose(ps[:, t, e * P:(e + 1) * P], xm[e][:, t * P:(t + 1) * P], ident)
                    last.then_inc(S("v_turned"), 1)
                pe.wait_ge(S("qkv_moved"), 12 * hd + 8)
                for part, src in ((2, xm), (0, [qk[:, e, :] for e in range(HC)]),
                                  (1, [qk[:, HC + e, :] for e in range(HC)])):
                    for e in range(HC):
                        for t in range(4):
                            last = mm(ps[:, 7, t * 16:(t + 1) * 16], src[e][:, t * P:(t + 1) * P],
                                      gate_w[:, part * KE + HC * hd + e, :],
                                      start=(hd == 0 and part == 2 and e == 0 and t == 0),
                                      stop=(hd == HEADS - 1 and part == 1 and e == HC - 1),
                                      skip_group_check=True)
                last.then_inc(S("gates_done"), 1)
                if hd:
                    pe.wait_ge(S("scores_moved"), hd)
                else:
                    pe.wait_ge(S("mod0_ready"), 1)
                    pe.wait_ge(S("mod1_ready"), 1)
                for t in range(4):
                    for e in range(HC):
                        last = mm(ps[:, 4 + t // 2, (t % 2) * SEQ:(t % 2 + 1) * SEQ],
                                  qk[:, HC + e, t * P:(t + 1) * P], qk[:, e, CTX:TOK],
                                  start=(e == 0), stop=(e == HC - 1))
                last.then_inc(S("scores_done"), 1)

            pe.wait_ge(S("gtok_ready"), 1)
            pe.wait_ge(S("scores_moved"), HEADS)
            for g in range(4):
                for t in range(4):
                    last = nc.tensor.transpose(ps[0:4, 4 + g, t * P:(t + 1) * P], gtok[:, t, 4 * g:4 * g + 4],
                                               ident)
            last.then_inc(S("grow_done"), 1)

            pe.wait_ge(S("qkv_moved"), 12 * HEADS)
            project(N_OZ, STARTS["oz"], lambda k: h[:, k, CTX:TOK], S("oz_moved"))

            pe.wait_ge(S("g_ready"), 1)
            for d in range(2):
                for t in range(4):
                    last = nc.tensor.transpose(ps[:, 4, (d * 4 + t) * 4:(d * 4 + t) * 4 + 4],
                                               grow(d)[:, 0, t // 2, (t % 2) * P:(t % 2 + 1) * P],
                                               ident[0:HEADS, 0:HEADS])
            last.then_inc(S("gcol_done"), 1)
            pe.wait_ge(S("floor_ready"), 1)
            pe.wait_ge(S("oz_moved"), N_OZ)

            def spread(hd):
                if hd:
                    pe.wait_ge(S("diag_ready"), hd)
                    pe.wait_ge(S("wexp_ready"), hd)
                sel = cc("select", hd * P, (hd + 1) * P)[0:HEADS]
                mm(ps[:, 0, :], sel, grow(2)[:, 0], start=True, stop=True)
                mm(ps[:, 1, :], sel, grow(3)[:, 0], start=True, stop=True).then_inc(S("spread_done"), 1)

            def denominators(hd):
                pe.wait_ge(S("weighted_ready"), hd + 1)
                w = wexp[hd % 2]
                for t in range(4):
                    last = mm(ps[:, 2, :], ones[:, :], w[:, :, t, :], start=(t == 0), stop=(t == 3))
                last.then_inc(S("den_done"), 1)

            def mix_values(hd):
                pe.wait_ge(S("probs_ready"), hd + 1)
                if hd == 0:
                    pe.wait_ge(S("gcol_ready"), 1)
                if hd >= 2:
                    pe.wait_ge(S("heads_moved"), hd - 1)
                for e in range(HC):
                    for t in range(4):
                        last = mm(ps[:, 4 + 2 * (hd % 2) + e // 2, (e % 2) * SEQ:(e % 2 + 1) * SEQ],
                                  V[:, HC * hd + t, e * P:(e + 1) * P], scores[:, hd, t, :],
                                  start=(t == 0), stop=(t == 3))
                last.then_inc(S("values_done"), 1)

            for n in range(HEADS + 2):
                if n < HEADS:
                    spread(n)
                if 1 <= n <= HEADS:
                    denominators(n - 1)
                if n >= 2:
                    pe.wait_ge(S("heads_moved"), n - 1)
                    if n >= 3:
                        pe.wait_ge(S("head_root"), n - 2)
                    column_sum(ps[:, 3, 0:SEQ], ones_h[:, :], lambda k: work(2 * (n % 2))[:, k, :], HC, None,
                               S("head_mean"))
                if 1 <= n <= HEADS:
                    mix_values(n - 1)
                if n >= 2:
                    pe.wait_ge(S("head_squares"), n - 1)
                    column_sum(ps[:, 3, SEQ:2 * SEQ], ones_h[:, :], lambda k: work(3)[:, k, :], HC, None,
                               S("head_var"))

            pe.wait_ge(S("heads_moved"), HEADS)
            accumulate(N_MOUT, STARTS["mout"], lambda t, k: o_sb[:, t * 2 + k, :],
                       lambda t, k: pe.wait_ge(S("y_ready"), t * 2 + k + 1))

            def norm(name, centred, n=KD, weight=ones_d, src=X, sqs=sq):
                if centred:
                    column_sum(mean_ps, weight[:, :], lambda k: src[:, k, :], n, S(f"in_{name}"),
                               S(f"mean_{name}"))
                column_sum(var_ps, weight[:, :], lambda k: sqs[:, k, :], n, S(f"squares_{name}"),
                           S(f"var_{name}"))

            norm("rms1", False)
            pe.wait_ge(S("dft_ready"), 16)
            project(N_FIN, STARTS["fin"], lambda k: h2[:, k, :], S("fin_moved"), S("out_rms1"))

            pe.wait_ge(S("fin_moved"), N_FIN)
            def channels(g):
                if g >= 2:
                    pe.wait_ge(S("pq_moved"), 2 * (g - 1))
                for n in range(2):
                    for k in range(2):
                        last = mm(ps[:, 2 * (g % 2) + n, :], U[:, 2 * g + k, n * P:(n + 1) * P], dft[:, k, 0:512],
                                  start=(k == 0), stop=(k == 1))
                    last.then_inc(S("pq_done"), 1)

            def positions(g):
                pe.wait_ge(S("pq_moved"), 2 * (g + 1))
                if g >= 4:
                    pe.wait_ge(S("f_moved"), g - 3)
                for c in range(2):
                    for n in range(2):
                        for q, col in ((0, 0), (1, 2 * SEQ)):
                            last = mm(ps[:, 4 + g % 4, c * SEQ:(c + 1) * SEQ],
                                      pq[:, g % 2, n, q * SEQ + c * P:q * SEQ + (c + 1) * P],
                                      dft[:, n, col:col + SEQ], start=(n == 0 and q == 0), stop=(n == 1 and q == 1))
                last.then_inc(S("f_done"), 1)

            channels(0)
            for g in range(GROUPS):
                if g + 1 < GROUPS:
                    channels(g + 1)
                positions(g)
            pe.wait_ge(S("f_moved"), GROUPS)
            accumulate(N_FOUT, STARTS["fout"], lambda t, k: G[:, t * 2 + k, :], lambda t, k: None)
            norm("rmsf", False)

            project(N_EVIN, STARTS["evin"], lambda k: X[:, k, :], S("evin_moved"), S("out_rmsf"))
            pe.wait_ge(S("evin_moved"), N_EVIN)
            for g in range(KH):
                pe.wait_ge(S("pooled_ready"), g + 1)
                last = mm(ps[:, g // 2, (g % 2) * SEQ:(g % 2 + 1) * SEQ], pool_w[:, g, :], h2[:, g, :],
                          start=True, stop=True)
            last.then_inc(S("pool_done"), 1)
            accumulate(N_EVOUT, STARTS["evout"], lambda t, k: U[:, 2 * t + k, :],
                       lambda t, k: pe.wait_ge(S("evmix_ready"), 2 * t + k + 1))
            norm("mix0", True)

            def feed_forward(l):
                project(N_FFI, STARTS[f"ffi{l}"], lambda k: X[:, k, :], S(f"ffi{l}_moved"), S(f"out_mix{l}"))
                accumulate(N_FFO, STARTS[f"ffo{l}"], lambda t, k: G[:, t * 2 + k, :],
                           lambda t, k: pe.wait_ge(S(f"ffi{l}_moved"), t * 2 + k + 1))
                norm(f"ffn{l}", True)

            feed_forward(0)

            start = STARTS["odin"]
            for t in range(8):
                s = weights(start + t)
                if t >= 4:
                    pe.wait_ge(S("odin_moved"), t - 3)
                for b in range(2):
                    for k in range(KD):
                        if t == 0 and b == 0:
                            pe.wait_ge(S("out_ffn0"), k + 1)
                        last = mm(ps[:, t % 4, b * SEQ:(b + 1) * SEQ], tile8[:, s, k, b * P:(b + 1) * P],
                                  X[:, k, :], start=(k == 0), stop=(k == KD - 1))
                last.then_inc(S("slot_done"), 1)
            for t in range(8, N_ODIN):
                s = weights(start + t)
                pe.wait_ge(S("odin_moved"), t - 3)
                for b in range(2):
                    for k in range(KD):
                        last = mm(ps[:, t % 4, b * SEQ:(b + 1) * SEQ], X[:, k, b * P:(b + 1) * P],
                                  tile8[:, s, k, :], start=(k == 0), stop=(k == KD - 1))
                last.then_inc(S("slot_done"), 1)
            for k in range(KD):
                last = mm(ps[0:FH, 4, 0:SEQ], forget_w[:, k, :], X[:, k, :], start=(k == 0), stop=(k == KD - 1))
            last.then_inc(S("forget_done"), 1)

            pe.wait_ge(S("cum_ready"), 1)
            pe.wait_ge(S("odin_moved"), N_ODIN)
            for hd in range(FH):
                if hd >= 4:
                    pe.wait_ge(S("logits_moved"), hd - 3)
                lo = FD * (hd % 2)
                for t in range(2):
                    n = P * (t + 1)
                    mm(ps[:, hd % 4, t * SEQ:t * SEQ + n], U[lo:lo + FD, hd // 2, t * P:(t + 1) * P],
                       U[lo:lo + FD, KH + hd // 2, 0:n], start=True, stop=False)
                    last = mm(ps[:, hd % 4, t * SEQ:t * SEQ + n], cc("select", hd * P, (hd + 1) * P)[0:FH],
                              frow[:, 3, 0:n], start=False, stop=True)
                last.then_inc(S("logits_done"), 1)
            for hd in range(FH):
                pe.wait_ge(S("prob_ready"), hd + 1)
                if hd >= 2:
                    pe.wait_ge(S("probT_moved"), hd - 1)
                b = hd % 2
                if hd < 2:
                    pe.wait_ge(S("logits_moved"), FH)
                nc.tensor.transpose(ps[:, b, 0:P], logit[:, hd, 0, 0:P], ident)
                nc.tensor.transpose(ps[:, b, P:2 * P], logit[:, hd, 1, 0:P], ident)
                nc.tensor.transpose(ps[:, b, 3 * P:4 * P], logit[:, hd, 1, P:2 * P], ident)\
                    .then_inc(S("probT_done"), 1)
                pe.wait_ge(S("probT_moved"), hd + 1)
                lo, c = FD * (hd % 2), hd // 2
                if c >= 2 and hd % 2 == 0:
                    pe.wait_ge(S("attn_moved"), c - 1)
                mm(ps[lo:lo + FD, 2 + c % 2, 0:SEQ], vtok[:, 0, hd * FD:(hd + 1) * FD], probT[:, b, 0, :],
                   start=True, stop=False, skip_group_check=True)
                mm(ps[lo:lo + FD, 2 + c % 2, P:SEQ], vtok[:, 1, hd * FD:(hd + 1) * FD], probT[:, b, 1, P:SEQ],
                   start=False, stop=True, skip_group_check=True).then_inc(S("attn_done"), 1)
            pe.wait_ge(S("attn_moved"), KH)


            def mixed(t, k):
                if 2 * t + k == KH:
                    norm("conv", True, KH, ones_h, acc31)
                if 2 * t + k >= KH:
                    pe.wait_ge(S("out_conv"), 2 * t + k - KH + 1)

            accumulate(N_ODOUT, STARTS["odout"], lambda t, k: G[:, 2 * t + k, :], mixed)
            norm("mix1", True)
            feed_forward(1)

        @block.scalar
        def _(act):
            do = nc.scalar.activation
            chain = Chain(act, S("act_order"))

            def units(n, body):
                rounds = n // RING
                for t in range(min(n, RING)):
                    body(t, t % RING)
                at = RING
                if rounds > 2:
                    with act.Fori(1, rounds) as i:
                        for u in range(RING):
                            body(i * RING + u, u)
                    at = rounds * RING
                for t in range(at, n):
                    body(t, t % RING)

            act.dma_start(vec[:, :], vec_in).then_inc(S("vec_ready"), 16)
            act.dma_start(X[:, :, :], x_in).then_inc(S("x_ready"), 16)
            act.dma_start(h[:, :, 0:CTX], ctx_in).then_inc(S("ctx_ready"), 16)
            act.dma_start(cst[:, :], cst_in).then_inc(S("ident_ready"), 16)
            act.dma_start(rows[:, :], row_in).then_inc(S("rows_ready"), 16)
            act.wait_ge(S("vec_ready"), 16)
            do(silc[:, :, :].rearrange("p k t -> p (k t)"), vcol("c", 0, 2 * KD), ACT.Silu)\
                .then_inc(S("silc_ready"), 1)
            act.wait_ge(S("x_ready"), 16)
            act.wait_ge(S("ctx_ready"), 16)
            for k in range(KD):
                chain.step(do(V[:, k, 0:CTX], h[:, k, 0:CTX], ACT.Square))
                do(V[:, k, CTX:TOK], X[:, k, :], ACT.Square).then_inc(S("squares_0"), 1)
            act.wait_ge(S("meansq_0"), 1)
            do(rstd[:, :], ps[:, 6, :], ACT.Sqrt, bias=eps[:, 0:1]).then_inc(S("root_0"), 1)
            for k in range(KD):
                for t, col in ((0, 1), (1, 0)):
                    act.wait_ge(S("scaled_0"), 2 * k + t + 1)
                    part = h[:, k, t * CTX:t * CTX + SEQ]
                    do(part, part, ACT.Identity, bias=modl[:, k, col:col + 1]).then_inc(S("h_ready"), 1)

            def move_xm(i, r):
                if r % 2 == 0:
                    act.wait_ge(S("xm_half"), i * 2 + r // 2 + 1)
                else:
                    act.wait_ge(S("slot_done"), i * 6 + STARTS["mix"] + 3 * (r // 2) + 1)
                do(V[:, i * 4 + HC + r, :], ps[:, r, :], ACT.Copy).then_inc(S("xm_moved"), 1)

            def silu(i, r):
                act.wait_ge(S("conv_done"), i * 4 + r + 1)
                a = xconv[:, i * 4 + r, :]
                do(a, a, ACT.Silu).then_inc(S("xconv_ready"), 1)

            for r in range(4):
                move_xm(0, r)
            with act.Fori(1, KE // 4) as i:
                for r in range(4):
                    move_xm(i, r)
                    silu(i - 1, r)
            for r in range(4):
                silu(KE // 4 - 1, r)

            for hd in range(HEADS):
                for r in range(12):
                    if r < 8:
                        if r % 4 < 3:
                            act.wait_ge(S("qk_done"), 6 * hd + 3 * (r // 4) + r % 4 + 1)
                        else:
                            act.wait_ge(S("slot_done"), STARTS["qk"] + 2 * hd + r // 4 + 1)
                        if r == 0 and hd:
                            act.wait_ge(S("scores_done"), hd)
                        do(qk[:, r, :], ps[:, r % 4, :], ACT.Copy, scale=1.0 if r < 4 else DH ** -0.5)\
                            .then_inc(S("qkv_moved"), 1)
                    else:
                        act.wait_ge(S("v_turned"), 4 * hd + r - 7)
                        if r == 8 and hd:
                            act.wait_ge(S("gates_done"), hd)
                        do(V[:, HC * hd + r - 8, :], ps[:, r % 4, :], ACT.Copy).then_inc(S("qkv_moved"), 1)

            def softplus_of_minus(x, t, ready, done):
                act.wait_ge(ready, 1)
                chain.step(do(t, x, ACT.Abs))
                chain.join()
                chain.step(do(t, t, ACT.Exp, scale=-1.0))
                chain.join()
                do(t, t, ACT.Ln, bias=1.0).then_inc(done, 1)

            rows2 = lambda a: grow(a, 2).rearrange("p r t j -> p (r t) j")
            softplus_of_minus(rows2(2), rows2(4), S("grow_moved"), S("grow_log"))
            act.wait_ge(S("m_ready"), 1)
            do(grow(3)[:, 0], grow(3)[:, 0], ACT.Exp, scale=-1.0).then_inc(S("floor_ready"), 1)
            def move_oz(t, u, dst, fn, at):
                act.wait_ge(S("slot_done"), t + STARTS["oz"] + at + 1)
                do(dst[:, bass.ds(t * 2, 2), :], ps[:, u, :].rearrange("p (b j) -> p b j", b=2), fn)\
                    .then_inc(S("oz_moved"), 1)

            for t in range(8):
                move_oz(t, t % 4, o_sb, ACT.Sigmoid, 0)
            act.wait_ge(S("scores_done"), HEADS)
            for t in range(8):
                move_oz(t, t % 4, z_sb, ACT.Silu, 8)

            def weigh(hd):
                w = wexp[hd % 2]
                act.wait_ge(S("spread_done"), hd + 1)
                if hd:
                    act.wait_ge(S("probs_ready"), hd)
                else:
                    act.wait_ge(S("gcol_ready"), 1)
                    act.wait_ge(S("wexp_clear"), 4)
                if hd >= 2:
                    act.wait_ge(S("den_done"), hd - 1)
                chain.step(do(em[:, :, :].rearrange("p d j -> p (d j)"), ps[:, 1, :], ACT.Copy))
                act.wait_ge(S("diag_ready"), hd + 1)
                for d, t, lo, hi in ((0, 0, 0, SEQ), (0, 1, 0, SEQ), (0, 2, P, SEQ),
                                     (1, 0, 0, SEQ), (1, 1, 0, SEQ), (1, 3, 0, P)):
                    chain.step(do(w[:, d, t, lo:hi], ps[:, 0, d * SEQ + lo:d * SEQ + hi], ACT.Exp,
                                  bias=gcol[:, d, t, hd:hd + 1]))
                for n, (d, t, lo) in enumerate(((0, 2, 0), (0, 3, P), (1, 2, 0), (1, 3, P))):
                    last = do(w[:, d, t, lo:lo + P], diag[:, n, :], ACT.Exp)
                    if n < 3:
                        chain.step(last)
                last.then_inc(S("wexp_ready"), 1)

            for n in range(HEADS + 2):
                if n < HEADS:
                    weigh(n)
                if 1 <= n <= HEADS:
                    act.wait_ge(S("values_done"), n)
                    if n >= 3:
                        act.wait_ge(S("y_ready"), 4 * (n - 2))
                    b = 4 + 2 * ((n - 1) % 2)
                    do(work(2 * ((n - 1) % 2)),
                       ps[:, b:b + 2, :].rearrange("p b (c j) -> p (b c) j", c=2), ACT.Copy)\
                        .then_inc(S("heads_moved"), 1)
                if n >= 2:
                    act.wait_ge(S("head_centred"), n - 1)
                    if n >= 3:
                        act.wait_ge(S("head_var"), n - 2)
                    do(work(3), work(2 * (n % 2)), ACT.Square).then_inc(S("head_squares"), 1)
                    act.wait_ge(S("head_var"), n - 1)
                    if n >= 3:
                        act.wait_ge(S("y_ready"), 4 * (n - 2))
                    do(rstd[:, 0:SEQ], ps[:, 3, SEQ:2 * SEQ], ACT.Sqrt, bias=eps[:, 0:1])\
                        .then_inc(S("head_root"), 1)

            def norm(name, bias, n=KD, src=X, dst=X, fn=ACT.Identity, centred=True):
                for k in range(n):
                    act.wait_ge(S(f"centred_{name}" if centred else f"in_{name}"), k + 1)
                    do(sq[:, k, :], src[:, k, :], ACT.Square).then_inc(S(f"squares_{name}"), 1)
                act.wait_ge(S(f"var_{name}"), 1)
                e = 1 if centred else 0
                do(rstd[:, 0:SEQ], var_ps, ACT.Sqrt, bias=eps[:, e:e + 1]).then_inc(S(f"root_{name}"), 1)
                if bias is not None:
                    for k in range(n):
                        act.wait_ge(S(f"scaled_{name}"), k + 1)
                        do(dst[:, k, :], src[:, k, :] if src is not X else dst[:, k, :], fn, bias=bias(k))\
                            .then_inc(S(f"out_{name}"), 1)

            act.wait_ge(S("y_ready"), KE)
            act.dma_start(dft[:, :, :], dft_in).then_inc(S("dft_ready"), 16)
            norm("rms1", lambda k: modl[:, 3 * KD + k, 0:1], dst=h2, centred=False)

            def move_fin(t, u, dst, fn, at):
                act.wait_ge(S("slot_done"), t + STARTS["fin"] + at + 1)
                do(dst[:, bass.ds(t * 2, 2), :], ps[:, u, :].rearrange("p (b j) -> p b j", b=2), fn)\
                    .then_inc(S("fin_moved"), 1)

            for t in range(8):
                move_fin(t, t % 4, U, ACT.Copy, 0)
            for t in range(8):
                move_fin(t, t % 4, G, ACT.Silu, 8)
            for g in range(GROUPS):
                if g >= 2:
                    act.wait_ge(S("f_done"), g - 1)
                for n in range(2):
                    act.wait_ge(S("pq_done"), 2 * g + n + 1)
                    do(pq[:, g % 2, n, :], ps[:, 2 * (g % 2) + n, :], ACT.Copy).then_inc(S("pq_moved"), 1)
            norm("rmsf", None, centred=False)

            act.wait_ge(S("pads_clear"), 4)
            for t in range(N_EVIN):
                act.wait_ge(S("slot_done"), STARTS["evin"] + t + 1)
                if t < 6:
                    dst = U[:, 2 * t:2 * t + 2, :]
                else:
                    dst = pad_a[:, 2 * (t - 6):2 * (t - 6) + 2, 32:]
                do(dst, ps[:, t % 4, :].rearrange("p (b j) -> p b j", b=2), ACT.Copy)\
                    .then_inc(S("evin_moved"), 1)
            norm("mix0", lambda k: vcol("mix_b0", k))

            def feed_forward(l):
                def gated(t, u):
                    act.wait_ge(S("slot_done"), t + STARTS[f"ffi{l}"] + 1)
                    if not isinstance(t, int) or t >= 2:
                        act.wait_ge(S(f"ffi{l}_moved"), t - 1)
                    do(gate[:, u % 2, :], ps[:, u, 0:SEQ], ACT.Silu).then_inc(S(f"gate{l}_ready"), 1)
                units(N_FFI, gated)
                norm(f"ffn{l}", lambda k: vcol(f"ffn_b{l}", k))

            feed_forward(0)

            for t in range(N_ODIN):
                act.wait_ge(S("slot_done"), STARTS["odin"] + t + 1)
                if t < 4:
                    if t >= 2:
                        act.wait_ge(S("odin_moved"), t - 1)
                    do(gate[:, t % 2, :], ps[:, t, SEQ:2 * SEQ], ACT.Sigmoid).then_inc(S("glu_ready"), 1)
                    continue
                if t == 4:
                    act.wait_ge(S("odin_moved"), 4)
                if t < 8:
                    dst = U[:, 2 * (t - 4):2 * (t - 4) + 2, :]
                else:
                    dst = vtok[:, :, (t - 8) * SEQ:(t - 7) * SEQ]
                do(dst, ps[:, t % 4, :].rearrange("p (b j) -> p b j", b=2), ACT.Copy)\
                    .then_inc(S("odin_moved"), 1)
            softplus_of_minus(frow[:, 0, :], frow[:, 1, :], S("forget_moved"), S("forget_log"))
            for hd in range(FH):
                act.wait_ge(S("max_ready"), hd + 1)
                for t in range(2):
                    a = logit[:, hd, t, :]
                    last = do(a, a, ACT.Exp, scale=FD ** -0.5, bias=stat[:, 1, 2 * hd + t:2 * hd + t + 1],
                              accum_out=stat[:, 2, 2 * hd + t:2 * hd + t + 1])
                    if t == 0:
                        chain.step(last)
                last.then_inc(S("exp_ready"), 1)
            for hd in range(FH):
                act.wait_ge(S("probT_done"), hd + 1)
                if hd >= 2:
                    act.wait_ge(S("attn_done"), hd - 1)
                chain.step(do(probT[:, hd % 2, 0, :], ps[:, hd % 2, 0:SEQ], ACT.Copy))
                do(probT[:, hd % 2, 1, P:SEQ], ps[:, hd % 2, 3 * P:4 * P], ACT.Copy)\
                    .then_inc(S("probT_moved"), 1)
            norm("conv", lambda k: vcol("cn_b", k), KH, acc31, G[:, KH:2 * KH, :], ACT.Silu)
            norm("mix1", lambda k: vcol("mix_b1", k))
            feed_forward(1)

        @block.gpsimd
        def _(pool):
            pool.wait_ge(S("slot_done"), STARTS["oz"])
            pool.wait_ge(S("vec_ready"), 16)
            for c in range(KE):
                a = xconv[:, c, CTX:TOK]
                nc.gpsimd.tensor_scalar(a, a, vcol("skip", c), None, ALU.mult).then_inc(S("skip_ready"), 1)
            pool.wait_ge(S("slot_done"), STARTS["mout"])
            for b in range(2):
                for d, t, lo in ((0, 3, 0), (1, 2, P)):
                    nc.gpsimd.memset(wexp[b][:, d, t, lo:lo + P], 0.0).then_inc(S("wexp_clear"), 1)
            pool.wait_ge(S("out_rms1"), KD)
            for a in (pad_a, pad_b, pad_c, pad_d):
                nc.gpsimd.memset(a[:, :, 0:32], 0.0).then_inc(S("pads_clear"), 1)
            nc.gpsimd.memset(logit[:, :, 0, P:SEQ], NEG).then_inc(S("logit_clear"), 1)

        @block.vector
        def _(dve):
            v = nc.vector
            chain = Chain(dve, S("dve_order"))

            def units(n, body):
                rounds = n // RING
                for t in range(min(n, RING)):
                    body(t, t % RING)
                at = RING
                if rounds > 2:
                    with dve.Fori(1, rounds) as i:
                        for u in range(RING):
                            body(i * RING + u, u)
                    at = rounds * RING
                for t in range(at, n):
                    body(t, t % RING)

            chain.step(v.memset(eps[:, 0:1], RMS_EPS))
            chain.step(v.memset(eps[:, 1:2], LN_EPS))
            v.memset(ones_d[:, :], 1.0 / D).then_inc(S("ones_ready"), 1)
            v.memset(ones_h[:, :], 1.0 / HALF).then_inc(S("ones_ready"), 1)
            v.memset(ones[:, :], 1.0).then_inc(S("ones_ready"), 1)
            chain.step(v.memset(ones_row[:, :], 1.0))
            dve.wait_ge(S("root_0"), 1)
            chain.step(v.reciprocal(rstd[:, :], rstd[:, :]))
            b_ada = vcol("b_ada", 0, 6 * KD).rearrange("p (m o) -> p m o", o=1).to_broadcast([P, 6 * KD, 2])
            dve.wait_ge(S("vec_ready"), 16)
            dve.wait_ge(S("slot_done"), N_ADA0)
            chain.step(v.tensor_tensor(modl[:, 0:2 * KD, :],
                                       ps[:, 4, 0:4 * KD].rearrange("p (m t) -> p m t", t=2),
                                       b_ada[:, 0:2 * KD, :], ALU.add))
            chain.join()
            chain.step(v.scalar_tensor_tensor(scl[:, 0:KD], modl[:, KD:2 * KD, 1], 1.0, vcol("norm_g0", 0, KD),
                                              ALU.add, ALU.mult))
            v.scalar_tensor_tensor(scl[:, KD:2 * KD], modl[:, KD:2 * KD, 0], 1.0, vcol("norm_g0", 0, KD),
                                   ALU.add, ALU.mult).then_inc(S("mod0_ready"), 1)
            chain.join()
            dve.wait_ge(S("mod0_ready"), 1)
            dve.wait_ge(S("x_ready"), 16)
            dve.wait_ge(S("ctx_ready"), 16)
            for k in range(KD):
                v.scalar_tensor_tensor(h[:, k, 0:CTX], h[:, k, 0:CTX], scl[:, k:k + 1], rstd[:, 0:CTX],
                                       ALU.mult, ALU.mult).then_inc(S("scaled_0"), 1)
                v.scalar_tensor_tensor(h[:, k, CTX:TOK], X[:, k, :], scl[:, KD + k:KD + k + 1],
                                       rstd[:, CTX:TOK], ALU.mult, ALU.mult).then_inc(S("scaled_0"), 1)

            with dve.Fori(0, KE) as c:
                chain.enter(c, 10)
                dve.wait_ge(S("xm_moved"), c + 1)
                src, dst = V[:, c + HC, :], xconv[:, c, :]
                tap = lambda n: vcol("conv_w", c * 9 + n)
                chain.step(v.tensor_scalar(dst, src, tap(4), vcol("conv_b", c), ALU.mult, ALU.add))
                grid_in = src[:, CTX:TOK].rearrange("p (y x) -> p y x", x=GRID)
                grid_out = dst[:, CTX:TOK].rearrange("p (y x) -> p y x", x=GRID)
                for n in (1, 7, 3, 5, 0, 2, 6, 8):
                    dy, dx = n // 3 - 1, n % 3 - 1
                    y0, y1, x0, x1 = max(0, -dy), ROWS - max(0, dy), max(0, -dx), GRID - max(0, dx)
                    o = grid_out[:, y0:y1, x0:x1]
                    chain.join()
                    ins = v.scalar_tensor_tensor(o, grid_in[:, y0 + dy:y1 + dy, x0 + dx:x1 + dx], tap(n), o,
                                                 ALU.mult, ALU.add)
                    chain.step(ins)
                    if n == 3:
                        o = dst[:, 1:CTX]
                        chain.step(v.scalar_tensor_tensor(o, src[:, 0:CTX - 1], tap(3), o, ALU.mult, ALU.add))
                chain.join()
                o = dst[:, 0:CTX - 1]
                v.scalar_tensor_tensor(o, src[:, 1:CTX], tap(5), o, ALU.mult, ALU.add)\
                    .then_inc(S("conv_done"), 1)
            chain.leave(KE)
            dve.wait_ge(S("slot_done"), STARTS["qk"])
            chain.step(v.tensor_tensor(modl[:, 2 * KD:6 * KD, :],
                                       ps[:, 5, 0:8 * KD].rearrange("p (m t) -> p m t", t=2),
                                       b_ada[:, 2 * KD:6 * KD, :], ALU.add))
            chain.join()
            v.scalar_tensor_tensor(scl[:, 2 * KD:3 * KD], modl[:, 4 * KD:5 * KD, 0], 1.0,
                                   vcol("norm_g1", 0, KD), ALU.add, ALU.mult).then_inc(S("mod1_ready"), 1)

            for hd in range(HEADS):
                dve.wait_ge(S("scores_done"), hd + 1)
                v.tensor_copy(scores[:, hd, :, :],
                              ps[:, 4:6, :].rearrange("p b (t j) -> p (b t) j", t=2)).then_inc(S("scores_moved"), 1)
            dve.wait_ge(S("gates_done"), HEADS)
            v.tensor_copy(gtok[:, :, :].rearrange("p t g -> p (t g)"), ps[:, 7, 0:64])\
                .then_inc(S("gtok_ready"), 1)

            dve.wait_ge(S("grow_done"), 1)
            dve.wait_ge(S("rows_ready"), 16)
            for g, a in ((0, 0), (2, 1), (1, 2), (3, 3)):
                ins = v.tensor_scalar(grow(a)[:, 0], ps[0:HEADS, 4 + g, :].rearrange("p (t j) -> p t j", t=2),
                                      rows[0:HEADS, g:g + 1], None, ALU.add)
                if a < 3:
                    chain.step(ins)
            ins.then_inc(S("grow_moved"), 1)
            rows2 = lambda a: grow(a, 2).rearrange("p r t j -> p (r t) j")
            dve.wait_ge(S("grow_log"), 1)
            chain.step(v.scalar_tensor_tensor(rows2(2), rows2(2), 0.0, rows2(4), ALU.min, ALU.subtract))
            chain.join()

            def scan(dst, src, first, op0, op1, weight=None):
                for half in range(2):
                    for d in range(2):
                        o, a = grow(dst + d)[:, 0, half], grow(src + d)[:, 0, half]
                        prev = grow(dst + d)[:, 0, 0]
                        w = a if weight is None else weight
                        if d:
                            o, a, w = o[:, ::-1], a[:, ::-1], w[:, ::-1]
                        start = first if half == 0 else (prev[:, 0:1] if d else prev[:, CTX - 1:CTX])
                        chain.step(v.tensor_tensor_scan(o, w, a, start, op0, op1))
                    chain.join()

            scan(6, 2, 0.0, ALU.mult, ALU.add, ones_row[:, :])
            v.tensor_tensor(rows2(0), rows2(0), rows2(6), ALU.subtract).then_inc(S("g_ready"), 1)
            dve.wait_ge(S("g_ready"), 1)
            scan(4, 0, 0.0, ALU.max, ALU.max)
            lat = lambda a: grow(a, 2)[:, :, 1, :]
            chain.step(v.tensor_tensor(grow(3)[:, 0], lat(4), lat(6), ALU.add))
            chain.step(v.tensor_scalar(grow(2)[:, 0], lat(4), -1.0, None, ALU.mult))
            chain.join()
            v.tensor_scalar(grow(3)[:, 0], grow(3)[:, 0], -88.0, None, ALU.max).then_inc(S("m_ready"), 1)
            dve.wait_ge(S("gcol_done"), 1)
            v.tensor_copy(gcol[:, :, :, :].rearrange("p d t h -> p (d t h)"), ps[:, 4, 0:32])\
                .then_inc(S("gcol_ready"), 1)
            dve.wait_ge(S("gcol_ready"), 1)
            dve.wait_ge(S("skip_ready"), KE)

            def mask_diagonals(hd):
                dve.wait_ge(S("spread_done"), hd + 1)
                if hd:
                    dve.wait_ge(S("wexp_ready"), hd)
                for n, (d, t, lo) in enumerate(((0, 2, 0), (0, 3, P), (1, 2, 0), (1, 3, P))):
                    ins = v.scalar_tensor_tensor(diag[:, n, :], ps[:, 0, d * SEQ + lo:d * SEQ + lo + P],
                                                 gcol[:, d, t, hd:hd + 1], cc("mask_b" if d else "mask_f"),
                                                 ALU.add, ALU.add)
                    if n < 3:
                        chain.step(ins)
                ins.then_inc(S("diag_ready"), 1)

            def normalise(hd):
                w = wexp[hd % 2]
                dve.wait_ge(S("den_done"), hd + 1)
                r = rden[:, :, :]
                chain.join()
                den = ps[:, 2, :].rearrange("p (d j) -> p d j", d=2)
                chain.step(v.scalar_tensor_tensor(r, den, -1.0, em[:, :, :], ALU.mult, ALU.max))
                chain.join()
                chain.step(v.tensor_tensor(r, den, r, ALU.max))
                chain.join()
                chain.step(v.reciprocal(r, r))
                chain.join()
                for d in range(2):
                    chain.step(v.tensor_tensor(w[:, d], w[:, d], wide(rden[:, d, :], 4), ALU.mult))
                chain.join()
                v.tensor_tensor(scores[:, hd], w[:, 0], w[:, 1], ALU.add).then_inc(S("probs_ready"), 1)

            def centre(hd):
                dve.wait_ge(S("head_mean"), hd + 1)
                a = work(2 * (hd % 2))
                v.tensor_tensor(a, a, wide(ps[:, 3, 0:SEQ], HC), ALU.subtract).then_inc(S("head_centred"), 1)

            def weigh_scores(hd):
                dve.wait_ge(S("wexp_ready"), hd + 1)
                w = wexp[hd % 2]
                chain.step(v.tensor_tensor(w[:, 0], w[:, 0], scores[:, hd], ALU.mult))
                v.tensor_tensor(w[:, 1], w[:, 1], scores[:, hd], ALU.mult).then_inc(S("weighted_ready"), 1)
                dve.wait_ge(S("weighted_ready"), hd + 1)

            def finish_head(hd):
                a = work(2 * (hd % 2))
                dve.wait_ge(S("head_root"), hd + 1)
                chain.step(v.reciprocal(rstd[:, 0:SEQ], rstd[:, 0:SEQ]))
                chain.join()
                chain.step(v.tensor_tensor(a, a, wide(rstd[:, 0:SEQ], HC), ALU.mult))
                chain.join()
                chain.step(v.tensor_tensor(a, a, o_sb[:, HC * hd:HC * hd + HC, :], ALU.mult))
                chain.join()
                for k in range(HC):
                    c = HC * hd + k
                    chain.step(v.scalar_tensor_tensor(a[:, k, :], a[:, k, :], vcol("ln_w", c),
                                                      xconv[:, c, CTX:TOK], ALU.mult, ALU.add))
                for k in range(HC):
                    c = HC * hd + k
                    chain.join(HC - 1 - k)
                    v.tensor_tensor(o_sb[:, c, :], a[:, k, :], z_sb[:, c, :], ALU.mult)\
                        .then_inc(S("y_ready"), 1)

            for n in range(HEADS + 2):
                if n < HEADS:
                    mask_diagonals(n)
                if 1 <= n <= HEADS:
                    normalise(n - 1)
                if n >= 2:
                    centre(n - 2)
                if n < HEADS:
                    weigh_scores(n)
                if n >= 2:
                    finish_head(n - 2)

            def norm(name, gain, centred, n=KD, src=X, dst=X, out=None):
                if centred:
                    dve.wait_ge(S(f"mean_{name}"), 1)
                    for k in range(n):
                        v.tensor_tensor(src[:, k, :], src[:, k, :], mean_ps, ALU.subtract)\
                            .then_inc(S(f"centred_{name}"), 1)
                    dve.wait_ge(S(f"centred_{name}"), n)
                dve.wait_ge(S(f"root_{name}"), 1)
                chain.step(v.reciprocal(rstd[:, 0:SEQ], rstd[:, 0:SEQ]))
                chain.join()
                for k in range(n):
                    v.scalar_tensor_tensor(dst[:, k, :], src[:, k, :], gain(k), rstd[:, 0:SEQ], ALU.mult, ALU.mult)\
                        .then_inc(S(out or f"scaled_{name}"), 1)
                dve.wait_ge(S(out or f"scaled_{name}"), n)

            def add_gated(name, start, block_at):
                dve.wait_ge(S("slot_done"), start)
                for m in range(KD):
                    v.scalar_tensor_tensor(X[:, m, :], acc[:, m, :], modl[:, block_at + m, 0:1], X[:, m, :],
                                           ALU.mult, ALU.add).then_inc(S(f"in_{name}"), 1)
                dve.wait_ge(S(f"in_{name}"), KD)

            def add_scaled(name, start):
                dve.wait_ge(S("slot_done"), start)
                for m in range(KD):
                    v.scalar_tensor_tensor(X[:, m, :], X[:, m, :], ALPHA, acc[:, m, :],
                                           ALU.mult, ALU.add).then_inc(S(f"in_{name}"), 1)
                dve.wait_ge(S(f"in_{name}"), KD)

            dve.wait_ge(S("mod1_ready"), 1)
            add_gated("rms1", STARTS["fin"], 2 * KD)
            norm("rms1", lambda k: scl[:, 2 * KD + k:2 * KD + k + 1], False, dst=h2)
            dve.wait_ge(S("fin_moved"), N_FIN)
            for g in range(GROUPS):
                dve.wait_ge(S("f_done"), g + 1)
                a = G[:, 2 * g:2 * g + 2, :]
                v.tensor_tensor(a, ps[:, 4 + g % 4, :].rearrange("p (c j) -> p c j", c=2), a, ALU.mult)\
                    .then_inc(S("f_moved"), 1)
            add_gated("rmsf", STARTS["evin"], 5 * KD)
            norm("rmsf", lambda k: vcol("norm_f", k), False, out="out_rmsf")

            for t in range(KH):
                dve.wait_ge(S("evin_moved"), t + 1)
                chain.step(v.tensor_tensor(pad_d[:, t, 32:], U[:, 2 * t, :], U[:, 2 * t + 1, :], ALU.mult))
            dve.wait_ge(S("evin_moved"), 6)
            dve.wait_ge(S("pads_clear"), 4)
            tap = lambda k, t: vcol("ev_conv", 3 * t + k)
            chain.join()
            for t in range(KH):
                chain.step(v.tensor_scalar(U[:, t, :], pad_d[:, t, 30:30 + SEQ], tap(0, t), None, ALU.mult))
            for k in (1, 2):
                for t in range(KH):
                    chain.join(KH - 1)
                    chain.step(v.scalar_tensor_tensor(U[:, t, :], pad_d[:, t, 30 + k:30 + k + SEQ], tap(k, t),
                                                      U[:, t, :], ALU.mult, ALU.add))
            for t in range(KH):
                chain.join(KH - 1 - t)
                v.tensor_tensor(U[:, t, :], U[:, t, :], U[:, 2 * KH + t, :], ALU.mult)\
                    .then_inc(S("evmix_ready"), 1)
            dve.wait_ge(S("evin_moved"), N_EVIN)
            a = pad_a
            for n, b in enumerate((pad_b, pad_c, pad_b, pad_c)):
                chain.join()
                chain.step(v.tensor_tensor(b[:, n:, 32:], a[:, n:, 32:], a[:, n:, 32 - (1 << n):32 - (1 << n) + SEQ],
                                           ALU.add))
                a = b
            for g, w in enumerate(WINDOWS):
                b = (pad_b, pad_c)[g % 2]
                chain.join()
                chain.step(v.scalar_tensor_tensor(h2[:, g, :], b[:, g, 32:], 1.0 / w, pad_a[:, g, 32:], ALU.mult,
                                                  ALU.subtract))
                chain.join()
                o = h2[:, g, 0:w]
                chain.step(v.tensor_tensor(o, b[:, g, 32:32 + w], cc("count", 16 * g, 16 * g + w), ALU.mult))
                chain.join()
                v.tensor_tensor(o, o, pad_a[:, g, 32:32 + w], ALU.subtract).then_inc(S("pooled_ready"), 1)
            dve.wait_ge(S("pool_done"), 1)
            for g in range(KH):
                v.tensor_scalar(U[:, KH + g, :], ps[:, g // 2, (g % 2) * SEQ:(g % 2 + 1) * SEQ],
                                vcol("pool_s", g), None, ALU.mult).then_inc(S("evmix_ready"), 1)
            add_scaled("mix0", STARTS["ffi0"])
            norm("mix0", lambda k: vcol("mix_g0", k), True)

            def feed_forward(l, start):
                def gated(t, u):
                    dve.wait_ge(S(f"gate{l}_ready"), t + 1)
                    v.tensor_tensor(G[:, t, :], gate[:, u % 2, :], ps[:, u, SEQ:2 * SEQ], ALU.mult)\
                        .then_inc(S(f"ffi{l}_moved"), 1)
                units(N_FFI, gated)
                add_scaled(f"ffn{l}", start)
                norm(f"ffn{l}", lambda k: vcol(f"ffn_g{l}", k), True)

            feed_forward(0, STARTS["odin"])

            for t in range(KH):
                dve.wait_ge(S("glu_ready"), t + 1)
                v.tensor_tensor(pad_a[:, t, 32:], gate[:, t % 2, :], ps[:, t, 0:SEQ], ALU.mult)\
                    .then_inc(S("odin_moved"), 1)
            dve.wait_ge(S("odin_moved"), KH)
            for t in range(KH):
                chain.step(v.tensor_scalar(acc31[:, t, :], pad_a[:, t, 2:2 + SEQ], vcol("dw_w", t),
                                           vcol("dw_b", t), ALU.mult, ALU.add))
            with dve.Fori(0, TAPS - 2) as k:
                chain.enter(k, KH)
                for t in range(KH):
                    chain.join(KH - 1)
                    chain.step(v.scalar_tensor_tensor(acc31[:, t, :], pad_a[:, t, bass.ds(k + 3, SEQ)],
                                                      vcol("dw_w", (k + 1) * KH + t), acc31[:, t, :],
                                                      ALU.mult, ALU.add))
            chain.leave(TAPS - 2)
            for t in range(KH):
                chain.join(KH - 1 - t)
                v.scalar_tensor_tensor(acc31[:, t, :], pad_a[:, t, TAPS + 1:TAPS + 1 + SEQ],
                                       vcol("dw_w", (TAPS - 1) * KH + t), acc31[:, t, :],
                                       ALU.mult, ALU.add).then_inc(S("in_conv"), 1)

            chain.step(v.memset(frow[:, 4, :], 1.0))
            dve.wait_ge(S("forget_done"), 1)
            v.tensor_scalar(frow[:, 0, :], ps[0:FH, 4, 0:SEQ], rows[0:FH, 4:5], None, ALU.add)\
                .then_inc(S("forget_moved"), 1)
            dve.wait_ge(S("forget_log"), 1)
            chain.step(v.scalar_tensor_tensor(frow[:, 0, :], frow[:, 0, :], 0.0, frow[:, 1, :], ALU.min,
                                              ALU.subtract))
            chain.join()
            chain.step(v.tensor_tensor_scan(frow[:, 2, :], frow[:, 4, :], frow[:, 0, :], 0.0, ALU.mult, ALU.add))
            chain.join()
            v.tensor_scalar(frow[:, 3, :], frow[:, 2, :], -float(FD) ** 0.5, None, ALU.mult)\
                .then_inc(S("cum_ready"), 1)

            dve.wait_ge(S("logit_clear"), 1)
            for hd in range(FH):
                dve.wait_ge(S("logits_done"), hd + 1)
                a = ps[:, hd % 4, :]
                chain.step(v.tensor_tensor(logit[:, hd, 0, 0:P], a[:, 0:P], cc("mask_b"), ALU.add))
                chain.step(v.tensor_tensor(logit[:, hd, 1, P:SEQ], a[:, 3 * P:4 * P], cc("mask_b"), ALU.add))
                v.tensor_copy(logit[:, hd, 1, 0:P], a[:, 2 * P:3 * P]).then_inc(S("logits_moved"), 1)
                chain.join()
                dve.wait_ge(S("logits_moved"), hd + 1)
                chain.step(v.tensor_reduce(stat[:, 0, 2 * hd:2 * hd + 2], logit[:, hd, :, :], AX.X, ALU.max))
                chain.join()
                v.tensor_scalar(stat[:, 1, 2 * hd:2 * hd + 2], stat[:, 0, 2 * hd:2 * hd + 2], -FD ** -0.5, None,
                                ALU.mult).then_inc(S("max_ready"), 1)
            for hd in range(FH):
                dve.wait_ge(S("exp_ready"), hd + 1)
                r = stat[:, 2, 2 * hd:2 * hd + 2]
                chain.step(v.reciprocal(r, r))
                chain.join()
                chain.step(v.tensor_scalar(logit[:, hd, 0, :], logit[:, hd, 0, :], r[:, 0:1], None, ALU.mult))
                v.tensor_scalar(logit[:, hd, 1, :], logit[:, hd, 1, :], r[:, 1:2], None, ALU.mult)\
                    .then_inc(S("prob_ready"), 1)
            for c in range(KH):
                dve.wait_ge(S("attn_done"), 2 * c + 2)
                v.tensor_copy(G[:, c, :], ps[:, 2 + c % 2, 0:SEQ]).then_inc(S("attn_moved"), 1)
            norm("conv", lambda k: vcol("cn_g", k), True, KH, acc31, acc31)
            add_scaled("mix1", STARTS["ffi1"])
            norm("mix1", lambda k: vcol("mix_g1", k), True)
            feed_forward(1, SLOTS)


def _columns(a):
    a = np.asarray(a)
    return np.moveaxis(a.reshape(*a.shape[:-1], -1, P), -1, 0)


def _wide_slots(w, order=None):
    blocks = w.reshape(KD, P, -1, P)
    if order is not None:
        blocks = blocks[:, :, order]
    k, p, n, c = blocks.shape
    return blocks.reshape(k, p, n // 2, 2 * c).transpose(2, 1, 0, 3).reshape(n // 2, P, SLOT)


def _deep_slots(w):
    n = w.shape[0] // (2 * P)
    return w.reshape(n, 2, P, D).transpose(0, 2, 1, 3).reshape(n, P, SLOT)


def _by_feature(x):
    return np.ascontiguousarray(x[0].T.reshape(KD, P, -1).transpose(1, 0, 2))


def _stream(a):
    pairs = lambda n: [b for t in range(n) for b in (t, n + t)]
    ada = [_wide_slots(a["w_ada"][l]) for l in range(2)]
    w_in = _wide_slots(a["m_w_in"][0])
    rest = np.concatenate([ada[0][8:], ada[1]])
    mixed = np.concatenate([np.stack([w_in[t], rest[2 * t], rest[2 * t + 1]]) for t in range(N_XM)])
    heads = np.stack([a["m_w_q"][0], a["m_w_k"][0]], axis=1).reshape(2 * HEADS, HC, P, DH)
    od = a["od_w_in_2"][0]
    od_cols = np.concatenate([od[:, 3 * HALF + FH:], od[:, :3 * HALF]], axis=1)
    parts = [ada[0][:8], mixed, heads.transpose(0, 2, 1, 3).reshape(-1, P, SLOT), w_in[8:],
             _deep_slots(a["m_w_out"][0]), _wide_slots(a["f_w_in"][0]), _deep_slots(a["f_w_out"][0]),
             _wide_slots(a["ev_w_in_2"][0], [4, 8, 5, 9, 6, 10, 7, 11, 0, 1, 2, 3, 12, 13, 14, 15]),
             _deep_slots(a["ev_w_out_2"][0]),
             _wide_slots(a["ffn_w_in_2"][0], pairs(KF)), _deep_slots(a["ffn_w_out_2"][0]),
             _wide_slots(od_cols, pairs(KH) + list(range(2 * KH, 5 * KH))), _deep_slots(a["od_w_out_2"][0]),
             _wide_slots(a["ffn_w_in_2"][1], pairs(KF)), _deep_slots(a["ffn_w_out_2"][1])]
    return np.concatenate(parts)


def _vectors(a):
    od = a["od_w_in_2"][0]
    parts = {
        "c": np.stack([_columns(a["c"][0]), _columns(a["c_ctx"])], axis=-1),
        "norm_g0": _columns(a["norm_g"][0]), "norm_g1": _columns(a["norm_g"][1]),
        "norm_f": _columns(a["norm_f"]), "b_ada": _columns(a["b_ada"]),
        "conv_w": _columns(a["m_conv_w"][0, :, :, 0].reshape(9, E)).transpose(0, 2, 1),
        "conv_b": _columns(a["m_conv_b"][0]), "ln_w": _columns(a["m_ln_w"][0]),
        "skip": _columns(a["m_skip"][0]),
        "gate_w": a["m_w_if"][0].transpose(1, 2, 0, 3).reshape(3 * KE, P, 16).transpose(1, 0, 2),
        "ev_conv": _columns(a["ev_conv_w_2"][0]).transpose(0, 2, 1),
        "pool_s": _columns(a["ev_pool_scale_2"][0]), "pool_w": a["ev_pool_w_2"][0].transpose(1, 0, 2),
        "dw_w": _columns(a["od_dw_w_2"][0]), "dw_b": _columns(a["od_dw_b_2"][0]),
        "cn_g": _columns(a["od_cn_g_2"][0]), "cn_b": _columns(a["od_cn_b_2"][0]),
        "forget_w": od[:, 3 * HALF:3 * HALF + FH].reshape(KD, P, FH).transpose(1, 0, 2),
    }
    for l in range(2):
        for k, n in (("mix", "ln_mix"), ("ffn", "ln_ffn")):
            parts[f"{k}_g{l}"] = _columns(a[f"{n}_g_2"][l])
            parts[f"{k}_b{l}"] = _columns(a[f"{n}_b_2"][l])
    return np.concatenate([parts[k].reshape(P, VEC[k][1]) for k in VEC], axis=1)


def _constants():
    c = np.zeros((P, CSTS), np.float32)
    i, j = np.arange(P)[:, None], np.arange(P)[None, :]

    def put(name, value, rows=P):
        a, n = CST[name]
        c[:rows, a:a + n] = value
    put("ident", i == j)
    put("mask_f", np.where(i <= j, 0.0, NEG))
    put("mask_b", np.where(i >= j, 0.0, NEG))
    put("count", np.concatenate([1.0 / np.minimum(np.arange(16) + 1, w) for w in WINDOWS])[None])
    put("select", np.repeat(np.eye(FH), P, axis=1), FH)
    return c


def _dft():
    a = 2 * np.pi * (np.outer(np.arange(SEQ), np.arange(SEQ)) % SEQ) / SEQ
    t = np.concatenate([np.cos(a), -np.sin(a), np.sin(a)], axis=1) / 16
    return np.ascontiguousarray(t.reshape(2, P, 3 * SEQ).transpose(1, 0, 2), np.float32)


def kernel(**inputs):
    import concourse.bacc as bacc
    from concourse.bass_utils import run_bass_kernel_spmd

    a = {k: np.asarray(v) for k, v in inputs.items()}
    rows = np.zeros((FH, 8), np.float32)
    rows[:HEADS, 0:4] = np.stack([a["m_b_i"][0, 0], a["m_b_f"][0, 0], a["m_b_i"][0, 1], a["m_b_f"][0, 1]], axis=1)
    rows[:, 4] = a["od_forget_b_2"][0]
    arrays = {"weights": _stream(a), "x": _by_feature(a["x"]), "ctx": _by_feature(a["ctx"]),
              "vectors": _vectors(a), "constants": _constants(), "dft": _dft(), "rows": rows}
    nc = bacc.Bacc("TRN2", target_bir_lowering=False, num_devices=1)
    args = [nc.dram_tensor(f"in_{k}", v.shape, F32, kind="ExternalInput").ap() for k, v in arrays.items()]
    result = nc.dram_tensor("result", (P, KD, SEQ), F32, kind="ExternalOutput").ap()
    program(nc, *args, result)
    r = run_bass_kernel_spmd(nc, [{f"in_{k}": np.ascontiguousarray(v) for k, v in arrays.items()}], core_ids=[0])
    y = np.asarray(r.results[0]["result"])
    return np.ascontiguousarray(y.transpose(2, 1, 0).reshape(1, SEQ, D))
```

```python
from contextlib import ExitStack

import numpy as np

import concourse.bass as bass
from concourse import mybir

F32 = mybir.dt.float32
F32R = mybir.dt.float32r
ALU = mybir.AluOpType
ACT = mybir.ActivationFunctionType
AX = mybir.AxisListType

P = 128
D = 1024
KD = D // P
SEQ = 256
CTX = 256
TOK = CTX + SEQ
E = 2048
KE = E // P
HEADS = 4
DH = E // HEADS
HC = DH // P
GRID = 64
ROWS = SEQ // GRID
GROUPS = 8
GD = E // GROUPS
FF = 2816
KF = FF // P
HALF = 512
KH = HALF // P
FH = 8
FD = 64
TAPS = 31
WINDOWS = (2, 4, 8, 16)
ALPHA = 4.0 ** 0.25
RMS_EPS = 1e-6
LN_EPS = 1e-5
NEG = -1e30
RING = 2
UNROLL = 4
SLOT = 2048

N_ADA0, N_XM, N_QK, N_OZ, N_ADA1, N_MOUT = 8, 8, 8, 16, 16, 8
N_FIN, N_FOUT, N_EVIN, N_EVOUT = 16, 8, 8, 4
N_FFI, N_FFO, N_ODIN, N_ODOUT = KF, KF // 2, 10, 4
STARTS = {}
_at = 0
for _name, _n in (("ada0", N_ADA0), ("xm", N_XM), ("qk", N_QK), ("oz", N_OZ), ("ada1", N_ADA1),
                  ("mout", N_MOUT),
                  ("fin", N_FIN), ("fout", N_FOUT), ("evin", N_EVIN), ("evout", N_EVOUT),
                  ("ffi0", N_FFI), ("ffo0", N_FFO), ("odin", N_ODIN), ("odout", N_ODOUT),
                  ("ffi1", N_FFI), ("ffo1", N_FFO)):
    STARTS[_name] = _at
    _at += _n
SLOTS = _at

VEC = {}
_at = 0
for _name, _n in (("c", 2 * KD), ("norm_g0", KD), ("norm_g1", KD), ("norm_f", KD), ("b_ada", 6 * KD),
                  ("conv_w", 9 * KE), ("conv_b", KE), ("ln_w", KE), ("skip", KE),
                  ("gate_w", 3 * KE * 16)):
    VEC[_name] = (_at, _n)
    _at += _n
VECS = _at

VEC2 = {}
_at = 0
for _name, _n in (("ev_conv", 3 * KH), ("pool_s", KH), ("pool_w", KH * P),
                  ("dw_w", TAPS * KH), ("dw_b", KH), ("cn_g", KH), ("cn_b", KH), ("forget_w", KD * FH),
                  ("mix_g0", KD), ("mix_b0", KD), ("ffn_g0", KD), ("ffn_b0", KD),
                  ("mix_g1", KD), ("mix_b1", KD), ("ffn_g1", KD), ("ffn_b1", KD)):
    VEC2[_name] = (_at, _n)
    _at += _n
VECS2 = _at

CST = {}
_at = 0
for _name, _n in (("ident", P), ("mask_f", P), ("mask_b", P), ("count", 4 * 16), ("select", HEADS * P),
                  ("fold", 2)):
    CST[_name] = (_at, _n)
    _at += _n
CSTS = _at


NORMS = {"rms1": (KD, False, True, False), "rmsf": (KD, False, True, True), "mix0": (KD, True, True, True),
         "ffn0": (KD, True, True, True), "conv": (KH, True, False, False), "mix1": (KD, True, True, True),
         "ffn1": (KD, True, False, True)}


def since(kind, name):
    total = 0
    for other, (n, centred, split, keep) in NORMS.items():
        if other == name:
            return total
        total += {"mean": centred, "centred": centred * n, "var": 1, "root": 1, "hi": split * n,
                  "split": split * n, "out": keep * n}.get(kind, n)


class Chain:

    def __init__(self, eng, sem):
        self.eng, self.sem, self.base, self.n = eng, sem, 0, 0

    def step(self, ins):
        ins.then_inc(self.sem, 1)
        self.n += 1

    def join(self, back=0):
        self.eng.wait_ge(self.sem, self.base + self.n - back)

    def enter(self, i, per):
        self.start, self.per = self.n, per
        self.base, self.n = i * per + self.start, 0

    def leave(self, rounds):
        assert self.n == self.per, (self.n, self.per)
        self.base, self.n = 0, self.start + rounds * self.per


def program(nc, w_in, x_in, ctx_in, vec_in, vec2_in, cst_in, dft_in, fsel_in, row_in, out):
    with ExitStack() as ctx:
        sems = {}

        def S(name):
            if name not in sems:
                sems[name] = ctx.enter_context(nc.semaphore(name))
            return sems[name]

        def tensors(stack):
            return lambda name, shape, dtype=F32: stack.enter_context(nc.sbuf_tensor(name, list(shape), dtype))

        sb = tensors(ctx)
        ring = sb("ring", (P, RING, SLOT))
        w_hi = sb("w_hi", (P, 2, SLOT), F32R)
        w_lo = sb("w_lo", (P, 2, SLOT), F32R)
        X = sb("X", (P, KD, SEQ))
        vec = sb("vec", (P, VECS))
        cst = sb("cst", (P, CSTS))
        rows = sb("rows", (FH, 8))
        ones_d = sb("ones_d", (P, P))
        ones_h = sb("ones_h", (P, P))
        ones = sb("ones", (P, P))
        modl = sb("modl", (P, 6 * KD, 2))
        scl = sb("scl", (P, 3 * KD))
        eps = sb("eps", (P, 2))
        rstd = sb("rstd", (P, TOK))

        def one_place(name, shape, *others):
            out = []
            for n, (nm, sh, dt) in enumerate((*others, (name, shape, F32))):
                stack = first if n == len(others) else ExitStack()
                out.append(tensors(stack)(nm, sh, dt))
                if stack is not first:
                    stack.close()
            return out

        first = ExitStack()
        sa = tensors(first)
        hc, scores = one_place("scores", (P, HEADS, 4, SEQ), ("hc", (P, 2, KD, CTX), F32R))
        hl, wexp2 = one_place("wexp", (P, 2, 2, 4, SEQ), ("hl", (P, 2, KD, SEQ), F32R))
        xsplit, y_hi, o_sb = one_place("o_sb", (P, KE, SEQ), ("xsplit", (P, 2, HC, TOK), F32R),
                                       ("y_hi", (P, KE, SEQ), F32R))
        y_lo, z_sb, qk = one_place("qk", (P, 2 * HC, TOK), ("y_lo", (P, KE, SEQ), F32R),
                                   ("z_sb", (P, KE, SEQ), F32))
        V = sa("V", (P, HC + KE, TOK))
        xconv = sa("xconv", (P, KE, TOK))
        ones_row = sa("ones_row", (HEADS, CTX))
        em_even = sa("em_even", (P, 2, SEQ))
        gcol = sa("gcol", (P, 2, 4, HEADS))
        silc = sa("silc", (P, KD, 2))
        silc_parts = sa("silc_parts", (P, KD, 4), F32R)
        wexp = [wexp2[:, b] for b in range(2)]
        arow = V[0:4, KE:KE + 2, :]
        gates = V[0:16, KE + 2, :]
        em = [em_even[:, :, :], V[:, KE + 3, :].rearrange("p (d j) -> p d j", d=2)]

        def work(n):
            return xconv[:, 4 * n:4 * n + 4, 0:CTX]

        def grow(a, n=1, half=slice(0, 2)):
            v = xconv[0:HEADS, :, 0:CTX].rearrange("p (r t) j -> p r t j", t=2)
            return v[:, a:a + n, half, :]

        first.close()

        second = ExitStack()
        sc = tensors(second)
        x_hi = sc("x_hi", (P, KD, SEQ), F32R)
        x_lo = sc("x_lo", (P, KD, SEQ), F32R)
        U = sc("U", (P, KE, SEQ))
        g_hi = sc("g_hi", (P, KF, SEQ), F32R)
        g_lo = sc("g_lo", (P, KF, SEQ), F32R)
        sq = sc("sq", (P, KD, SEQ))
        gate = sc("gate", (P, 2, SEQ))
        gated = sc("gated", (P, 4, SEQ))
        vec2 = sc("vec2", (P, VECS2))
        pad_a = sc("pad_a", (P, KH, 32 + SEQ))
        third = ExitStack()
        st = tensors(third)
        dft = st("dft", (P, 2, 3 * SEQ))
        pq = st("pq", (P, 2, 2, 512))
        zf = st("zf", (P, KE, SEQ))
        third.close()
        third = ExitStack()
        st = tensors(third)
        pad_b = st("pad_b", (P, KH, 32 + SEQ))
        pad_c = st("pad_c", (P, KH, 32 + SEQ))
        pad_d = st("pad_d", (P, KH, 32 + SEQ))
        h2 = st("h2", (P, KH, SEQ))
        third.close()
        acc31 = sc("acc31", (P, KH, SEQ))
        logit = sc("logit", (P, FH, 2, SEQ))
        probT = sc("probT", (P, 2, 2, SEQ))
        vtok = sc("vtok", (P, 2, HALF))
        frow = sc("frow", (FH, 5, SEQ))
        fsel = sc("fsel", (FH, FH, P))
        stat = sc("stat", (P, 3, 2 * FH))
        second.close()

        ps = ctx.enter_context(nc.psum_tensor("ps", [P, 8, 512], F32))

        def vcol(name, k=0, n=1):
            if name in VEC:
                return vec[:, bass.ds(VEC[name][0] + k, n)]
            return vec2[:, bass.ds(VEC2[name][0] + k, n)]

        def cc(name, a=0, b=None):
            o, n = CST[name]
            return cst[:, o + a:o + (n if b is None else b)]

        ident = cc("ident")
        gate_w = vcol("gate_w", 0, 48 * 16).rearrange("p (c g) -> p c g", g=16)
        forget_w = vcol("forget_w", 0, KD * FH).rearrange("p (k f) -> p k f", f=FH)
        pool_w = vcol("pool_w", 0, KH * P).rearrange("p (g d) -> p g d", d=P)
        wide_tiles = [w[:, :, :].rearrange("p s (k n) -> p s k n", k=8) for w in (w_hi, w_lo)]
        head_tiles = [w[:, :, :].rearrange("p s (k n) -> p s k n", k=4) for w in (w_hi, w_lo)]
        deep_tiles = [w[:, :, :].rearrange("p s (k n) -> p s k n", k=2) for w in (w_hi, w_lo)]
        acc = ps[:, 4:8, :].rearrange("p b n -> p (b n)").rearrange("p (m t) -> p m t", t=SEQ)
        mean_ps = ps[:, 0, 0:SEQ]
        var_ps = ps[:, 1, 0:SEQ]

        def wide(a, n):
            return a.rearrange("p (o t) -> p o t", o=1).to_broadcast([P, n, a.shape[1]])

        loaded = [S(f"weights_loaded_{s}") for s in range(RING)]
        block = ctx.enter_context(nc.Block())

        @block.sync
        def _(sp):
            for s in range(RING):
                sp.dma_start(ring[:, s, :], w_in[s]).then_inc(loaded[s], 16)
            with sp.Fori(0, SLOTS // RING - 1) as i:
                for s in range(RING):
                    sp.wait_ge(S("lo_ready"), i * (2 * RING) + 2 * s + 2)
                    sp.dma_start(ring[:, s, :], w_in[i * RING + (RING + s)]).then_inc(loaded[s], 16)
            for s in range(SLOTS % RING):
                q = SLOTS - 1
                sp.wait_ge(S("lo_ready"), 2 * (q - RING) + 2)
                sp.dma_start(ring[:, q % RING, :], w_in[q]).then_inc(loaded[q % RING], 16)
            sp.wait_ge(S("norm_out"), since("out", "ffn1") + KD)
            sp.dma_start(out, X[:, :, :]).then_inc(S("result_stored"), 16)
            sp.wait_ge(S("result_stored"), 16)

        @block.tensor
        def _(pe):
            mm = nc.tensor.matmul

            def slot(q0, body, t, u, i=0):
                for half in range(2):
                    pe.wait_ge(S("lo_ready"), i * (2 * UNROLL) + (2 * (q0 + u) + half + 1))
                    body(t, u % 4, (q0 + u) % 2, half)\
                        .then_inc(S("slot_done") if half else S("half_used"), 1)

            def walk(n, q0, body):
                for t in range(min(n, UNROLL)):
                    slot(q0, body, t, t)
                at = UNROLL
                if n // UNROLL > 2:
                    with pe.Fori(1, n // UNROLL) as i:
                        for u in range(UNROLL):
                            slot(q0, body, i * UNROLL + u, u, i)
                    at = n // UNROLL * UNROLL
                for t in range(at, n):
                    slot(q0, body, t, t)

            def triple(dst, w, x, start, stop):
                (w_h, w_l), (x_h, x_l) = w, x
                mm(dst, w_h, x_h, start=start, stop=False, skip_group_check=True)
                mm(dst, w_h, x_l, start=False, stop=False, skip_group_check=True)
                return mm(dst, w_l, x_h, start=False, stop=stop, skip_group_check=True)

            def project(n, name, x, moved, norm=None, before=0):
                def body(t, u, s, half):
                    if half == 0 and (not isinstance(t, int) or t >= 4):
                        pe.wait_ge(moved, t + (before - 3))
                    for k in range(4 * half, 4 * half + 4):
                        if norm is not None and isinstance(t, int) and t == 0:
                            pe.wait_ge(S("norm_split"), since("split", norm) + k + 1)
                        for b in range(2):
                            last = triple(ps[:, u, b * SEQ:(b + 1) * SEQ],
                                          [w[:, s, k, b * P:(b + 1) * P] for w in wide_tiles],
                                          [a[:, k, :] for a in x], k == 0 and b == 0, k == KD - 1)
                    return last
                walk(n, STARTS[name], body)

            def summing(x, wait):
                def body(t, u, s, half):
                    wait(t * 2 + half, t)
                    for m in range(KD):
                        last = triple(acc[:, m, :], [w[:, s, half, m * P:(m + 1) * P] for w in deep_tiles],
                                      [a[:, t * 2 + half, :] for a in x],
                                      isinstance(t, int) and t == 0 and half == 0 and m % 2 == 0, half == 1)
                    return last
                return body

            def accumulate(n, name, x, wait):
                walk(n, STARTS[name], summing(x, wait))

            def column_sum(dst, weight, src, n, ready, done, before=0):
                for k in range(n):
                    if ready is not None:
                        pe.wait_ge(ready, before + k + 1)
                    last = mm(dst, weight, src(k), start=(k == 0), stop=(k == n - 1))
                last.then_inc(done, 1)

            pe.wait_ge(S("silc_split"), 1)

            def ada_rows(q, bank):
                def body(t, u, s, half):
                    for k in range(4 * half, 4 * half + 4):
                        for w in wide_tiles:
                            last = mm(ps[0:4, bank, u * SEQ:(u + 1) * SEQ], silc_parts[:, k, :], w[:, s, k, :],
                                      start=(k == 0 and w is wide_tiles[0]),
                                      stop=(k == KD - 1 and w is wide_tiles[1]), skip_group_check=True)
                    return last
                for u in range(2):
                    slot(q, body, u, u)

            def ada_turn(pair, bank, col):
                pe.wait_ge(S("ada_moved"), pair + 1)
                for b in range(4):
                    last = mm(ps[:, bank, col + 2 * b:col + 2 * b + 2], arow[:, pair % 2, b * P:(b + 1) * P],
                              cc("fold")[0:4], start=True, stop=True)
                last.then_inc(S("ada_turned"), 1)

            for pair in range(N_ADA0 // 2):
                if pair >= 2:
                    pe.wait_ge(S("ada_moved"), pair - 1)
                ada_rows(2 * pair, 2 + pair % 2)
                if pair == 0:
                    pe.wait_ge(S("ident_ready"), 16)
                else:
                    ada_turn(pair - 1, 4, 8 * (pair - 1))
                if pair == 1:
                    pe.wait_ge(S("ones_ready"), 3)
                    column_sum(ps[:, 6, :], ones_d[:, :], lambda k: V[:, k, :], KD, S("squares_0"),
                               S("meansq_0"))
            ada_turn(N_ADA0 // 2 - 1, 4, 8 * (N_ADA0 // 2 - 1))

            def xm_slot(t, u, i):
                for half in range(2):
                    pe.wait_ge(S("lo_ready"), i * 4 + (2 * (STARTS["xm"] + u) + half + 1))
                    for b in range(2):
                        bank = 2 * u + b
                        if half == 0 and (not isinstance(i, int) or i > 0):
                            pe.wait_ge(S("xm_moved"), i * 4 + bank - 3)
                        for k in range(4 * half, 4 * half + 4):
                            if isinstance(i, int) and i == 0 and u == 0 and b == 0:
                                pe.wait_ge(S("h_ready"), 2 * k + 2)
                            w = [a[:, u, k, b * P:(b + 1) * P] for a in wide_tiles]
                            triple(ps[:, bank, 0:CTX], w, [hc[:, a, k, :] for a in range(2)], k == 0, False)
                            last = triple(ps[:, bank, CTX:TOK], w, [hl[:, a, k, :] for a in range(2)], False,
                                          k == KD - 1)
                    last.then_inc(S("slot_done") if half else S("half_used"), 1)

            for u in range(2):
                xm_slot(u, u, 0)
            with pe.Fori(1, N_XM // 2) as i:
                for u in range(2):
                    xm_slot(i * 2 + u, u, i)

            pe.wait_ge(S("xm_moved"), KE)
            for hd in range(HEADS):
                for part in range(2):
                    for half in range(2):
                        pe.wait_ge(S("lo_ready"), 2 * (STARTS["qk"] + 2 * hd + part) + half + 1)
                        for e in range(HC):
                            unit = 12 * hd + 4 * part + e
                            if unit >= 4 and half == 0:
                                pe.wait_ge(S("qkv_moved"), unit - 3)
                            for k in range(2 * half, 2 * half + 2):
                                if part == 0 and e == 0:
                                    pe.wait_ge(S("xc_split"), HC * hd + k + 1)
                                last = triple(ps[:, e, :], [w[:, part, k, e * P:(e + 1) * P] for w in head_tiles],
                                              [xsplit[:, a, k, :] for a in range(2)], k == 0, k == HC - 1)
                            if half:
                                last.then_inc(S("qk_done") if e < HC - 1 else S("slot_done"), 1)
                        if not half:
                            last.then_inc(S("half_used"), 1)
                xm = [V[:, HC + HC * hd + e, :] for e in range(HC)]
                for t in range(4):
                    pe.wait_ge(S("qkv_moved"), 12 * hd + 8 + t - 3)
                    for e in range(HC):
                        last = nc.tensor.transpose(ps[:, t, e * P:(e + 1) * P], xm[e][:, t * P:(t + 1) * P], ident)
                    last.then_inc(S("v_turned"), 1)
                pe.wait_ge(S("qkv_moved"), 12 * hd + 8)
                for part, src in ((2, xm), (0, [qk[:, e, :] for e in range(HC)]),
                                  (1, [qk[:, HC + e, :] for e in range(HC)])):
                    for e in range(HC):
                        last = mm(ps[0:16, 7, :], gate_w[:, part * KE + HC * hd + e, :], src[e],
                                  start=(hd == 0 and part == 2 and e == 0),
                                  stop=(hd == HEADS - 1 and part == 1 and e == HC - 1),
                                  skip_group_check=True)
                last.then_inc(S("gates_done"), 1)
                if hd:
                    pe.wait_ge(S("scores_moved"), hd)
                else:
                    pe.wait_ge(S("mod0_ready"), 1)
                for t in range(4):
                    for e in range(HC):
                        last = mm(ps[:, 4 + t // 2, (t % 2) * SEQ:(t % 2 + 1) * SEQ],
                                  qk[:, HC + e, t * P:(t + 1) * P], qk[:, e, CTX:TOK],
                                  start=(e == 0), stop=(e == HC - 1))
                last.then_inc(S("scores_done"), 1)

            pe.wait_ge(S("gates_moved"), 1)
            pe.wait_ge(S("scores_moved"), HEADS)
            for g in range(4):
                last = mm(ps[0:4, 4 + g, :], ident[0:16, 4 * g:4 * g + 4], gates, start=True, stop=True)
            last.then_inc(S("grow_done"), 1)

            pe.wait_ge(S("qkv_moved"), 12 * HEADS)
            project(N_OZ, "oz", [hl[:, a] for a in range(2)], S("oz_moved"))

            pe.wait_ge(S("g_ready"), 1)
            for d in range(2):
                for t in range(4):
                    last = nc.tensor.transpose(ps[:, 4, (d * 4 + t) * 4:(d * 4 + t) * 4 + 4],
                                               grow(d)[:, 0, t // 2, (t % 2) * P:(t % 2 + 1) * P],
                                               ident[0:HEADS, 0:HEADS])
            last.then_inc(S("gcol_done"), 1)
            pe.wait_ge(S("floor_ready"), 1)
            pe.wait_ge(S("oz_moved"), N_OZ)

            def spread(hd):
                if hd:
                    pe.wait_ge(S("diag_ready"), hd)
                    pe.wait_ge(S("wexp_ready"), hd)
                sel = cc("select", hd * P, (hd + 1) * P)[0:HEADS]
                mm(ps[:, 0, :], sel, grow(2)[:, 0], start=True, stop=True)
                mm(ps[:, 1, :], sel, grow(3)[:, 0], start=True, stop=True).then_inc(S("spread_done"), 1)

            def denominators(hd):
                pe.wait_ge(S("weighted_ready"), hd + 1)
                w = wexp[hd % 2]
                for t in range(4):
                    last = mm(ps[:, 2, :], ones[:, :], w[:, :, t, :], start=(t == 0), stop=(t == 3))
                last.then_inc(S("den_done"), 1)

            def mix_values(hd):
                pe.wait_ge(S("probs_ready"), hd + 1)
                if hd == 0:
                    pe.wait_ge(S("gcol_ready"), 1)
                if hd:
                    pe.wait_ge(S("heads_moved"), hd)
                for e in range(HC):
                    for t in range(4):
                        last = mm(ps[:, (4 if hd < HEADS - 1 else 0) + e // 2, (e % 2) * SEQ:(e % 2 + 1) * SEQ],
                                  V[:, HC * hd + t, e * P:(e + 1) * P], scores[:, hd, t, :],
                                  start=(t == 0), stop=(t == 3))
                last.then_inc(S("values_done"), 1)

            def out_slots(a, z):
                body = summing((y_hi, y_lo), lambda c, t: pe.wait_ge(S("y_ready"), c // HC + 1))
                for t in range(a, z):
                    slot(STARTS["mout"], body, t, t)

            def head_mean(hd):
                pe.wait_ge(S("heads_moved"), hd + 1)
                if hd:
                    pe.wait_ge(S("head_root"), hd)
                column_sum(ps[:, 3, 0:SEQ], ones_h[:, :], lambda k: work(2 * (hd % 2))[:, k, :], HC, None,
                           S("head_mean"))

            def head_var(hd):
                pe.wait_ge(S("head_squares"), hd + 1)
                column_sum(ps[:, 3, SEQ:2 * SEQ], ones_h[:, :], lambda k: work(3)[:, k, :], HC, None,
                           S("head_var"))

            for n in range(HEADS):
                if n >= 1:
                    denominators(n - 1)
                spread(n)
                pair = N_ADA0 // 2 + 2 * n
                ada_rows(STARTS["ada1"] + 4 * n, 6)
                ada_turn(pair, 7, 16 * n)
                if n >= 2:
                    head_mean(n - 2)
                if n >= 1:
                    mix_values(n - 1)
                if n >= 2:
                    head_var(n - 2)
                ada_rows(STARTS["ada1"] + 4 * n + 2, 6)
                ada_turn(pair + 1, 7, 16 * n + 8)
            denominators(HEADS - 1)
            head_mean(HEADS - 2)
            pe.wait_ge(S("mod1_ready"), 1)
            out_slots(0, 1)
            head_var(HEADS - 2)
            out_slots(1, 2)
            mix_values(HEADS - 1)
            out_slots(2, 3)
            head_mean(HEADS - 1)
            out_slots(3, 4)
            head_var(HEADS - 1)
            out_slots(4, N_MOUT)

            def norm(name, centred, n=KD, weight=ones_d, src=X, sqs=sq):
                if centred:
                    column_sum(mean_ps, weight[:, :], lambda k: src[:, k, :], n, S("norm_in"),
                               S("norm_mean"), since("in", name))
                column_sum(var_ps, weight[:, :], lambda k: sqs[:, k, :], n, S("norm_squares"),
                           S("norm_var"), since("squares", name))

            norm("rms1", False)
            pe.wait_ge(S("dft_ready"), 16)
            project(N_FIN, "fin", (x_hi, x_lo), S("fin_moved"), "rms1")

            pe.wait_ge(S("fin_moved"), N_FIN)
            def channels(g):
                if g >= 2:
                    pe.wait_ge(S("pq_moved"), 2 * (g - 1))
                for n in range(2):
                    for k in range(2):
                        last = mm(ps[:, 2 * (g % 2) + n, :], U[:, 2 * g + k, n * P:(n + 1) * P], dft[:, k, 0:512],
                                  start=(k == 0), stop=(k == 1))
                    last.then_inc(S("pq_done"), 1)

            def positions(g):
                pe.wait_ge(S("pq_moved"), 2 * (g + 1))
                if g >= 4:
                    pe.wait_ge(S("f_moved"), g - 3)
                for c in range(2):
                    for n in range(2):
                        for q, col in ((0, 0), (1, 2 * SEQ)):
                            last = mm(ps[:, 4 + g % 4, c * SEQ:(c + 1) * SEQ],
                                      pq[:, g % 2, n, q * SEQ + c * P:q * SEQ + (c + 1) * P],
                                      dft[:, n, col:col + SEQ], start=(n == 0 and q == 0), stop=(n == 1 and q == 1))
                last.then_inc(S("f_done"), 1)

            channels(0)
            for g in range(GROUPS):
                if g + 1 < GROUPS:
                    channels(g + 1)
                positions(g)
            pe.wait_ge(S("f_moved"), GROUPS)
            accumulate(N_FOUT, "fout", (g_hi, g_lo), lambda c, t: pe.wait_ge(S("fy_split"), c // 2 + 1))
            norm("rmsf", False)

            project(N_EVIN, "evin", (x_hi, x_lo), S("evin_moved"), "rmsf")
            pe.wait_ge(S("evin_moved"), N_EVIN)
            for g in range(KH):
                pe.wait_ge(S("pooled_ready"), g + 1)
                last = mm(ps[:, g // 2, (g % 2) * SEQ:(g % 2 + 1) * SEQ], pool_w[:, g, :], h2[:, g, :],
                          start=True, stop=True)
            last.then_inc(S("pool_done"), 1)
            accumulate(N_EVOUT, "evout", (g_hi, g_lo), lambda c, t: pe.wait_ge(S("evmix_split"), c + 1))
            norm("mix0", True)

            def feed_forward(l):
                project(N_FFI, f"ffi{l}", (x_hi, x_lo), S("ffi_moved"), f"mix{l}", N_FFI * l)
                accumulate(N_FFO, f"ffo{l}", (g_hi, g_lo),
                           lambda c, t: pe.wait_ge(S("ffi_split"), N_FFI * l + c + 1))
                norm(f"ffn{l}", True)

            feed_forward(0)

            def odd_in(t, u, s, half):
                if half == 0 and t >= 4:
                    pe.wait_ge(S("odin_moved"), t - 3)
                for k in range(4 * half, 4 * half + 4):
                    if t == 0:
                        pe.wait_ge(S("norm_split"), since("split", "ffn0") + k + 1)
                    for b in range(2):
                        w = [a[:, s, k, b * P:(b + 1) * P] for a in wide_tiles]
                        x = [a[:, k, :] for a in (x_hi, x_lo)]
                        if t >= 8:
                            w, x = [a[:, k, b * P:(b + 1) * P] for a in (x_hi, x_lo)], \
                                [a[:, s, k, :] for a in wide_tiles]
                        last = triple(ps[:, u, b * SEQ:(b + 1) * SEQ], w, x, k == 0 and b == 0, k == KD - 1)
                return last

            walk(N_ODIN, STARTS["odin"], odd_in)
            pe.wait_ge(S("norm_out"), since("out", "ffn0") + KD)
            for k in range(KD):
                last = mm(ps[0:FH, 4, 0:SEQ], forget_w[:, k, :], X[:, k, :], start=(k == 0), stop=(k == KD - 1))
            last.then_inc(S("forget_done"), 1)

            pe.wait_ge(S("cum_ready"), 1)
            pe.wait_ge(S("fsel_ready"), 16)
            pe.wait_ge(S("odin_moved"), N_ODIN)
            for hd in range(FH):
                if hd >= 4:
                    pe.wait_ge(S("logits_moved"), hd - 3)
                lo = FD * (hd % 2)
                for t in range(2):
                    n = P * (t + 1)
                    mm(ps[:, hd % 4, t * SEQ:t * SEQ + n], U[lo:lo + FD, hd // 2, t * P:(t + 1) * P],
                       U[lo:lo + FD, KH + hd // 2, 0:n], start=True, stop=False)
                    last = mm(ps[:, hd % 4, t * SEQ:t * SEQ + n], fsel[:, hd, :],
                              frow[:, 3, 0:n], start=False, stop=True)
                last.then_inc(S("logits_done"), 1)
            for hd in range(FH):
                pe.wait_ge(S("prob_ready"), hd + 1)
                if hd >= 2:
                    pe.wait_ge(S("probT_moved"), hd - 1)
                b = hd % 2
                if hd < 2:
                    pe.wait_ge(S("logits_moved"), FH)
                nc.tensor.transpose(ps[:, b, 0:P], logit[:, hd, 0, 0:P], ident)
                nc.tensor.transpose(ps[:, b, P:2 * P], logit[:, hd, 1, 0:P], ident)
                nc.tensor.transpose(ps[:, b, 3 * P:4 * P], logit[:, hd, 1, P:2 * P], ident)\
                    .then_inc(S("probT_done"), 1)
                pe.wait_ge(S("probT_moved"), hd + 1)
                lo, c = FD * (hd % 2), hd // 2
                if c >= 2 and hd % 2 == 0:
                    pe.wait_ge(S("attn_moved"), c - 1)
                mm(ps[lo:lo + FD, 2 + c % 2, 0:SEQ], vtok[:, 0, hd * FD:(hd + 1) * FD], probT[:, b, 0, :],
                   start=True, stop=False, skip_group_check=True)
                mm(ps[lo:lo + FD, 2 + c % 2, P:SEQ], vtok[:, 1, hd * FD:(hd + 1) * FD], probT[:, b, 1, P:SEQ],
                   start=False, stop=True, skip_group_check=True).then_inc(S("attn_done"), 1)
            pe.wait_ge(S("attn_moved"), KH)
            def mixed(c, t):
                if c == KH:
                    norm("conv", True, KH, ones_h, acc31)
                if c >= KH:
                    pe.wait_ge(S("conv_split"), c - KH + 1)
                else:
                    pe.wait_ge(S("attn_split"), c + 1)

            accumulate(N_ODOUT, "odout", (g_hi, g_lo), mixed)
            norm("mix1", True)
            feed_forward(1)

        @block.scalar
        def _(act):
            do = nc.scalar.activation
            chain = Chain(act, S("act_order"))

            def hi(q, i=0, per=0):
                if isinstance(q, int) and q >= SLOTS:
                    return
                act.wait_ge(loaded[q % RING], i * (16 * per // RING) + (q // RING + 1) * 16)
                for half in range(2):
                    if q >= 2:
                        act.wait_ge(S("slot_done" if half else "half_used"), i * per + (q - 1))
                    part = slice(half * SLOT // 2, (half + 1) * SLOT // 2)
                    do(w_hi[:, q % 2, part], ring[:, q % RING, part], ACT.Copy).then_inc(S("hi_ready"), 1)

            def units(n, name, body=None):
                q0 = STARTS[name]

                def unit(t, u, i=0):
                    hi(q0 + u + 2, i, UNROLL)
                    if body is not None:
                        body(t, u % UNROLL)

                for t in range(min(n, UNROLL)):
                    unit(t, t)
                at = UNROLL
                if n // UNROLL > 2:
                    with act.Fori(1, n // UNROLL - 1) as i:
                        for u in range(UNROLL):
                            unit(i * UNROLL + u, u, i)
                    at = (n // UNROLL - 1) * UNROLL
                for t in range(at, n):
                    unit(t, t)

            act.dma_start(vec[:, :], vec_in).then_inc(S("vec_ready"), 16)
            act.dma_start(X[:, :, :], x_in).then_inc(S("x_ready"), 16)
            act.dma_start(xconv[:, 0:KD, 0:CTX], ctx_in).then_inc(S("ctx_ready"), 16)
            act.dma_start(cst[:, :], cst_in).then_inc(S("ident_ready"), 16)
            act.dma_start(rows[:, :], row_in).then_inc(S("rows_ready"), 16)
            act.wait_ge(S("vec_ready"), 16)
            do(silc[:, :, :].rearrange("p k t -> p (k t)"), vcol("c", 0, 2 * KD), ACT.Silu)\
                .then_inc(S("silc_ready"), 1)
            act.wait_ge(S("silc_ready"), 1)
            do(silc_parts[:, :, 0:2], silc[:, :, :], ACT.Copy).then_inc(S("silc_rounded"), 1)
            hi(0)
            hi(1)
            act.wait_ge(S("x_ready"), 16)
            for k in range(KD):
                chain.step(do(V[:, k, CTX:TOK], X[:, k, :], ACT.Square))
            hi(2)
            act.wait_ge(S("ctx_ready"), 16)
            for k in range(KD):
                do(V[:, k, 0:CTX], xconv[:, k, 0:CTX], ACT.Square).then_inc(S("squares_0"), 1)
            for q in range(3, N_ADA0 - 1):
                hi(q)
            act.wait_ge(S("meansq_0"), 1)
            do(rstd[:, :], ps[:, 6, :], ACT.Sqrt, bias=eps[:, 0:1]).then_inc(S("root_0"), 1)
            hi(N_ADA0 - 1)
            for k in range(KD):
                if k in (0, 3):
                    hi(STARTS["xm"] + k // 3)
                for t, col, dst in ((0, 1, hc), (1, 0, hl)):
                    act.wait_ge(S("scaled_0"), 2 * k + t + 1)
                    do(dst[:, 0, k, :], V[:, k, t * CTX:t * CTX + SEQ], ACT.Identity,
                       bias=modl[:, k, col:col + 1]).then_inc(S("h_rounded"), 1)

            def move_xm(i, u):
                act.wait_ge(S("slot_done"), i * 2 + (STARTS["xm"] + u + 1))
                for b in range(2):
                    do(V[:, i * 4 + (HC + 2 * u + b), :], ps[:, 2 * u + b, :], ACT.Copy)\
                        .then_inc(S("xm_moved"), 1)

            def silu(i, u):
                for b in range(2):
                    act.wait_ge(S("conv_done"), i * 4 + (2 * u + b + 1))
                    a = xconv[:, i * 4 + (2 * u + b), :]
                    do(a, a, ACT.Silu).then_inc(S("xconv_ready"), 1)

            for u in range(2):
                hi(STARTS["xm"] + 2 + u)
                move_xm(0, u)
            with act.Fori(1, N_XM // 2 - 1) as i:
                for u in range(2):
                    hi(STARTS["xm"] + 2 + u, i, 2)
                    move_xm(i, u)
                    silu(i - 1, u)

            def round_head(hd):
                if hd:
                    act.wait_ge(S("slot_done"), STARTS["qk"] + 2 * hd)
                for k in range(HC):
                    act.wait_ge(S("xconv_ready"), HC * hd + k + 1)
                    do(xsplit[:, 0, k, :], xconv[:, HC * hd + k, :], ACT.Copy).then_inc(S("xc_rounded"), 1)

            round_head(0)
            for u in range(2):
                hi(STARTS["qk"] + u)
                move_xm(N_XM // 2 - 1, u)
                silu(N_XM // 2 - 2, u)
            for u in range(2):
                silu(N_XM // 2 - 1, u)

            for hd in range(HEADS):
                for r in range(12):
                    if r < 8:
                        if r % 4 < 3:
                            act.wait_ge(S("qk_done"), 6 * hd + 3 * (r // 4) + r % 4 + 1)
                        else:
                            act.wait_ge(S("slot_done"), STARTS["qk"] + 2 * hd + r // 4 + 1)
                        if r == 0 and hd:
                            act.wait_ge(S("scores_done"), hd)
                        do(qk[:, r, :], ps[:, r % 4, :], ACT.Copy, scale=1.0 if r < 4 else DH ** -0.5)\
                            .then_inc(S("qkv_moved"), 1)
                        if r % 4 == 3:
                            hi(STARTS["qk"] + 2 * hd + r // 4 + 2)
                    else:
                        act.wait_ge(S("v_turned"), 4 * hd + r - 7)
                        if r == 8 and hd:
                            act.wait_ge(S("gates_done"), hd)
                        do(V[:, HC * hd + r - 8, :], ps[:, r % 4, :], ACT.Copy).then_inc(S("qkv_moved"), 1)
                if hd < HEADS - 1:
                    round_head(hd + 1)

            def softplus_of_minus(x, t, ready, done):
                act.wait_ge(ready, 1)
                chain.step(do(t, x, ACT.Abs))
                chain.join()
                chain.step(do(t, t, ACT.Exp, scale=-1.0))
                chain.join()
                do(t, t, ACT.Ln, bias=1.0).then_inc(done, 1)

            rows2 = lambda a: grow(a, 2).rearrange("p r t j -> p (r t) j")
            softplus_of_minus(rows2(2), rows2(4), S("grow_moved"), S("grow_log"))
            act.wait_ge(S("m_ready"), 1)
            do(grow(3)[:, 0], grow(3)[:, 0], ACT.Exp, scale=-1.0).then_inc(S("floor_ready"), 1)
            def move_oz(t, u):
                if t == 8:
                    act.wait_ge(S("scores_done"), HEADS)
                act.wait_ge(S("slot_done"), STARTS["oz"] + t + 1)
                dst = (o_sb if t < 8 else z_sb)[:, 2 * (t % 8):2 * (t % 8) + 2, :]
                do(dst, ps[:, u, :].rearrange("p (b j) -> p b j", b=2), ACT.Sigmoid if t < 8 else ACT.Silu)\
                    .then_inc(S("oz_moved"), 1)

            for t in range(N_OZ):
                hi(STARTS["oz"] + t + 2)
                move_oz(t, t % 4)

            def weigh(hd):
                w = wexp[hd % 2]
                act.wait_ge(S("spread_done"), hd + 1)
                if hd >= 2:
                    act.wait_ge(S("probs_ready"), hd - 1)
                else:
                    act.wait_ge(S("gcol_ready"), 1)
                    act.wait_ge(S("wexp_clear"), 4)
                chain.step(do(em[hd % 2], ps[:, 1, :].rearrange("p (d j) -> p d j", d=2), ACT.Copy))
                act.wait_ge(S("diag_ready"), hd + 1)
                for d, t, lo, hi in ((0, 0, 0, SEQ), (0, 1, 0, SEQ), (0, 2, P, SEQ),
                                     (1, 0, 0, SEQ), (1, 1, 0, SEQ), (1, 3, 0, P)):
                    chain.step(do(w[:, d, t, lo:hi], ps[:, 0, d * SEQ + lo:d * SEQ + hi], ACT.Exp,
                                  bias=gcol[:, d, t, hd:hd + 1]))
                for n, (d, t, lo) in enumerate(((0, 2, 0), (0, 3, P), (1, 2, 0), (1, 3, P))):
                    last = do(w[:, d, t, lo:lo + P], w[:, d, t, lo:lo + P], ACT.Exp)
                    if n < 3:
                        chain.step(last)
                last.then_inc(S("wexp_ready"), 1)

            def move_rows(pair):
                act.wait_ge(S("slot_done"), STARTS["ada1"] + 2 * pair + 2 - N_ADA0)
                act.wait_ge(S("ada_turned"), pair - 1)
                do(arow[:, pair % 2, :], ps[0:4, 6, :], ACT.Copy).then_inc(S("ada_moved"), 1)

            def move_values(hd):
                act.wait_ge(S("values_done"), hd + 1)
                if hd >= 2:
                    act.wait_ge(S("y_ready"), hd - 1)
                at = 4 if hd < HEADS - 1 else 0
                do(work(2 * (hd % 2)), ps[:, at:at + 2, :].rearrange("p b (c j) -> p (b c) j", c=2), ACT.Copy)\
                    .then_inc(S("heads_moved"), 1)

            def squares(hd):
                act.wait_ge(S("head_centred"), hd + 1)
                if hd:
                    act.wait_ge(S("head_var"), hd)
                do(work(3), work(2 * (hd % 2)), ACT.Square).then_inc(S("head_squares"), 1)

            def root(hd):
                act.wait_ge(S("head_var"), hd + 1)
                if hd:
                    act.wait_ge(S("y_rounded"), hd)
                do(rstd[:, 0:SEQ], ps[:, 3, SEQ:2 * SEQ], ACT.Sqrt, bias=eps[:, 0:1])\
                    .then_inc(S("head_root"), 1)

            for n in range(HEADS):
                hi(STARTS["ada1"] + 4 * n + 2)
                hi(STARTS["ada1"] + 4 * n + 3)
                move_rows(N_ADA0 // 2 + 2 * n)
                weigh(n)
                if n >= 2:
                    squares(n - 2)
                if n >= 1:
                    move_values(n - 1)
                if n >= 2:
                    root(n - 2)
                hi(STARTS["ada1"] + 4 * n + 4)
                hi(STARTS["ada1"] + 4 * n + 5)
                move_rows(N_ADA0 // 2 + 2 * n + 1)
            squares(HEADS - 2)
            hi(STARTS["mout"] + 2)
            root(HEADS - 2)
            hi(STARTS["mout"] + 3)
            move_values(HEADS - 1)
            hi(STARTS["mout"] + 4)
            squares(HEADS - 1)
            hi(STARTS["mout"] + 5)
            root(HEADS - 1)
            for t in range(6, N_MOUT + 2):
                hi(STARTS["mout"] + t)

            def norm(name, bias, n=KD, src=X, centred=True, split=True, keep=True):
                for k in range(n):
                    kind = "centred" if centred else "in"
                    act.wait_ge(S(f"norm_{kind}"), since(kind, name) + k + 1)
                    do(sq[:, k, :], src[:, k, :], ACT.Square).then_inc(S("norm_squares"), 1)
                act.wait_ge(S("norm_var"), since("var", name) + 1)
                e = 1 if centred else 0
                do(rstd[:, 0:SEQ], var_ps, ACT.Sqrt, bias=eps[:, e:e + 1]).then_inc(S("norm_root"), 1)
                if name == "conv":
                    for k in range(n):
                        act.wait_ge(S("norm_scaled"), since("scaled", name) + k + 1)
                        do(g_hi[:, KH + k, :], src[:, k, :], ACT.Silu, bias=bias(k)).then_inc(S("conv_hi"), 1)
                    for k in range(n):
                        do(sq[:, k, :], src[:, k, :], ACT.Silu, bias=bias(k)).then_inc(S("conv_whole"), 1)
                    return

                def shift(dst, k, done):
                    act.wait_ge(S("norm_scaled"), since("scaled", name) + k + 1)
                    if bias is None:
                        do(dst[:, k, :], sq[:, k, :], ACT.Copy).then_inc(done, 1)
                    else:
                        do(dst[:, k, :], sq[:, k, :], ACT.Identity, bias=bias(k)).then_inc(done, 1)

                if split:
                    for k in range(n):
                        shift(x_hi, k, S("norm_hi"))
                if keep:
                    for k in range(n):
                        shift(X, k, S("norm_out"))

            act.wait_ge(S("y_ready"), HEADS)
            act.dma_start(dft[:, :, :], dft_in).then_inc(S("dft_ready"), 16)
            act.dma_start(vec2[:, :], vec2_in).then_inc(S("vec2_ready"), 16)
            norm("rms1", lambda k: modl[:, 3 * KD + k, 0:1], centred=False, keep=False)

            def move_fin(t, u):
                act.wait_ge(S("slot_done"), STARTS["fin"] + t + 1)
                dst = (U if t < 8 else zf)[:, 2 * (t % 8):2 * (t % 8) + 2, :]
                do(dst, ps[:, u, :].rearrange("p (b j) -> p b j", b=2), ACT.Copy if t < 8 else ACT.Silu)\
                    .then_inc(S("fin_moved"), 1)

            for t in range(N_FIN):
                hi(STARTS["fin"] + t + 2)
                move_fin(t, t % 4)
            for g in range(GROUPS):
                if g >= 2:
                    act.wait_ge(S("f_done"), g - 1)
                for n in range(2):
                    act.wait_ge(S("pq_done"), 2 * g + n + 1)
                    do(pq[:, g % 2, n, :], ps[:, 2 * (g % 2) + n, :], ACT.Copy).then_inc(S("pq_moved"), 1)
            units(N_FOUT, "fout")
            norm("rmsf", None, centred=False)

            act.wait_ge(S("pads_clear"), 4)
            def move_evin(t, u):
                act.wait_ge(S("slot_done"), STARTS["evin"] + t + 1)
                if t < 6:
                    dst = U[:, 2 * t:2 * t + 2, :]
                else:
                    dst = pad_a[:, 2 * (t - 6):2 * (t - 6) + 2, 32:]
                do(dst, ps[:, u, :].rearrange("p (b j) -> p b j", b=2), ACT.Copy)\
                    .then_inc(S("evin_moved"), 1)

            units(N_EVIN, "evin", move_evin)
            units(N_EVOUT, "evout")
            norm("mix0", lambda k: vcol("mix_b0", k))
            act.dma_start(fsel[:, :, :], fsel_in).then_inc(S("fsel_ready"), 16)

            def feed_forward(l):
                def gating(t, u):
                    act.wait_ge(S("slot_done"), t + (STARTS[f"ffi{l}"] + 1))
                    if not isinstance(t, int) or t >= 2:
                        act.wait_ge(S("ffi_moved"), t + (N_FFI * l - 1))
                    do(gate[:, u % 2, :], ps[:, u, 0:SEQ], ACT.Silu).then_inc(S("gate_ready"), 1)
                units(N_FFI, f"ffi{l}", gating)
                units(N_FFO, f"ffo{l}")
                norm(f"ffn{l}", lambda k: vcol(f"ffn_b{l}", k), split=l == 0)

            feed_forward(0)

            def move_odin(t, u):
                act.wait_ge(S("slot_done"), STARTS["odin"] + t + 1)
                if t < 4:
                    if t >= 2:
                        act.wait_ge(S("odin_moved"), t - 1)
                    do(gate[:, t % 2, :], ps[:, t, SEQ:2 * SEQ], ACT.Sigmoid).then_inc(S("glu_ready"), 1)
                    return
                if t == 4:
                    act.wait_ge(S("odin_moved"), 4)
                if t < 8:
                    dst = U[:, 2 * (t - 4):2 * (t - 4) + 2, :]
                else:
                    dst = vtok[:, :, (t - 8) * SEQ:(t - 7) * SEQ]
                do(dst, ps[:, u, :].rearrange("p (b j) -> p b j", b=2), ACT.Copy)\
                    .then_inc(S("odin_moved"), 1)

            units(N_ODIN, "odin", move_odin)
            softplus_of_minus(frow[:, 0, :], frow[:, 1, :], S("forget_moved"), S("forget_log"))
            for hd in range(FH):
                act.wait_ge(S("max_ready"), hd + 1)
                for t in range(2):
                    a = logit[:, hd, t, :]
                    last = do(a, a, ACT.Exp, scale=FD ** -0.5, bias=stat[:, 1, 2 * hd + t:2 * hd + t + 1],
                              accum_out=stat[:, 2, 2 * hd + t:2 * hd + t + 1])
                    if t == 0:
                        chain.step(last)
                last.then_inc(S("exp_ready"), 1)
            for hd in range(FH):
                act.wait_ge(S("probT_done"), hd + 1)
                if hd >= 2:
                    act.wait_ge(S("attn_done"), hd - 1)
                chain.step(do(probT[:, hd % 2, 0, :], ps[:, hd % 2, 0:SEQ], ACT.Copy))
                do(probT[:, hd % 2, 1, P:SEQ], ps[:, hd % 2, 3 * P:4 * P], ACT.Copy)\
                    .then_inc(S("probT_moved"), 1)
            hi(STARTS["odout"] + 2)
            norm("conv", lambda k: vcol("cn_b", k), KH, acc31)
            for t in range(1, N_ODOUT):
                hi(STARTS["odout"] + t + 2)
            norm("mix1", lambda k: vcol("mix_b1", k))
            feed_forward(1)

        @block.gpsimd
        def _(pool):
            sub = nc.gpsimd.tensor_tensor
            def lo(q):
                for half in range(2):
                    pool.wait_ge(S("hi_ready"), 2 * q + half + 1)
                    part = slice(half * SLOT // 2, (half + 1) * SLOT // 2)
                    sub(w_lo[:, q % 2, part], ring[:, q % RING, part], w_hi[:, q % 2, part],
                        ALU.subtract).then_inc(S("lo_ready"), 1)

            pool.wait_ge(S("lo_ready"), 2 * STARTS["xm"])
            for q in range(STARTS["xm"], STARTS["qk"] + 2):
                lo(q)
            pool.wait_ge(S("slot_done"), STARTS["oz"])
            pool.wait_ge(S("vec_ready"), 16)
            for c in range(KE):
                a = xconv[:, c, CTX:TOK]
                nc.gpsimd.tensor_scalar(a, a, vcol("skip", c), None, ALU.mult).then_inc(S("skip_ready"), 1)
            pool.wait_ge(S("slot_done"), STARTS["ada1"])
            for b in range(2):
                for d, t, j in ((0, 3, 0), (1, 2, P)):
                    nc.gpsimd.memset(wexp[b][:, d, t, j:j + P], 0.0).then_inc(S("wexp_clear"), 1)
            def rest_of_y(hd):
                pool.wait_ge(S("y_rounded"), hd + 1)
                c = slice(HC * hd, HC * hd + HC)
                sub(y_lo[:, c, :], work(2 * (hd % 2)), y_hi[:, c, :], ALU.subtract).then_inc(S("y_ready"), 1)

            pool.wait_ge(S("lo_ready"), 2 * (STARTS["ada1"] + 2))
            for n in range(HEADS):
                for t in range(4 * n + 2, 4 * n + 6):
                    lo(STARTS["ada1"] + t)
                if n >= 2:
                    rest_of_y(n - 2)
            for hd in range(2, HEADS):
                rest_of_y(hd)
            for g in range(GROUPS):
                pool.wait_ge(S("fy_rounded"), g + 1)
                c = slice(2 * g, 2 * g + 2)
                sub(g_lo[:, c, :], zf[:, c, :], g_hi[:, c, :], ALU.subtract).then_inc(S("fy_split"), 1)
            pool.wait_ge(S("norm_in"), since("in", "rmsf") + KD)
            for a in (pad_a, pad_b, pad_c, pad_d):
                nc.gpsimd.memset(a[:, :, 0:32], 0.0).then_inc(S("pads_clear"), 1)
            for c in range(2 * KH):
                pool.wait_ge(S("evmix_rounded"), c + 1)
                sub(g_lo[:, c, :], U[:, c, :], g_hi[:, c, :], ALU.subtract).then_inc(S("evmix_split"), 1)

            def feed_forward(l):
                def rest(t, u):
                    pool.wait_ge(S("ffi_rounded"), t + (N_FFI * l + 1))
                    sub(g_lo[:, t, :], gated[:, u, :], g_hi[:, t, :], ALU.subtract).then_inc(S("ffi_split"), 1)
                for t in range(4):
                    rest(t, t)
                with pool.Fori(1, N_FFI // 4) as i:
                    for u in range(4):
                        rest(i * 4 + u, u)
                for t in range(N_FFI // 4 * 4, N_FFI):
                    rest(t, t % 4)

            pool.wait_ge(S("norm_in"), since("in", "mix0") + KD)
            nc.gpsimd.memset(logit[:, :, 0, P:SEQ], NEG).then_inc(S("logit_clear"), 1)
            feed_forward(0)
            for c in range(KH):
                pool.wait_ge(S("attn_rounded"), c + 1)
                sub(g_lo[:, c, :], gated[:, c, :], g_hi[:, c, :], ALU.subtract).then_inc(S("attn_split"), 1)
            feed_forward(1)

        @block.vector
        def _(dve):
            v = nc.vector
            chain = Chain(dve, S("dve_order"))

            def lo(q, i=0, per=0, halves=(0, 1)):
                if isinstance(q, int) and q >= SLOTS:
                    return
                for half in halves:
                    dve.wait_ge(S("hi_ready"), i * (2 * per) + (2 * q + half + 1))
                    part = slice(half * SLOT // 2, (half + 1) * SLOT // 2)
                    v.tensor_tensor(w_lo[:, q % 2, part], ring[:, q % RING, part], w_hi[:, q % 2, part],
                                    ALU.subtract).then_inc(S("lo_ready"), 1)

            def units(n, name, body=None):
                q0 = STARTS[name]
                for t in range(min(n, UNROLL)):
                    lo(q0 + t + 2, halves=(0,) if body is None and t == n - 1 else (0, 1))
                    if body is not None:
                        body(t, t)
                at = UNROLL
                if n // UNROLL > 2:
                    with dve.Fori(1, n // UNROLL - 1) as i:
                        for u in range(UNROLL):
                            lo(q0 + u + 2, i, UNROLL)
                            if body is not None:
                                body(i * UNROLL + u, u)
                    at = (n // UNROLL - 1) * UNROLL
                for t in range(at, n):
                    lo(q0 + t + 2, halves=(0,) if body is None and t == n - 1 else (0, 1))
                    if body is not None:
                        body(t, t % 4)

            chain.step(v.memset(eps[:, 0:1], RMS_EPS))
            chain.step(v.memset(eps[:, 1:2], LN_EPS))
            v.memset(ones_d[:, :], 1.0 / D).then_inc(S("ones_ready"), 1)
            v.memset(ones_h[:, :], 1.0 / HALF).then_inc(S("ones_ready"), 1)
            v.memset(ones[:, :], 1.0).then_inc(S("ones_ready"), 1)
            chain.step(v.memset(ones_row[:, :], 1.0))
            dve.wait_ge(S("silc_rounded"), 1)
            v.tensor_tensor(silc_parts[:, :, 2:4], silc[:, :, :], silc_parts[:, :, 0:2], ALU.subtract)\
                .then_inc(S("silc_split"), 1)
            lo(0)
            lo(1)
            for pair in range(N_ADA0 // 2):
                for q in (2 * pair + 2, 2 * pair + 3):
                    if q < N_ADA0:
                        lo(q)
                dve.wait_ge(S("slot_done"), 2 * pair + 2)
                if pair >= 2:
                    dve.wait_ge(S("ada_turned"), pair - 1)
                v.tensor_copy(arow[:, pair % 2, :], ps[0:4, 2 + pair % 2, :]).then_inc(S("ada_moved"), 1)
            dve.wait_ge(S("root_0"), 1)
            chain.step(v.reciprocal(rstd[:, :], rstd[:, :]))
            b_ada = vcol("b_ada", 0, 6 * KD).rearrange("p (m o) -> p m o", o=1).to_broadcast([P, 6 * KD, 2])
            dve.wait_ge(S("vec_ready"), 16)
            dve.wait_ge(S("ada_turned"), N_ADA0 // 2)
            chain.step(v.tensor_tensor(modl[:, 0:2 * KD, :],
                                       ps[:, 4, 0:4 * KD].rearrange("p (m t) -> p m t", t=2),
                                       b_ada[:, 0:2 * KD, :], ALU.add))
            chain.join()
            chain.step(v.scalar_tensor_tensor(scl[:, 0:KD], modl[:, KD:2 * KD, 1], 1.0, vcol("norm_g0", 0, KD),
                                              ALU.add, ALU.mult))
            v.scalar_tensor_tensor(scl[:, KD:2 * KD], modl[:, KD:2 * KD, 0], 1.0, vcol("norm_g0", 0, KD),
                                   ALU.add, ALU.mult).then_inc(S("mod0_ready"), 1)
            chain.join()
            dve.wait_ge(S("mod0_ready"), 1)
            dve.wait_ge(S("x_ready"), 16)
            dve.wait_ge(S("ctx_ready"), 16)
            def rest_of_h(k):
                for t, col, dst in ((0, 1, hc), (1, 0, hl)):
                    dve.wait_ge(S("h_rounded"), 2 * k + t + 1)
                    v.scalar_tensor_tensor(dst[:, 1, k, :], V[:, k, t * CTX:t * CTX + SEQ],
                                           modl[:, k, col:col + 1], dst[:, 0, k, :], ALU.add, ALU.subtract)\
                        .then_inc(S("h_ready"), 1)

            for k in range(KD):
                v.scalar_tensor_tensor(V[:, k, 0:CTX], xconv[:, k, 0:CTX], scl[:, k:k + 1], rstd[:, 0:CTX],
                                       ALU.mult, ALU.mult).then_inc(S("scaled_0"), 1)
                v.scalar_tensor_tensor(V[:, k, CTX:TOK], X[:, k, :], scl[:, KD + k:KD + k + 1],
                                       rstd[:, CTX:TOK], ALU.mult, ALU.mult).then_inc(S("scaled_0"), 1)
                if k:
                    rest_of_h(k - 1)
            rest_of_h(KD - 1)

            def convolve(c):
                tap = lambda b, n: vcol("conv_w", (c + b) * 9 + n)
                src = [V[:, c + (HC + b), :] for b in range(2)]
                dst = [xconv[:, c + b, :] for b in range(2)]
                grid_in, grid_out = [[a[:, CTX:TOK].rearrange("p (y x) -> p y x", x=GRID) for a in s]
                                     for s in (src, dst)]
                for b in range(2):
                    dve.wait_ge(S("xm_moved"), c + (b + 1))
                    chain.step(v.tensor_scalar(dst[b], src[b], tap(b, 4), vcol("conv_b", c + b), ALU.mult, ALU.add))
                for n in (1, 7, 3, 5, 0, 2, 6, 8):
                    dy, dx = n // 3 - 1, n % 3 - 1
                    y0, y1, x0, x1 = max(0, -dy), ROWS - max(0, dy), max(0, -dx), GRID - max(0, dx)
                    for b in range(2):
                        o = grid_out[b][:, y0:y1, x0:x1]
                        chain.join(1)
                        chain.step(v.scalar_tensor_tensor(o, grid_in[b][:, y0 + dy:y1 + dy, x0 + dx:x1 + dx],
                                                          tap(b, n), o, ALU.mult, ALU.add))
                        if n == 3:
                            o = dst[b][:, 1:CTX]
                            chain.step(v.scalar_tensor_tensor(o, src[b][:, 0:CTX - 1], tap(b, 3), o,
                                                              ALU.mult, ALU.add))
                chain.join()
                for b in range(2):
                    o = dst[b][:, 0:CTX - 1]
                    v.scalar_tensor_tensor(o, src[b][:, 1:CTX], tap(b, 5), o, ALU.mult, ALU.add)\
                        .then_inc(S("conv_done"), 1)

            def split_head(hd):
                for k in range(HC):
                    dve.wait_ge(S("xc_rounded"), HC * hd + k + 1)
                    v.tensor_tensor(xsplit[:, 1, k, :], xconv[:, HC * hd + k, :], xsplit[:, 0, k, :],
                                    ALU.subtract).then_inc(S("xc_split"), 1)

            for u in range(2):
                convolve(2 * u)
            with dve.Fori(1, N_XM // 2 - 1) as i:
                chain.enter(i - 1, 40)
                for u in range(2):
                    convolve(i * 4 + 2 * u)
            chain.leave(N_XM // 2 - 2)
            split_head(0)
            for c in range(KE - 4, KE, 2):
                convolve(c)
            dve.wait_ge(S("lo_ready"), 2 * (STARTS["qk"] + 2))

            for hd in range(HEADS):
                lo(STARTS["qk"] + 2 * hd + 2)
                lo(STARTS["qk"] + 2 * hd + 3)
                if hd < HEADS - 1:
                    split_head(hd + 1)
                dve.wait_ge(S("scores_done"), hd + 1)
                v.tensor_copy(scores[:, hd, :, :],
                              ps[:, 4:6, :].rearrange("p b (t j) -> p (b t) j", t=2)).then_inc(S("scores_moved"), 1)
            dve.wait_ge(S("gates_done"), HEADS)
            v.tensor_copy(gates, ps[0:16, 7, :]).then_inc(S("gates_moved"), 1)

            dve.wait_ge(S("grow_done"), 1)
            dve.wait_ge(S("rows_ready"), 16)
            for g, a in ((0, 0), (2, 1), (1, 2), (3, 3)):
                ins = v.tensor_scalar(grow(a)[:, 0], ps[0:HEADS, 4 + g, :].rearrange("p (t j) -> p t j", t=2),
                                      rows[0:HEADS, g:g + 1], None, ALU.add)
                if a < 3:
                    chain.step(ins)
            ins.then_inc(S("grow_moved"), 1)
            rows2 = lambda a: grow(a, 2).rearrange("p r t j -> p (r t) j")
            dve.wait_ge(S("grow_log"), 1)
            chain.step(v.scalar_tensor_tensor(rows2(2), rows2(2), 0.0, rows2(4), ALU.min, ALU.subtract))
            chain.join()

            def scan(dst, src, first, op0, op1, weight=None):
                for half in range(2):
                    for d in range(2):
                        o, a = grow(dst + d)[:, 0, half], grow(src + d)[:, 0, half]
                        prev = grow(dst + d)[:, 0, 0]
                        w = a if weight is None else weight
                        if d:
                            o, a, w = o[:, ::-1], a[:, ::-1], w[:, ::-1]
                        start = first if half == 0 else (prev[:, 0:1] if d else prev[:, CTX - 1:CTX])
                        chain.step(v.tensor_tensor_scan(o, w, a, start, op0, op1))
                    chain.join()

            scan(6, 2, 0.0, ALU.mult, ALU.add, ones_row[:, :])
            v.tensor_tensor(rows2(0), rows2(0), rows2(6), ALU.subtract).then_inc(S("g_ready"), 1)
            dve.wait_ge(S("g_ready"), 1)
            scan(4, 0, 0.0, ALU.max, ALU.max)
            lat = lambda a: grow(a, 2)[:, :, 1, :]
            chain.step(v.tensor_tensor(grow(3)[:, 0], lat(4), lat(6), ALU.add))
            chain.step(v.tensor_scalar(grow(2)[:, 0], lat(4), -1.0, None, ALU.mult))
            chain.join()
            v.tensor_scalar(grow(3)[:, 0], grow(3)[:, 0], -88.0, None, ALU.max).then_inc(S("m_ready"), 1)
            for t in range(N_OZ):
                lo(STARTS["oz"] + t + 2)
            dve.wait_ge(S("gcol_done"), 1)
            v.tensor_copy(gcol[:, :, :, :].rearrange("p d t h -> p (d t h)"), ps[:, 4, 0:32])\
                .then_inc(S("gcol_ready"), 1)
            dve.wait_ge(S("gcol_ready"), 1)
            dve.wait_ge(S("skip_ready"), KE)

            def mask_diagonals(hd):
                dve.wait_ge(S("spread_done"), hd + 1)
                if hd >= 2:
                    dve.wait_ge(S("den_done"), hd - 1)
                else:
                    dve.wait_ge(S("slot_done"), STARTS["ada1"])
                for n, (d, t, lo) in enumerate(((0, 2, 0), (0, 3, P), (1, 2, 0), (1, 3, P))):
                    ins = v.scalar_tensor_tensor(wexp[hd % 2][:, d, t, lo:lo + P], ps[:, 0, d * SEQ + lo:d * SEQ + lo + P],
                                                 gcol[:, d, t, hd:hd + 1], cc("mask_b" if d else "mask_f"),
                                                 ALU.add, ALU.add)
                    if n < 3:
                        chain.step(ins)
                ins.then_inc(S("diag_ready"), 1)

            def normalise(hd):
                w = wexp[hd % 2]
                dve.wait_ge(S("den_done"), hd + 1)
                r = em[hd % 2]
                chain.join()
                den = ps[:, 2, :].rearrange("p (d j) -> p d j", d=2)
                chain.step(v.scalar_tensor_tensor(r, den, -1.0, r, ALU.mult, ALU.max))
                chain.join()
                chain.step(v.tensor_tensor(r, den, r, ALU.max))
                chain.join()
                chain.step(v.reciprocal(r, r))
                chain.join()
                for d in range(2):
                    chain.step(v.tensor_tensor(w[:, d], w[:, d], wide(r[:, d, :], 4), ALU.mult))
                chain.join()
                v.tensor_tensor(scores[:, hd], w[:, 0], w[:, 1], ALU.add).then_inc(S("probs_ready"), 1)

            def centre(hd):
                dve.wait_ge(S("head_mean"), hd + 1)
                a = work(2 * (hd % 2))
                v.tensor_tensor(a, a, wide(ps[:, 3, 0:SEQ], HC), ALU.subtract).then_inc(S("head_centred"), 1)

            def weigh_scores(hd):
                dve.wait_ge(S("wexp_ready"), hd + 1)
                w = wexp[hd % 2]
                chain.step(v.tensor_tensor(w[:, 0], w[:, 0], scores[:, hd], ALU.mult))
                v.tensor_tensor(w[:, 1], w[:, 1], scores[:, hd], ALU.mult).then_inc(S("weighted_ready"), 1)
                dve.wait_ge(S("weighted_ready"), hd + 1)

            def finish_head(hd):
                a = work(2 * (hd % 2))
                dve.wait_ge(S("head_root"), hd + 1)
                chain.step(v.reciprocal(rstd[:, 0:SEQ], rstd[:, 0:SEQ]))
                chain.join()
                chain.step(v.tensor_tensor(a, a, wide(rstd[:, 0:SEQ], HC), ALU.mult))
                chain.join()
                chain.step(v.tensor_tensor(a, a, o_sb[:, HC * hd:HC * hd + HC, :], ALU.mult))
                chain.join()
                for k in range(HC):
                    c = HC * hd + k
                    chain.step(v.scalar_tensor_tensor(a[:, k, :], a[:, k, :], vcol("ln_w", c),
                                                      xconv[:, c, CTX:TOK], ALU.mult, ALU.add))
                chain.join()
                c = slice(HC * hd, HC * hd + HC)
                chain.step(v.tensor_tensor(a, a, z_sb[:, c, :], ALU.mult))
                chain.join()
                v.tensor_copy(y_hi[:, c, :], a).then_inc(S("y_rounded"), 1)

            def rest_of_modulation():
                dve.wait_ge(S("ada_turned"), (N_ADA0 + N_ADA1) // 2)
                chain.step(v.tensor_tensor(modl[:, 2 * KD:6 * KD, :],
                                           ps[:, 7, 0:8 * KD].rearrange("p (m t) -> p m t", t=2),
                                           b_ada[:, 2 * KD:6 * KD, :], ALU.add))
                chain.join()
                v.scalar_tensor_tensor(scl[:, 2 * KD:3 * KD], modl[:, 4 * KD:5 * KD, 0], 1.0,
                                       vcol("norm_g1", 0, KD), ALU.add, ALU.mult).then_inc(S("mod1_ready"), 1)

            for n in range(HEADS):
                if n >= 1:
                    normalise(n - 1)
                mask_diagonals(n)
                if n >= 2:
                    centre(n - 2)
                weigh_scores(n)
                if n >= 2:
                    finish_head(n - 2)
            rest_of_modulation()
            normalise(HEADS - 1)
            centre(HEADS - 2)
            dve.wait_ge(S("lo_ready"), 2 * (STARTS["mout"] + 2))
            lo(STARTS["mout"] + 2)
            finish_head(HEADS - 2)
            lo(STARTS["mout"] + 3)
            centre(HEADS - 1)
            lo(STARTS["mout"] + 4)
            lo(STARTS["mout"] + 5)
            finish_head(HEADS - 1)
            for t in range(6, N_MOUT + 2):
                lo(STARTS["mout"] + t, halves=(0, 1) if t < N_MOUT + 1 else (0,))

            def norm(name, gain, centred, n=KD, src=X, bias=None, split=True):
                dst = sq if src is X else src
                if centred:
                    dve.wait_ge(S("norm_mean"), since("mean", name) + 1)
                    for k in range(n):
                        v.tensor_tensor(src[:, k, :], src[:, k, :], mean_ps, ALU.subtract)\
                            .then_inc(S("norm_centred"), 1)
                    dve.wait_ge(S("norm_centred"), since("centred", name) + n)
                dve.wait_ge(S("norm_root"), since("root", name) + 1)
                chain.step(v.reciprocal(rstd[:, 0:SEQ], rstd[:, 0:SEQ]))
                chain.join()
                for k in range(n + 2 * split):
                    if k < n:
                        v.scalar_tensor_tensor(dst[:, k, :], src[:, k, :], gain(k), rstd[:, 0:SEQ],
                                               ALU.mult, ALU.mult).then_inc(S("norm_scaled"), 1)
                    if split and k >= 2:
                        k -= 2
                        dve.wait_ge(S("norm_hi"), since("hi", name) + k + 1)
                        v.scalar_tensor_tensor(x_lo[:, k, :], sq[:, k, :], 0.0 if bias is None else bias(k),
                                               x_hi[:, k, :], ALU.add, ALU.subtract)\
                            .then_inc(S("norm_split"), 1)

            def add_gated(name, stage, block_at):
                if stage != "mout":
                    units(STARTS[name_after[stage]] - STARTS[stage], stage)
                dve.wait_ge(S("slot_done"), STARTS[name_after[stage]])
                for m in range(KD):
                    v.scalar_tensor_tensor(X[:, m, :], acc[:, m, :], modl[:, block_at + m, 0:1], X[:, m, :],
                                           ALU.mult, ALU.add).then_inc(S("norm_in"), 1)
                lo(STARTS[name_after[stage]] + 1, halves=(1,))
                dve.wait_ge(S("norm_in"), since("in", name) + KD)

            def add_scaled(name, stage, n):
                units(n, stage)
                dve.wait_ge(S("slot_done"), STARTS[stage] + n)
                for m in range(KD):
                    v.scalar_tensor_tensor(X[:, m, :], X[:, m, :], ALPHA, acc[:, m, :],
                                           ALU.mult, ALU.add).then_inc(S("norm_in"), 1)
                lo(STARTS[stage] + n + 1, halves=(1,))
                dve.wait_ge(S("norm_in"), since("in", name) + KD)

            name_after = {"mout": "fin", "fout": "evin"}
            dve.wait_ge(S("mod1_ready"), 1)
            add_gated("rms1", "mout", 2 * KD)
            norm("rms1", lambda k: scl[:, 2 * KD + k:2 * KD + k + 1], False,
                 bias=lambda k: modl[:, 3 * KD + k, 0:1])
            for t in range(N_FIN):
                lo(STARTS["fin"] + t + 2)
            dve.wait_ge(S("fin_moved"), N_FIN)
            for g in range(GROUPS):
                dve.wait_ge(S("f_done"), g + 1)
                a = zf[:, 2 * g:2 * g + 2, :]
                v.tensor_tensor(a, ps[:, 4 + g % 4, :].rearrange("p (c j) -> p c j", c=2), a, ALU.mult)\
                    .then_inc(S("f_moved"), 1)
                dve.wait_ge(S("f_moved"), g + 1)
                v.tensor_copy(g_hi[:, 2 * g:2 * g + 2, :], a).then_inc(S("fy_rounded"), 1)
            add_gated("rmsf", "fout", 5 * KD)
            norm("rmsf", lambda k: vcol("norm_f", k), False)

            dve.wait_ge(S("vec2_ready"), 16)
            for t in range(KH):
                lo(STARTS["evin"] + t + 2)
                dve.wait_ge(S("evin_moved"), t + 1)
                chain.step(v.tensor_tensor(pad_d[:, t, 32:], U[:, 2 * t, :], U[:, 2 * t + 1, :], ALU.mult))
            for t in range(KH, N_EVIN):
                lo(STARTS["evin"] + t + 2)
            dve.wait_ge(S("evin_moved"), 6)
            dve.wait_ge(S("pads_clear"), 4)
            tap = lambda k, t: vcol("ev_conv", 3 * t + k)
            chain.join()
            for t in range(KH):
                chain.step(v.tensor_scalar(U[:, t, :], pad_d[:, t, 30:30 + SEQ], tap(0, t), None, ALU.mult))
            for k in (1, 2):
                for t in range(KH):
                    chain.join(KH - 1)
                    chain.step(v.scalar_tensor_tensor(U[:, t, :], pad_d[:, t, 30 + k:30 + k + SEQ], tap(k, t),
                                                      U[:, t, :], ALU.mult, ALU.add))
            for t in range(KH):
                chain.join(KH - 1 - t)
                chain.step(v.tensor_tensor(U[:, t, :], U[:, t, :], U[:, 2 * KH + t, :], ALU.mult))
            for t in range(KH):
                chain.join(KH - 1 - t)
                v.tensor_copy(g_hi[:, t, :], U[:, t, :]).then_inc(S("evmix_rounded"), 1)
            dve.wait_ge(S("evin_moved"), N_EVIN)
            a = pad_a
            for n, b in enumerate((pad_b, pad_c, pad_b, pad_c)):
                chain.join()
                chain.step(v.tensor_tensor(b[:, n:, 32:], a[:, n:, 32:], a[:, n:, 32 - (1 << n):32 - (1 << n) + SEQ],
                                           ALU.add))
                a = b
            for g, w in enumerate(WINDOWS):
                b = (pad_b, pad_c)[g % 2]
                chain.join()
                chain.step(v.scalar_tensor_tensor(h2[:, g, :], b[:, g, 32:], 1.0 / w, pad_a[:, g, 32:], ALU.mult,
                                                  ALU.subtract))
                chain.join()
                o = h2[:, g, 0:w]
                chain.step(v.tensor_tensor(o, b[:, g, 32:32 + w], cc("count", 16 * g, 16 * g + w), ALU.mult))
                chain.join()
                v.tensor_tensor(o, o, pad_a[:, g, 32:32 + w], ALU.subtract).then_inc(S("pooled_ready"), 1)
            dve.wait_ge(S("pool_done"), 1)
            for g in range(KH):
                chain.step(v.tensor_scalar(U[:, KH + g, :], ps[:, g // 2, (g % 2) * SEQ:(g % 2 + 1) * SEQ],
                                           vcol("pool_s", g), None, ALU.mult))
                chain.join()
                v.tensor_copy(g_hi[:, KH + g, :], U[:, KH + g, :]).then_inc(S("evmix_rounded"), 1)
            add_scaled("mix0", "evout", N_EVOUT)
            norm("mix0", lambda k: vcol("mix_g0", k), True, bias=lambda k: vcol("mix_b0", k))

            def feed_forward(l):
                def gating(t, u):
                    dve.wait_ge(S("gate_ready"), t + (N_FFI * l + 1))
                    if not isinstance(t, int) or t >= 4:
                        dve.wait_ge(S("ffi_split"), t + (N_FFI * l - 3))
                    v.tensor_tensor(gated[:, u, :], gate[:, u % 2, :], ps[:, u, SEQ:2 * SEQ], ALU.mult)\
                        .then_inc(S("ffi_moved"), 1)
                    dve.wait_ge(S("ffi_moved"), t + (N_FFI * l + 1))
                    v.tensor_copy(g_hi[:, t, :], gated[:, u, :]).then_inc(S("ffi_rounded"), 1)
                units(N_FFI, f"ffi{l}", gating)
                add_scaled(f"ffn{l}", f"ffo{l}", N_FFO)
                norm(f"ffn{l}", lambda k: vcol(f"ffn_g{l}", k), True, bias=lambda k: vcol(f"ffn_b{l}", k),
                     split=l == 0)

            feed_forward(0)

            for t in range(KH):
                lo(STARTS["odin"] + t + 2)
                dve.wait_ge(S("glu_ready"), t + 1)
                v.tensor_tensor(pad_a[:, t, 32:], gate[:, t % 2, :], ps[:, t, 0:SEQ], ALU.mult)\
                    .then_inc(S("odin_moved"), 1)
            dve.wait_ge(S("odin_moved"), KH)
            for t in range(KH):
                chain.step(v.tensor_scalar(acc31[:, t, :], pad_a[:, t, 2:2 + SEQ], vcol("dw_w", t),
                                           vcol("dw_b", t), ALU.mult, ALU.add))

            def taps(k):
                for t in range(KH):
                    chain.join(KH - 1)
                    chain.step(v.scalar_tensor_tensor(acc31[:, t, :], pad_a[:, t, bass.ds(k + 2, SEQ)],
                                                      vcol("dw_w", k * KH + t), acc31[:, t, :],
                                                      ALU.mult, ALU.add))

            for n in range(6):
                with dve.Fori(0, 5) as k:
                    chain.enter(k, KH)
                    taps(k + (1 + 5 * n))
                chain.leave(5)
                lo(STARTS["odin"] + KH + n + 2)

            chain.join()
            v.memset(frow[:, 4, :], 1.0).then_inc(S("norm_in"), KH)
            dve.wait_ge(S("norm_in"), since("in", "conv") + KH)
            dve.wait_ge(S("forget_done"), 1)
            v.tensor_scalar(frow[:, 0, :], ps[0:FH, 4, 0:SEQ], rows[0:FH, 4:5], None, ALU.add)\
                .then_inc(S("forget_moved"), 1)
            dve.wait_ge(S("forget_log"), 1)
            chain.step(v.scalar_tensor_tensor(frow[:, 0, :], frow[:, 0, :], 0.0, frow[:, 1, :], ALU.min,
                                              ALU.subtract))
            chain.join()
            chain.step(v.tensor_tensor_scan(frow[:, 2, :], frow[:, 4, :], frow[:, 0, :], 0.0, ALU.mult, ALU.add))
            chain.join()
            v.tensor_scalar(frow[:, 3, :], frow[:, 2, :], -float(FD) ** 0.5, None, ALU.mult)\
                .then_inc(S("cum_ready"), 1)

            dve.wait_ge(S("logit_clear"), 1)
            for hd in range(FH):
                dve.wait_ge(S("logits_done"), hd + 1)
                a = ps[:, hd % 4, :]
                chain.step(v.tensor_tensor(logit[:, hd, 0, 0:P], a[:, 0:P], cc("mask_b"), ALU.add))
                chain.step(v.tensor_tensor(logit[:, hd, 1, P:SEQ], a[:, 3 * P:4 * P], cc("mask_b"), ALU.add))
                v.tensor_copy(logit[:, hd, 1, 0:P], a[:, 2 * P:3 * P]).then_inc(S("logits_moved"), 1)
                chain.join()
                dve.wait_ge(S("logits_moved"), hd + 1)
                chain.step(v.tensor_reduce(stat[:, 0, 2 * hd:2 * hd + 2], logit[:, hd, :, :], AX.X, ALU.max))
                chain.join()
                v.tensor_scalar(stat[:, 1, 2 * hd:2 * hd + 2], stat[:, 0, 2 * hd:2 * hd + 2], -FD ** -0.5, None,
                                ALU.mult).then_inc(S("max_ready"), 1)
            for hd in range(FH):
                dve.wait_ge(S("exp_ready"), hd + 1)
                r = stat[:, 2, 2 * hd:2 * hd + 2]
                chain.step(v.reciprocal(r, r))
                chain.join()
                chain.step(v.tensor_scalar(logit[:, hd, 0, :], logit[:, hd, 0, :], r[:, 0:1], None, ALU.mult))
                v.tensor_scalar(logit[:, hd, 1, :], logit[:, hd, 1, :], r[:, 1:2], None, ALU.mult)\
                    .then_inc(S("prob_ready"), 1)
            for c in range(KH):
                dve.wait_ge(S("attn_done"), 2 * c + 2)
                v.tensor_copy(gated[:, c, :], ps[:, 2 + c % 2, 0:SEQ]).then_inc(S("attn_moved"), 1)
                dve.wait_ge(S("attn_moved"), c + 1)
                v.tensor_copy(g_hi[:, c, :], gated[:, c, :]).then_inc(S("attn_rounded"), 1)
            lo(STARTS["odout"] + 2)
            norm("conv", lambda k: vcol("cn_g", k), True, KH, acc31, split=False)
            for k in range(KH):
                dve.wait_ge(S("conv_whole"), k + 1)
                v.tensor_tensor(g_lo[:, KH + k, :], sq[:, k, :], g_hi[:, KH + k, :], ALU.subtract)\
                    .then_inc(S("conv_split"), 1)
            for t in range(1, N_ODOUT):
                lo(STARTS["odout"] + t + 2, halves=(0, 1) if t < N_ODOUT - 1 else (0,))
            dve.wait_ge(S("slot_done"), STARTS["ffi1"])
            for m in range(KD):
                v.scalar_tensor_tensor(X[:, m, :], X[:, m, :], ALPHA, acc[:, m, :],
                                       ALU.mult, ALU.add).then_inc(S("norm_in"), 1)
            lo(STARTS["ffi1"] + 1, halves=(1,))
            dve.wait_ge(S("norm_in"), since("in", "mix1") + KD)
            norm("mix1", lambda k: vcol("mix_g1", k), True, bias=lambda k: vcol("mix_b1", k))
            feed_forward(1)


def _columns(a):
    a = np.asarray(a)
    return np.moveaxis(a.reshape(*a.shape[:-1], -1, P), -1, 0)


def _wide_slots(w, order=None):
    blocks = w.reshape(KD, P, -1, P)
    if order is not None:
        blocks = blocks[:, :, order]
    k, p, n, c = blocks.shape
    return blocks.reshape(k, p, n // 2, 2 * c).transpose(2, 1, 0, 3).reshape(n // 2, P, SLOT)


def _deep_slots(w):
    n = w.shape[0] // (2 * P)
    return w.reshape(n, 2, P, D).transpose(0, 2, 1, 3).reshape(n, P, SLOT)


def _by_feature(x):
    return np.ascontiguousarray(x[0].T.reshape(KD, P, -1).transpose(1, 0, 2))


def _stream(a):
    pairs = lambda n: [b for t in range(n) for b in (t, n + t)]
    ada = [_wide_slots(a["w_ada"][l]) for l in range(2)]
    w_in = _wide_slots(a["m_w_in"][0])
    heads = np.stack([a["m_w_q"][0], a["m_w_k"][0]], axis=1).reshape(2 * HEADS, HC, P, DH)
    od = a["od_w_in_2"][0]
    od_cols = np.concatenate([od[:, 3 * HALF + FH:], od[:, :3 * HALF]], axis=1)
    parts = [ada[0][:8], w_in[:8], heads.transpose(0, 2, 1, 3).reshape(-1, P, SLOT), w_in[8:], ada[0][8:],
             ada[1], _deep_slots(a["m_w_out"][0]), _wide_slots(a["f_w_in"][0]), _deep_slots(a["f_w_out"][0]),
             _wide_slots(a["ev_w_in_2"][0], [4, 8, 5, 9, 6, 10, 7, 11, 0, 1, 2, 3, 12, 13, 14, 15]),
             _deep_slots(a["ev_w_out_2"][0]),
             _wide_slots(a["ffn_w_in_2"][0], pairs(KF)), _deep_slots(a["ffn_w_out_2"][0]),
             _wide_slots(od_cols, pairs(KH) + list(range(2 * KH, 5 * KH))), _deep_slots(a["od_w_out_2"][0]),
             _wide_slots(a["ffn_w_in_2"][1], pairs(KF)), _deep_slots(a["ffn_w_out_2"][1])]
    return np.concatenate(parts)


def _vectors(a):
    od = a["od_w_in_2"][0]
    parts = {
        "c": np.stack([_columns(a["c"][0]), _columns(a["c_ctx"])], axis=-1),
        "norm_g0": _columns(a["norm_g"][0]), "norm_g1": _columns(a["norm_g"][1]),
        "norm_f": _columns(a["norm_f"]), "b_ada": _columns(a["b_ada"]),
        "conv_w": _columns(a["m_conv_w"][0, :, :, 0].reshape(9, E)).transpose(0, 2, 1),
        "conv_b": _columns(a["m_conv_b"][0]), "ln_w": _columns(a["m_ln_w"][0]),
        "skip": _columns(a["m_skip"][0]),
        "gate_w": a["m_w_if"][0].transpose(1, 2, 0, 3).reshape(3 * KE, P, 16).transpose(1, 0, 2),
        "ev_conv": _columns(a["ev_conv_w_2"][0]).transpose(0, 2, 1),
        "pool_s": _columns(a["ev_pool_scale_2"][0]), "pool_w": a["ev_pool_w_2"][0].transpose(1, 0, 2),
        "dw_w": _columns(a["od_dw_w_2"][0]), "dw_b": _columns(a["od_dw_b_2"][0]),
        "cn_g": _columns(a["od_cn_g_2"][0]), "cn_b": _columns(a["od_cn_b_2"][0]),
        "forget_w": od[:, 3 * HALF:3 * HALF + FH].reshape(KD, P, FH).transpose(1, 0, 2),
    }
    for l in range(2):
        for k, n in (("mix", "ln_mix"), ("ffn", "ln_ffn")):
            parts[f"{k}_g{l}"] = _columns(a[f"{n}_g_2"][l])
            parts[f"{k}_b{l}"] = _columns(a[f"{n}_b_2"][l])
    return [np.concatenate([parts[k].reshape(P, table[k][1]) for k in table], axis=1) for table in (VEC, VEC2)]


def _constants():
    c = np.zeros((P, CSTS), np.float32)
    i, j = np.arange(P)[:, None], np.arange(P)[None, :]

    def put(name, value, rows=P):
        a, n = CST[name]
        c[:rows, a:a + n] = value
    put("ident", i == j)
    put("mask_f", np.where(i <= j, 0.0, NEG))
    put("mask_b", np.where(i >= j, 0.0, NEG))
    put("count", np.concatenate([1.0 / np.minimum(np.arange(16) + 1, w) for w in WINDOWS])[None])
    put("fold", np.tile(np.eye(2), (2, 1)), 4)
    put("select", np.repeat(np.eye(HEADS), P, axis=1), HEADS)
    return c


def _dft():
    a = 2 * np.pi * (np.outer(np.arange(SEQ), np.arange(SEQ)) % SEQ) / SEQ
    t = np.concatenate([np.cos(a), -np.sin(a), np.sin(a)], axis=1) / 16
    return np.ascontiguousarray(t.reshape(2, P, 3 * SEQ).transpose(1, 0, 2), np.float32)


def kernel(**inputs):
    import concourse.bacc as bacc
    from concourse.bass_utils import run_bass_kernel_spmd

    a = {k: np.asarray(v) for k, v in inputs.items()}
    rows = np.zeros((FH, 8), np.float32)
    rows[:HEADS, 0:4] = np.stack([a["m_b_i"][0, 0], a["m_b_f"][0, 0], a["m_b_i"][0, 1], a["m_b_f"][0, 1]], axis=1)
    rows[:, 4] = a["od_forget_b_2"][0]
    vectors, vectors2 = _vectors(a)
    select = np.repeat(np.eye(FH, dtype=np.float32), P, axis=1).reshape(FH, FH, P)
    arrays = {"weights": _stream(a), "x": _by_feature(a["x"]), "ctx": _by_feature(a["ctx"]),
              "vectors": vectors, "vectors2": vectors2, "constants": _constants(), "dft": _dft(),
              "select": select, "rows": rows}
    nc = bacc.Bacc("TRN2", target_bir_lowering=False, num_devices=1)
    args = [nc.dram_tensor(f"in_{k}", v.shape, F32, kind="ExternalInput").ap() for k, v in arrays.items()]
    result = nc.dram_tensor("result", (P, KD, SEQ), F32, kind="ExternalOutput").ap()
    program(nc, *args, result)
    r = run_bass_kernel_spmd(nc, [{f"in_{k}": np.ascontiguousarray(v) for k, v in arrays.items()}], core_ids=[0])
    y = np.asarray(r.results[0]["result"])
    return np.ascontiguousarray(y.transpose(2, 1, 0).reshape(1, SEQ, D))
```

```python
from contextlib import ExitStack

import numpy as np

import concourse.bass as bass
from concourse import mybir

F32 = mybir.dt.float32
F32R = mybir.dt.float32r
ALU = mybir.AluOpType
ACT = mybir.ActivationFunctionType
AX = mybir.AxisListType

P = 128
D = 1024
KD = D // P
SEQ = 256
CTX = 256
TOK = CTX + SEQ
E = 2048
KE = E // P
HEADS = 4
DH = E // HEADS
HC = DH // P
GRID = 64
ROWS = SEQ // GRID
GROUPS = 8
GD = E // GROUPS
FF = 2816
KF = FF // P
HALF = 512
KH = HALF // P
FH = 8
FD = 64
TAPS = 31
WINDOWS = (2, 4, 8, 16)
ALPHA = 4.0 ** 0.25
RMS_EPS = 1e-6
LN_EPS = 1e-5
NEG = -1e30
RING = 2
DFT_H = GD // 2 + 1
DFT_C = 2 * DFT_H
UNROLL = 4
SLOT = 2048

N_ADA0, N_XM, N_QK, N_OZ, N_ADA1, N_MOUT = 8, 8, 8, 16, 16, 8
N_FIN, N_FOUT, N_EVIN, N_EVOUT = 16, 8, 8, 4
N_FFI, N_FFO, N_ODIN, N_ODOUT = KF, KF // 2, 10, 4
STARTS = {}
_at = 0
for _name, _n in (("ada0", N_ADA0), ("xm", N_XM), ("qk", N_QK), ("oz", N_OZ), ("ada1", N_ADA1),
                  ("mout", N_MOUT),
                  ("fin", N_FIN), ("fout", N_FOUT), ("evin", N_EVIN), ("evout", N_EVOUT),
                  ("ffi0", N_FFI), ("ffo0", N_FFO), ("odin", N_ODIN), ("odout", N_ODOUT),
                  ("ffi1", N_FFI), ("ffo1", N_FFO)):
    STARTS[_name] = _at
    _at += _n
SLOTS = _at
STARTS["end"] = _at

VEC = {}
_at = 0
for _name, _n in (("c", 2 * KD), ("norm_g0", KD), ("norm_g1", KD), ("norm_f", KD), ("b_ada", 6 * KD),
                  ("conv_w", 9 * KE), ("conv_b", KE), ("ln_w", KE), ("skip", KE),
                  ("gate_w", 3 * KE * 16)):
    VEC[_name] = (_at, _n)
    _at += _n
VECS = _at

VEC2 = {}
_at = 0
for _name, _n in (("ev_conv", 3 * KH), ("pool_s", KH), ("pool_w", KH * P),
                  ("dw_w", TAPS * KH), ("dw_b", KH), ("cn_g", KH), ("cn_b", KH), ("forget_w", KD * FH),
                  ("mix_g0", KD), ("mix_b0", KD), ("ffn_g0", KD), ("ffn_b0", KD),
                  ("mix_g1", KD), ("mix_b1", KD), ("ffn_g1", KD), ("ffn_b1", KD)):
    VEC2[_name] = (_at, _n)
    _at += _n
VECS2 = _at

CST = {}
_at = 0
for _name, _n in (("ident", P), ("mask_f", P), ("mask_b", P), ("count", 4 * 16), ("select", HEADS * P),
                  ("fold", 2), ("fold_gates", 16)):
    CST[_name] = (_at, _n)
    _at += _n
CSTS = _at


NORMS = {"rms1": (KD, False, True, False), "rmsf": (KD, False, True, True), "mix0": (KD, True, True, True),
         "ffn0": (KD, True, True, True), "conv": (KH, True, False, False), "mix1": (KD, True, True, True),
         "ffn1": (KD, True, False, True)}


def since(kind, name):
    total = 0
    for other, (n, centred, split, keep) in NORMS.items():
        if other == name:
            return total
        total += {"mean": centred, "centred": centred * n, "var": 1, "root": 1, "hi": split * n,
                  "split": split * n, "out": keep * n}.get(kind, n)


class Chain:

    def __init__(self, eng, sem):
        self.eng, self.sem, self.base, self.n = eng, sem, 0, 0

    def step(self, ins):
        ins.then_inc(self.sem, 1)
        self.n += 1

    def join(self, back=0):
        self.eng.wait_ge(self.sem, self.base + self.n - back)

    def enter(self, i, per):
        self.start, self.per = self.n, per
        self.base, self.n = i * per + self.start, 0

    def leave(self, rounds):
        assert self.n == self.per, (self.n, self.per)
        self.base, self.n = 0, self.start + rounds * self.per


def program(nc, w_in, x_in, ctx_in, vec_in, vec2_in, cst_in, dft_in, fsel_in, row_in, out):
    with ExitStack() as ctx:
        sems = {}

        def S(name):
            if name not in sems:
                sems[name] = ctx.enter_context(nc.semaphore(name))
            return sems[name]

        def tensors(stack):
            return lambda name, shape, dtype=F32: stack.enter_context(nc.sbuf_tensor(name, list(shape), dtype))

        sb = tensors(ctx)
        ring = sb("ring", (P, RING, SLOT))
        w_hi = sb("w_hi", (P, 2, SLOT), F32R)
        w_lo = sb("w_lo", (P, 2, SLOT), F32R)
        X = sb("X", (P, KD, SEQ))
        vec = sb("vec", (P, VECS))
        cst = sb("cst", (P, CSTS))
        rows = sb("rows", (FH, 8))
        ones_d = sb("ones_d", (P, P))
        ones_h = sb("ones_h", (P, P))
        ones = sb("ones", (P, P))
        modl = sb("modl", (P, 6 * KD, 2))
        scl = sb("scl", (P, 3 * KD))
        eps = sb("eps", (P, 2))
        rstd = sb("rstd", (P, TOK))
        warm = sb("warm", (P, 1))

        def one_place(name, shape, *others):
            out = []
            for n, (nm, sh, dt) in enumerate((*others, (name, shape, F32))):
                stack = first if n == len(others) else ExitStack()
                out.append(tensors(stack)(nm, sh, dt))
                if stack is not first:
                    stack.close()
            return out

        first = ExitStack()
        sa = tensors(first)
        hc, qk_hi, room = one_place("room", (P, KE, CTX), ("hc", (P, 2, KD, CTX), F32R),
                                    ("qk_hi", (P, 2 * HC, TOK), F32R))
        hl, wexp2 = one_place("wexp", (P, 2, 2, 4, SEQ), ("hl", (P, 2, KD, SEQ), F32R))
        xsplit, y_hi, o_sb = one_place("o_sb", (P, KE, SEQ), ("xsplit", (P, 2, HC, TOK), F32R),
                                       ("y_hi", (P, KE, SEQ), F32R))
        y_lo, qk_lo, z_sb = one_place("z_sb", (P, KE, SEQ), ("y_lo", (P, KE, SEQ), F32R),
                                      ("qk_lo", (P, 2 * HC, TOK), F32R))
        V = sa("V", (P, HC + KE, TOK))
        xconv = sa("xconv", (P, KE, TOK))
        ones_row = sa("ones_row", (HEADS, CTX))
        gate_parts = sa("gate_parts", (P, 2, 2 * HC, 32), F32R)
        gcol = sa("gcol", (P, 2, 4, HEADS))
        silc = sa("silc", (P, KD, 2))
        silc_parts = sa("silc_parts", (P, KD, 4), F32R)
        wexp = [wexp2[:, b] for b in range(2)]
        arow = V[0:4, KE:KE + 2, :]
        gates = V[0:32, KE + 2, :]
        em = [V[:, KE + 2 + n, :].rearrange("p (d j) -> p d j", d=2) for n in range(2)]

        scores = xconv[:, :, 0:CTX].rearrange("p (h t) j -> p h t j", h=HEADS)

        def work(n):
            return room[:, 4 * n:4 * n + 4, :]

        def grow(a, n=1, half=slice(0, 2)):
            v = room[0:HEADS, :, :].rearrange("p (r t) j -> p r t j", t=2)
            return v[:, a:a + n, half, :]

        first.close()

        second = ExitStack()
        sc = tensors(second)
        x_hi = sc("x_hi", (P, KD, SEQ), F32R)
        x_lo = sc("x_lo", (P, KD, SEQ), F32R)
        fourier = ExitStack()
        dft_room = tensors(fourier)("dft_parts", (P, 4 * (DFT_C + 3 * SEQ)), F32R)
        fourier.close()
        U_room = sc("U", (P, 4 * (DFT_C + 3 * SEQ)))
        dft_parts = [dft_room[:, :].rearrange("p (a k n) -> p a k n", a=2, k=2)[:, a] for a in range(2)]
        U = U_room[:, 0:KE * SEQ].rearrange("p (k j) -> p k j", j=SEQ)
        g_hi = sc("g_hi", (P, KF, SEQ), F32R)
        g_lo = sc("g_lo", (P, KF, SEQ), F32R)
        sq = sc("sq", (P, KD, SEQ))
        gate = sc("gate", (P, 2, SEQ))
        gated = sc("gated", (P, 4, SEQ))
        vec2 = sc("vec2", (P, VECS2))
        pad_a = sc("pad_a", (P, KH, 32 + SEQ))
        third = ExitStack()
        st = tensors(third)
        dft = st("dft", (P, 2, DFT_C + 3 * SEQ))
        pq = [st(f"pq_{part}", (P, 2, 2, DFT_C), F32R) for part in ("hi", "lo")]
        zf = st("zf", (P, KE, SEQ))
        third.close()
        third = ExitStack()
        st = tensors(third)
        pad_b = st("pad_b", (P, KH, 32 + SEQ))
        pad_c = st("pad_c", (P, KH, 32 + SEQ))
        pad_d = st("pad_d", (P, KH, 32 + SEQ))
        h2 = st("h2", (P, KH, SEQ))
        third.close()
        acc31 = sc("acc31", (P, KH, SEQ))
        logit = sc("logit", (P, FH, 2, SEQ))
        probT = sc("probT", (P, 2, 2, SEQ))
        vtok = sc("vtok", (P, 2, HALF))
        frow = sc("frow", (FH, 5, SEQ))
        fsel = sc("fsel", (FH, FH, P))
        stat = sc("stat", (P, 3, 2 * FH))
        second.close()

        ps = ctx.enter_context(nc.psum_tensor("ps", [P, 8, 512], F32))

        def vcol(name, k=0, n=1):
            if name in VEC:
                return vec[:, bass.ds(VEC[name][0] + k, n)]
            return vec2[:, bass.ds(VEC2[name][0] + k, n)]

        def cc(name, a=0, b=None):
            o, n = CST[name]
            return cst[:, o + a:o + (n if b is None else b)]

        ident = cc("ident")
        gate_w = vcol("gate_w", 0, 48 * 16).rearrange("p (c g) -> p c g", g=16)
        forget_w = vcol("forget_w", 0, KD * FH).rearrange("p (k f) -> p k f", f=FH)
        pool_w = vcol("pool_w", 0, KH * P).rearrange("p (g d) -> p g d", d=P)
        wide_tiles = [w[:, :, :].rearrange("p s (k n) -> p s k n", k=8) for w in (w_hi, w_lo)]
        head_tiles = [w[:, :, :].rearrange("p s (k n) -> p s k n", k=4) for w in (w_hi, w_lo)]
        deep_tiles = [w[:, :, :].rearrange("p s (k n) -> p s k n", k=2) for w in (w_hi, w_lo)]
        acc = ps[:, 4:8, :].rearrange("p b n -> p (b n)").rearrange("p (m t) -> p m t", t=SEQ)
        mean_ps = ps[:, 0, 0:SEQ]
        var_ps = ps[:, 1, 0:SEQ]

        def wide(a, n):
            return a.rearrange("p (o t) -> p o t", o=1).to_broadcast([P, n, a.shape[1]])

        loaded = [S(f"weights_loaded_{s}") for s in range(RING)]
        block = ctx.enter_context(nc.Block())

        @block.sync
        def _(sp):
            for s in range(RING):
                sp.dma_start(ring[:, s, :], w_in[s]).then_inc(loaded[s], 16)
            with sp.Fori(0, SLOTS // RING - 1) as i:
                for s in range(RING):
                    sp.wait_ge(S("lo_ready"), i * (2 * RING) + 2 * s + 2)
                    sp.dma_start(ring[:, s, :], w_in[i * RING + (RING + s)]).then_inc(loaded[s], 16)
            for s in range(SLOTS % RING):
                q = SLOTS - 1
                sp.wait_ge(S("lo_ready"), 2 * (q - RING) + 2)
                sp.dma_start(ring[:, q % RING, :], w_in[q]).then_inc(loaded[q % RING], 16)
            for half in range(2):
                k = slice(half * KD // 2, (half + 1) * KD // 2)
                sp.wait_ge(S("norm_out"), since("out", "ffn1") + (half + 1) * KD // 2)
                sp.dma_start(out[:, k], X[:, k, :]).then_inc(S("result_stored"), 16)
            sp.wait_ge(S("result_stored"), 32)

        @block.tensor
        def _(pe):
            mm = nc.tensor.matmul

            def slot(q0, body, t, u, i=0):
                for half in range(2):
                    pe.wait_ge(S("lo_ready"), i * (2 * UNROLL) + (2 * (q0 + u) + half + 1))
                    body(t, u % 4, (q0 + u) % 2, half)\
                        .then_inc(S("slot_done") if half else S("half_used"), 1)

            def walk(n, q0, body):
                for t in range(min(n, UNROLL)):
                    slot(q0, body, t, t)
                at = UNROLL
                if n // UNROLL > 2:
                    with pe.Fori(1, n // UNROLL) as i:
                        for u in range(UNROLL):
                            slot(q0, body, i * UNROLL + u, u, i)
                    at = n // UNROLL * UNROLL
                for t in range(at, n):
                    slot(q0, body, t, t)

            def triple(dst, w, x, start, stop):
                (w_h, w_l), (x_h, x_l) = w, x
                mm(dst, w_h, x_h, start=start, stop=False, skip_group_check=True)
                mm(dst, w_h, x_l, start=False, stop=False, skip_group_check=True)
                return mm(dst, w_l, x_h, start=False, stop=stop, skip_group_check=True)

            def project(n, name, x, moved, norm=None, before=0, last_slot=None):
                def body(t, u, s, half):
                    if half == 0 and (not isinstance(t, int) or t >= 4):
                        pe.wait_ge(moved, t + (before - 3))
                    if half == 0 and last_slot is not None and t == n - 1:
                        last_slot()
                    for k in range(4 * half, 4 * half + 4):
                        if norm is not None and isinstance(t, int) and t == 0:
                            pe.wait_ge(S("norm_split"), since("split", norm) + k + 1)
                        for b in range(2):
                            last = triple(ps[:, u, b * SEQ:(b + 1) * SEQ],
                                          [w[:, s, k, b * P:(b + 1) * P] for w in wide_tiles],
                                          [a[:, k, :] for a in x], k == 0 and b == 0, k == KD - 1)
                    return last
                walk(n, STARTS[name], body)

            def summing(x, wait, slots):
                def body(t, u, s, half):
                    wait(t * 2 + half, t)
                    for m in range(KD):
                        last = triple(acc[:, m, :], [w[:, s, half, m * P:(m + 1) * P] for w in deep_tiles],
                                      [a[:, t * 2 + half, :] for a in x],
                                      isinstance(t, int) and t == 0 and half == 0 and m % 2 == 0, half == 1)
                        if t == slots - 1 and half == 1 and m in (1, 3, 5):
                            last.then_inc(S("bank_summed"), 1)
                    return last
                return body

            def accumulate(n, name, x, wait):
                walk(n, STARTS[name], summing(x, wait, n))

            def column_sum(dst, weight, src, n, ready, done, before=0):
                for k in range(n):
                    if ready is not None:
                        pe.wait_ge(ready, before + k + 1)
                    last = mm(dst, weight, src(k), start=(k == 0), stop=(k == n - 1))
                last.then_inc(done, 1)

            pe.wait_ge(S("silc_split"), 1)

            def ada_rows(q, bank):
                def body(t, u, s, half):
                    for k in range(4 * half, 4 * half + 4):
                        for w in wide_tiles:
                            last = mm(ps[0:4, bank, u * SEQ:(u + 1) * SEQ], silc_parts[:, k, :], w[:, s, k, :],
                                      start=(k == 0 and w is wide_tiles[0]),
                                      stop=(k == KD - 1 and w is wide_tiles[1]), skip_group_check=True)
                    return last
                for u in range(2):
                    slot(q, body, u, u)

            def ada_turn(pair, bank, col):
                pe.wait_ge(S("ada_moved"), pair + 1)
                for b in range(4):
                    last = mm(ps[:, bank, col + 2 * b:col + 2 * b + 2], arow[:, pair % 2, b * P:(b + 1) * P],
                              cc("fold")[0:4], start=True, stop=True)
                last.then_inc(S("ada_turned"), 1)

            for pair in range(N_ADA0 // 2):
                if pair >= 2:
                    pe.wait_ge(S("ada_moved"), pair - 1)
                ada_rows(2 * pair, 2 + pair % 2)
                if pair == 0:
                    pe.wait_ge(S("ident_ready"), 16)
                else:
                    ada_turn(pair - 1, 4, 8 * (pair - 1))
                if pair == 1:
                    pe.wait_ge(S("ones_ready"), 3)
                    column_sum(ps[:, 6, :], ones_d[:, :], lambda k: V[:, k, :], KD, S("squares_0"),
                               S("meansq_0"))
            ada_turn(N_ADA0 // 2 - 1, 4, 8 * (N_ADA0 // 2 - 1))

            def xm_slot(t, u, i):
                for half in range(2):
                    pe.wait_ge(S("lo_ready"), i * 4 + (2 * (STARTS["xm"] + u) + half + 1))
                    for b in range(2):
                        bank = 2 * u + b
                        if half == 0 and (not isinstance(i, int) or i > 0):
                            pe.wait_ge(S("xm_moved"), i * 4 + bank - 3)
                        for k in range(4 * half, 4 * half + 4):
                            if isinstance(i, int) and i == 0 and u == 0 and b == 0:
                                pe.wait_ge(S("h_ready"), 2 * k + 2)
                            w = [a[:, u, k, b * P:(b + 1) * P] for a in wide_tiles]
                            triple(ps[:, bank, 0:CTX], w, [hc[:, a, k, :] for a in range(2)], k == 0, False)
                            last = triple(ps[:, bank, CTX:TOK], w, [hl[:, a, k, :] for a in range(2)], False,
                                          k == KD - 1)
                    last.then_inc(S("slot_done") if half else S("half_used"), 1)

            for u in range(2):
                xm_slot(u, u, 0)
            with pe.Fori(1, N_XM // 2) as i:
                for u in range(2):
                    xm_slot(i * 2 + u, u, i)

            for hd in range(HEADS):
                for part in range(2):
                    for half in range(2):
                        pe.wait_ge(S("lo_ready"), 2 * (STARTS["qk"] + 2 * hd + part) + half + 1)
                        for e in range(HC):
                            if half == 0 and part == 1:
                                pe.wait_ge(S("qk_split"), 2 * HC * hd + e + 1)
                            elif half == 0 and hd == 0:
                                pe.wait_ge(S("xm_moved"), KE - HC + e + 1)
                            elif half == 0:
                                pe.wait_ge(S("v_moved"), 4 * (hd - 1) + e + 1)
                            for k in range(2 * half, 2 * half + 2):
                                if part == 0 and e == 0:
                                    pe.wait_ge(S("xc_split"), HC * hd + k + 1)
                                last = triple(ps[:, e, :], [w[:, part, k, e * P:(e + 1) * P] for w in head_tiles],
                                              [xsplit[:, a, k, :] for a in range(2)], k == 0, k == HC - 1)
                            if half:
                                last.then_inc(S("qk_done") if e < HC - 1 else S("slot_done"), 1)
                        if not half:
                            last.then_inc(S("half_used"), 1)
                xm = [V[:, HC + HC * hd + e, :] for e in range(HC)]
                for t in range(4):
                    pe.wait_ge(S("qk_split"), 2 * HC * hd + HC + t + 1)
                    for e in range(HC):
                        last = nc.tensor.transpose(ps[:, t, e * P:(e + 1) * P], xm[e][:, t * P:(t + 1) * P], ident)
                    last.then_inc(S("v_turned"), 1)
                pe.wait_ge(S("gate_split"), hd + 1)
                for r in range(2 * HC):
                    for x in (qk_hi, qk_lo):
                        mm(ps[0:32, 7, :], gate_parts[:, hd % 2, r, :], x[:, r, :],
                           start=(hd == 0 and r == 0 and x is qk_hi), stop=False, skip_group_check=True)
                for e in range(HC):
                    last = mm(ps[0:16, 7, :], gate_w[:, 2 * KE + HC * hd + e, :], xm[e], start=False,
                              stop=(hd == HEADS - 1 and e == HC - 1), skip_group_check=True)
                last.then_inc(S("gates_done"), 1)
                if hd:
                    pe.wait_ge(S("scores_moved"), hd)
                else:
                    pe.wait_ge(S("mod0_ready"), 1)
                for t in range(4):
                    for e in range(HC):
                        last = triple(ps[:, 4 + t // 2, (t % 2) * SEQ:(t % 2 + 1) * SEQ],
                                      [a[:, HC + e, t * P:(t + 1) * P] for a in (qk_hi, qk_lo)],
                                      [a[:, e, CTX:TOK] for a in (qk_hi, qk_lo)],
                                      e == 0 and t % 2 == 0, e == HC - 1)
                last.then_inc(S("scores_done"), 1)

            pe.wait_ge(S("gates_moved"), 1)
            for g in range(4):
                if g == 2:
                    pe.wait_ge(S("scores_moved"), HEADS)
                last = mm(ps[0:4, (6, 7, 4, 5)[g], :], cc("fold_gates", 4 * g, 4 * g + 4)[0:32], gates, start=True, stop=True)
            last.then_inc(S("grow_done"), 1)

            pe.wait_ge(S("v_moved"), 4 * HEADS)
            project(N_OZ, "oz", [hl[:, a] for a in range(2)], S("oz_moved"))

            pe.wait_ge(S("g_ready"), 1)
            for d in range(2):
                for t in range(4):
                    last = nc.tensor.transpose(ps[:, 4, (d * 4 + t) * 4:(d * 4 + t) * 4 + 4],
                                               grow(d)[:, 0, t // 2, (t % 2) * P:(t % 2 + 1) * P],
                                               ident[0:HEADS, 0:HEADS])
            last.then_inc(S("gcol_done"), 1)
            pe.wait_ge(S("floor_ready"), 1)
            pe.wait_ge(S("oz_moved"), N_OZ)

            def spread(hd):
                if hd:
                    pe.wait_ge(S("diag_ready"), hd)
                    pe.wait_ge(S("wexp_ready"), hd)
                sel = cc("select", hd * P, (hd + 1) * P)[0:HEADS]
                mm(ps[:, 0, :], sel, grow(2)[:, 0], start=True, stop=True)
                mm(ps[:, 1, :], sel, grow(3)[:, 0], start=True, stop=True).then_inc(S("spread_done"), 1)

            def denominators(hd):
                pe.wait_ge(S("weighted_ready"), hd + 1)
                w = wexp[hd % 2]
                for t in range(4):
                    last = mm(ps[:, 2, :], ones[:, :], w[:, :, t, :], start=(t == 0), stop=(t == 3))
                last.then_inc(S("den_done"), 1)

            def mix_values(hd):
                pe.wait_ge(S("probs_ready"), hd + 1)
                if hd == 0:
                    pe.wait_ge(S("gcol_ready"), 1)
                if hd:
                    pe.wait_ge(S("heads_moved"), hd)
                for e in range(HC):
                    for t in range(4):
                        last = mm(ps[:, (4 if hd < HEADS - 1 else 0) + e // 2, (e % 2) * SEQ:(e % 2 + 1) * SEQ],
                                  V[:, HC * hd + t, e * P:(e + 1) * P], scores[:, hd, t, :],
                                  start=(t == 0), stop=(t == 3))
                last.then_inc(S("values_done"), 1)

            def out_slots(a, z):
                body = summing((y_hi, y_lo), lambda c, t: pe.wait_ge(S("y_ready"), c // HC + 1), N_MOUT)
                for t in range(a, z):
                    slot(STARTS["mout"], body, t, t)

            def head_mean(hd):
                pe.wait_ge(S("heads_moved"), hd + 1)
                if hd:
                    pe.wait_ge(S("head_root"), hd)
                column_sum(ps[:, 3, 0:SEQ], ones_h[:, :], lambda k: work(2 * (hd % 2))[:, k, :], HC, None,
                           S("head_mean"))

            def head_var(hd):
                pe.wait_ge(S("head_squares"), hd + 1)
                column_sum(ps[:, 3, SEQ:2 * SEQ], ones_h[:, :], lambda k: work(3)[:, k, :], HC, None,
                           S("head_var"))

            for n in range(HEADS):
                if n >= 1:
                    denominators(n - 1)
                spread(n)
                pair = N_ADA0 // 2 + 2 * n
                if n >= 1:
                    ada_turn(pair - 1, 7, 16 * n - 8)
                ada_rows(STARTS["ada1"] + 4 * n, 6)
                if n >= 2:
                    head_mean(n - 2)
                if n >= 1:
                    mix_values(n - 1)
                ada_turn(pair, 7, 16 * n)
                ada_rows(STARTS["ada1"] + 4 * n + 2, 6)
                if n >= 2:
                    head_var(n - 2)
            denominators(HEADS - 1)
            ada_turn(pair + 1, 7, 16 * HEADS - 8)
            head_mean(HEADS - 2)
            pe.wait_ge(S("mod1_ready"), 1)
            out_slots(0, 1)
            mix_values(HEADS - 1)
            head_var(HEADS - 2)
            out_slots(1, 2)
            head_mean(HEADS - 1)
            out_slots(2, 3)
            head_var(HEADS - 1)
            out_slots(3, N_MOUT)

            def norm(name, centred, n=KD, weight=ones_d, src=X, sqs=sq):
                if centred:
                    column_sum(mean_ps, weight[:, :], lambda k: src[:, k, :], n, S("norm_in"),
                               S("norm_mean"), since("in", name))
                column_sum(var_ps, weight[:, :], lambda k: sqs[:, k, :], n, S("norm_squares"),
                           S("norm_var"), since("squares", name))

            norm("rms1", False)
            project(N_FIN, "fin", (x_hi, x_lo), S("fin_moved"), "rms1")

            pe.wait_ge(S("fin_moved"), N_FIN)
            def channels(g):
                if g >= 2:
                    pe.wait_ge(S("pq_moved"), 2 * (g - 1))
                for n in range(2):
                    for k in range(2):
                        last = triple(ps[:, 2 * (g % 2) + n, 0:DFT_C],
                                      [a[:, 2 * g + k, n * P:(n + 1) * P] for a in (g_hi, g_lo)],
                                      [a[:, k, 0:DFT_C] for a in dft_parts], k == 0, k == 1)
                    last.then_inc(S("pq_done"), 1)

            def positions(g):
                pe.wait_ge(S("pq_moved"), 2 * (g + 1))
                if g >= 4:
                    pe.wait_ge(S("f_moved"), g - 3)
                for c in range(2):
                    for n in range(2):
                        for q, col in ((0, 0), (1, 2 * SEQ if c == 0 else SEQ)):
                            last = triple(ps[:, 4 + g % 4, c * SEQ:(c + 1) * SEQ],
                                          [a[:, g % 2, n, q * DFT_H + c:q * DFT_H + c + P] for a in pq],
                                          [a[:, n, DFT_C + col:DFT_C + col + SEQ] for a in dft_parts],
                                          c == 0 and n == 0 and q == 0, n == 1 and q == 1)
                last.then_inc(S("f_done"), 1)

            pe.wait_ge(S("dft_split"), 1)
            channels(0)
            for g in range(GROUPS):
                if g + 1 < GROUPS:
                    channels(g + 1)
                positions(g)
            pe.wait_ge(S("f_moved"), GROUPS)
            accumulate(N_FOUT, "fout", (g_hi, g_lo), lambda c, t: pe.wait_ge(S("fy_split"), c // 2 + 1))
            norm("rmsf", False)

            def pool_map():
                for g in range(KH):
                    pe.wait_ge(S("pooled_ready"), g + 1)
                    last = mm(ps[:, 4 + g // 2, (g % 2) * SEQ:(g % 2 + 1) * SEQ], pool_w[:, g, :], h2[:, g, :],
                              start=True, stop=True)
                last.then_inc(S("pool_done"), 1)

            project(N_EVIN, "evin", (x_hi, x_lo), S("evin_moved"), "rmsf", last_slot=pool_map)
            accumulate(N_EVOUT, "evout", (g_hi, g_lo), lambda c, t: pe.wait_ge(S("evmix_split"), max(c + 1, KH)))
            norm("mix0", True)

            def feed_forward(l):
                project(N_FFI, f"ffi{l}", (x_hi, x_lo), S("ffi_moved"), f"mix{l}", N_FFI * l)
                accumulate(N_FFO, f"ffo{l}", (g_hi, g_lo),
                           lambda c, t: pe.wait_ge(S("ffi_split"), N_FFI * l + c + 1))
                norm(f"ffn{l}", True)

            feed_forward(0)

            def forget():
                pe.wait_ge(S("norm_out"), since("out", "ffn0") + KD)
                for k in range(KD):
                    last = mm(ps[0:FH, 4, 0:SEQ], forget_w[:, k, :], X[:, k, :], start=(k == 0),
                              stop=(k == KD - 1))
                last.then_inc(S("forget_done"), 1)

            def odd_in(t, u, s, half):
                if half == 0 and t >= 4:
                    pe.wait_ge(S("odin_moved"), t - 3)
                if half == 0 and t == 3:
                    forget()
                for k in range(4 * half, 4 * half + 4):
                    if t == 0:
                        pe.wait_ge(S("norm_split"), since("split", "ffn0") + k + 1)
                    for b in range(2):
                        w = [a[:, s, k, b * P:(b + 1) * P] for a in wide_tiles]
                        x = [a[:, k, :] for a in (x_hi, x_lo)]
                        if t >= 8:
                            w, x = [a[:, k, b * P:(b + 1) * P] for a in (x_hi, x_lo)], \
                                [a[:, s, k, :] for a in wide_tiles]
                        last = triple(ps[:, u, b * SEQ:(b + 1) * SEQ], w, x, k == 0 and b == 0, k == KD - 1)
                return last

            walk(N_ODIN, STARTS["odin"], odd_in)
            pe.wait_ge(S("cum_ready"), 1)
            pe.wait_ge(S("fsel_ready"), 16)
            for hd in range(FH):
                pe.wait_ge(S("odin_moved"), 8 if hd < 2 else N_ODIN)
                if hd == 4:
                    column_sum(ps[:, 4, 0:SEQ], ones_h[:, :], lambda k: acc31[:, k, :], KH, S("norm_in"),
                               S("norm_mean"), since("in", "conv"))
                    column_sum(ps[:, 5, 0:SEQ], ones_h[:, :], lambda k: sq[:, k, :], KH, S("norm_squares"),
                               S("norm_var"), since("squares", "conv"))
                if hd >= 4:
                    pe.wait_ge(S("logits_moved"), hd - 3)
                lo = FD * (hd % 2)
                for t in range(2):
                    n = P * (t + 1)
                    mm(ps[:, (hd + 2) % 4, t * SEQ:t * SEQ + n], U[lo:lo + FD, hd // 2, t * P:(t + 1) * P],
                       U[lo:lo + FD, KH + hd // 2, 0:n], start=True, stop=False)
                    last = mm(ps[:, (hd + 2) % 4, t * SEQ:t * SEQ + n], fsel[:, hd, :],
                              frow[:, 3, 0:n], start=False, stop=True)
                last.then_inc(S("logits_done"), 1)

            def mixed(c, t):
                pe.wait_ge(S("conv_split"), min(c, KH - 1) + 1)
                if c >= KH:
                    pe.wait_ge(S("attn_split"), c - KH + 1)

            body = summing((g_hi, g_lo), mixed, N_ODOUT)
            for t in range(N_ODOUT // 2):
                slot(STARTS["odout"], body, t, t)
            def turn(hd):
                pe.wait_ge(S("prob_ready"), hd + 1)
                if hd >= 2:
                    pe.wait_ge(S("probT_moved"), hd - 1)
                b = hd % 2
                nc.tensor.transpose(ps[:, b, 0:P], logit[:, hd, 0, 0:P], ident)
                nc.tensor.transpose(ps[:, b, P:2 * P], logit[:, hd, 1, 0:P], ident)
                nc.tensor.transpose(ps[:, b, 3 * P:4 * P], logit[:, hd, 1, P:2 * P], ident)\
                    .then_inc(S("probT_done"), 1)

            pe.wait_ge(S("logits_moved"), FH)
            turn(0)
            for hd in range(FH):
                if hd + 1 < FH:
                    turn(hd + 1)
                pe.wait_ge(S("probT_moved"), hd + 1)
                b, lo, c = hd % 2, FD * (hd % 2), hd // 2
                if c >= 2 and hd % 2 == 0:
                    pe.wait_ge(S("attn_moved"), c - 1)
                mm(ps[lo:lo + FD, 2 + c % 2, 0:SEQ], vtok[:, 0, hd * FD:(hd + 1) * FD], probT[:, b, 0, :],
                   start=True, stop=False, skip_group_check=True)
                mm(ps[lo:lo + FD, 2 + c % 2, P:SEQ], vtok[:, 1, hd * FD:(hd + 1) * FD], probT[:, b, 1, P:SEQ],
                   start=False, stop=True, skip_group_check=True).then_inc(S("attn_done"), 1)
            for t in range(N_ODOUT // 2, N_ODOUT):
                slot(STARTS["odout"], body, t, t)
            norm("mix1", True)
            feed_forward(1)

        @block.scalar
        def _(act):
            do = nc.scalar.activation
            chain = Chain(act, S("act_order"))

            def hi(q, i=0, per=0):
                if isinstance(q, int) and q >= SLOTS:
                    return
                act.wait_ge(loaded[q % RING], i * (16 * per // RING) + (q // RING + 1) * 16)
                for half in range(2):
                    if q >= 2:
                        act.wait_ge(S("slot_done" if half else "half_used"), i * per + (q - 1))
                    part = slice(half * SLOT // 2, (half + 1) * SLOT // 2)
                    do(w_hi[:, q % 2, part], ring[:, q % RING, part], ACT.Copy).then_inc(S("hi_ready"), 1)

            def load_root():
                chain.join()
                chain.step(do(warm[:, :], eps[:, 0:1], ACT.Sqrt))

            def units(n, name, body=None):
                q0 = STARTS[name]

                def unit(t, u, i=0):
                    if body is None and isinstance(t, int) and t == n - 1:
                        load_root()
                    hi(q0 + u + 2, i, UNROLL)
                    if body is not None:
                        body(t, u % UNROLL)

                for t in range(min(n, UNROLL)):
                    unit(t, t)
                at = UNROLL
                if n // UNROLL > 2:
                    with act.Fori(1, n // UNROLL - 1) as i:
                        for u in range(UNROLL):
                            unit(i * UNROLL + u, u, i)
                    at = (n // UNROLL - 1) * UNROLL
                for t in range(at, n):
                    unit(t, t)

            act.dma_start(vec[:, :], vec_in).then_inc(S("vec_ready"), 16)
            act.dma_start(X[:, :, :], x_in).then_inc(S("x_ready"), 16)
            act.wait_ge(S("vec_ready"), 16)
            do(silc[:, :, :].rearrange("p k t -> p (k t)"), vcol("c", 0, 2 * KD), ACT.Silu)\
                .then_inc(S("silc_ready"), 1)
            act.wait_ge(S("silc_ready"), 1)
            do(silc_parts[:, :, 0:2], silc[:, :, :], ACT.Copy).then_inc(S("silc_rounded"), 1)
            hi(0)
            hi(1)
            act.wait_ge(S("x_ready"), 16)
            for k in range(KD):
                chain.step(do(V[:, k, CTX:TOK], X[:, k, :], ACT.Square))
            act.dma_start(xconv[:, 0:KD, 0:CTX], ctx_in).then_inc(S("ctx_ready"), 16)
            act.dma_start(cst[:, :], cst_in).then_inc(S("ident_ready"), 16)
            act.dma_start(rows[:, :], row_in).then_inc(S("rows_ready"), 16)
            hi(2)
            act.wait_ge(S("ctx_ready"), 16)
            for k in range(KD):
                do(V[:, k, 0:CTX], xconv[:, k, 0:CTX], ACT.Square).then_inc(S("squares_0"), 1)
            for q in range(3, N_ADA0 - 2):
                hi(q)
            act.wait_ge(S("meansq_0"), 1)
            do(rstd[:, :], ps[:, 6, :], ACT.Sqrt, bias=eps[:, 0:1]).then_inc(S("root_0"), 1)
            hi(N_ADA0 - 2)
            hi(N_ADA0 - 1)
            for k in range(KD):
                if k in (0, 3):
                    hi(STARTS["xm"] + k // 3)
                for t, col, dst in ((0, 1, hc), (1, 0, hl)):
                    act.wait_ge(S("scaled_0"), 2 * k + t + 1)
                    do(dst[:, 0, k, :], V[:, k, t * CTX:t * CTX + SEQ], ACT.Identity,
                       bias=modl[:, k, col:col + 1]).then_inc(S("h_rounded"), 1)

            def move_xm(i, u):
                act.wait_ge(S("slot_done"), i * 2 + (STARTS["xm"] + u + 1))
                for b in range(2):
                    do(V[:, i * 4 + (HC + 2 * u + b), :], ps[:, 2 * u + b, :], ACT.Copy)\
                        .then_inc(S("xm_moved"), 1)

            def silu(i, u):
                for b in range(2):
                    act.wait_ge(S("conv_done"), i * 4 + (2 * u + b + 1))
                    a = xconv[:, i * 4 + (2 * u + b), :]
                    do(a, a, ACT.Silu).then_inc(S("xconv_ready"), 1)

            for u in range(2):
                hi(STARTS["xm"] + 2 + u)
                move_xm(0, u)
            with act.Fori(1, N_XM // 2 - 1) as i:
                for u in range(2):
                    hi(STARTS["xm"] + 2 + u, i, 2)
                    move_xm(i, u)
                    silu(i - 1, u)

            def round_head(hd):
                if hd:
                    act.wait_ge(S("slot_done"), STARTS["qk"] + 2 * hd)
                for k in range(HC):
                    act.wait_ge(S("xconv_ready"), HC * hd + k + 1)
                    do(xsplit[:, 0, k, :], xconv[:, HC * hd + k, :], ACT.Copy).then_inc(S("xc_rounded"), 1)

            round_head(0)
            for u in range(2):
                hi(STARTS["qk"] + u)
                move_xm(N_XM // 2 - 1, u)
                silu(N_XM // 2 - 2, u)
            for u in range(2):
                silu(N_XM // 2 - 1, u)

            def gate_w_of(hd):
                return gate_w[:, 0:2 * KE, :].rearrange("p (a h e) g -> p h a e g", a=2, h=HEADS)[:, hd]

            def round_gate_weights(hd):
                if hd >= 2:
                    act.wait_ge(S("gates_done"), hd - 1)
                do(gate_parts[:, hd % 2, :, 0:16].rearrange("p (a e) g -> p a e g", a=2), gate_w_of(hd), ACT.Copy)\
                    .then_inc(S("gate_rounded"), 1)

            for hd in range(HEADS):
                for r in range(12):
                    if r < 8:
                        if r % 4 < 3:
                            act.wait_ge(S("qk_done"), 6 * hd + 3 * (r // 4) + r % 4 + 1)
                        else:
                            act.wait_ge(S("slot_done"), STARTS["qk"] + 2 * hd + r // 4 + 1)
                        if r == 0 and hd:
                            act.wait_ge(S("scores_done"), hd)
                        do(qk_hi[:, r, :], ps[:, r % 4, :], ACT.Copy, scale=1.0 if r < 4 else DH ** -0.5)\
                            .then_inc(S("qk_rounded"), 1)
                        if r == 3:
                            round_gate_weights(hd)
                        if r % 4 == 3:
                            hi(STARTS["qk"] + 2 * hd + r // 4 + 2)
                    else:
                        act.wait_ge(S("v_turned"), 4 * hd + r - 7)
                        if r == 8 and hd:
                            act.wait_ge(S("gates_done"), hd)
                        do(V[:, HC * hd + r - 8, :], ps[:, r % 4, :], ACT.Copy).then_inc(S("v_moved"), 1)
                if hd < HEADS - 1:
                    round_head(hd + 1)

            def softplus_of_minus(x, t, ready, done):
                act.wait_ge(ready, 1)
                chain.step(do(t, x, ACT.Abs))
                chain.join()
                chain.step(do(t, t, ACT.Exp, scale=-1.0))
                chain.join()
                do(t, t, ACT.Ln, bias=1.0).then_inc(done, 1)

            rows2 = lambda a: grow(a, 2).rearrange("p r t j -> p (r t) j")
            softplus_of_minus(rows2(2), rows2(4), S("grow_moved"), S("grow_log"))
            def move_oz(t, u):
                if t == 8:
                    act.wait_ge(S("scores_done"), HEADS)
                act.wait_ge(S("slot_done"), STARTS["oz"] + t + 1)
                dst = (o_sb if t < 8 else z_sb)[:, 2 * (t % 8):2 * (t % 8) + 2, :]
                do(dst, ps[:, u, :].rearrange("p (b j) -> p b j", b=2), ACT.Sigmoid if t < 8 else ACT.Silu)\
                    .then_inc(S("oz_moved"), 1)

            for t in range(N_OZ):
                hi(STARTS["oz"] + t + 2)
                move_oz(t, t % 4)
                if t == N_OZ // 2:
                    act.wait_ge(S("m_ready"), 1)
                    do(grow(3)[:, 0], grow(3)[:, 0], ACT.Exp, scale=-1.0).then_inc(S("floor_ready"), 1)

            def weigh(hd):
                w = wexp[hd % 2]
                act.wait_ge(S("spread_done"), hd + 1)
                if hd >= 2:
                    act.wait_ge(S("probs_ready"), hd - 1)
                else:
                    act.wait_ge(S("gcol_ready"), 1)
                    act.wait_ge(S("wexp_clear"), 4)
                chain.step(do(em[hd % 2], ps[:, 1, :].rearrange("p (d j) -> p d j", d=2), ACT.Copy))
                act.wait_ge(S("diag_ready"), hd + 1)
                for d, t, lo, hi in ((0, 0, 0, SEQ), (0, 1, 0, SEQ), (0, 2, P, SEQ),
                                     (1, 0, 0, SEQ), (1, 1, 0, SEQ), (1, 3, 0, P)):
                    chain.step(do(w[:, d, t, lo:hi], ps[:, 0, d * SEQ + lo:d * SEQ + hi], ACT.Exp,
                                  bias=gcol[:, d, t, hd:hd + 1]))
                for n, (d, t, lo) in enumerate(((0, 2, 0), (0, 3, P), (1, 2, 0), (1, 3, P))):
                    last = do(w[:, d, t, lo:lo + P], w[:, d, t, lo:lo + P], ACT.Exp)
                    if n < 3:
                        chain.step(last)
                last.then_inc(S("wexp_ready"), 1)

            def move_rows(pair):
                act.wait_ge(S("slot_done"), STARTS["ada1"] + 2 * pair + 2 - N_ADA0)
                act.wait_ge(S("ada_turned"), pair - 1)
                do(arow[:, pair % 2, :], ps[0:4, 6, :], ACT.Copy).then_inc(S("ada_moved"), 1)

            def move_values(hd):
                act.wait_ge(S("values_done"), hd + 1)
                if hd >= 2:
                    act.wait_ge(S("y_ready"), hd - 1)
                at = 4 if hd < HEADS - 1 else 0
                do(work(2 * (hd % 2)), ps[:, at:at + 2, :].rearrange("p b (c j) -> p (b c) j", c=2), ACT.Copy)\
                    .then_inc(S("heads_moved"), 1)

            def squares(hd):
                act.wait_ge(S("head_centred"), hd + 1)
                if hd:
                    act.wait_ge(S("head_var"), hd)
                do(work(3), work(2 * (hd % 2)), ACT.Square).then_inc(S("head_squares"), 1)

            def root(hd):
                act.wait_ge(S("head_var"), hd + 1)
                if hd:
                    act.wait_ge(S("y_rounded"), hd)
                do(rstd[:, 0:SEQ], ps[:, 3, SEQ:2 * SEQ], ACT.Sqrt, bias=eps[:, 0:1])\
                    .then_inc(S("head_root"), 1)

            for n in range(HEADS):
                hi(STARTS["ada1"] + 4 * n + 2)
                hi(STARTS["ada1"] + 4 * n + 3)
                move_rows(N_ADA0 // 2 + 2 * n)
                weigh(n)
                if n >= 2:
                    squares(n - 2)
                if n >= 1:
                    move_values(n - 1)
                if n >= 2:
                    root(n - 2)
                hi(STARTS["ada1"] + 4 * n + 4)
                hi(STARTS["ada1"] + 4 * n + 5)
                move_rows(N_ADA0 // 2 + 2 * n + 1)
            squares(HEADS - 2)
            hi(STARTS["mout"] + 2)
            move_values(HEADS - 1)
            root(HEADS - 2)
            hi(STARTS["mout"] + 3)
            squares(HEADS - 1)
            hi(STARTS["mout"] + 4)
            root(HEADS - 1)
            hi(STARTS["mout"] + 5)
            for t in range(6, N_MOUT + 2):
                if t == N_MOUT + 1:
                    load_root()
                hi(STARTS["mout"] + t)

            def norm(name, bias, n=KD, src=X, centred=True, split=True, keep=True):
                for k in range(n):
                    kind = "centred" if centred else "in"
                    act.wait_ge(S(f"norm_{kind}"), since(kind, name) + k + 1)
                    do(sq[:, k, :], src[:, k, :], ACT.Square).then_inc(S("norm_squares"), 1)
                act.wait_ge(S("norm_var"), since("var", name) + 1)
                e = 1 if centred else 0
                do(rstd[:, 0:SEQ], var_ps, ACT.Sqrt, bias=eps[:, e:e + 1]).then_inc(S("norm_root"), 1)
                def shift(dst, k, done):
                    act.wait_ge(S("norm_scaled"), since("scaled", name) + k + 1)
                    if bias is None:
                        do(dst[:, k, :], sq[:, k, :], ACT.Copy).then_inc(done, 1)
                    else:
                        do(dst[:, k, :], sq[:, k, :], ACT.Identity, bias=bias(k)).then_inc(done, 1)

                if split:
                    for k in range(n):
                        shift(x_hi, k, S("norm_hi"))
                if keep:
                    for k in range(n):
                        shift(X, k, S("norm_out"))

            act.wait_ge(S("y_ready"), HEADS)
            act.dma_start(dft[:, :, :], dft_in).then_inc(S("dft_ready"), 16)
            act.dma_start(vec2[:, :], vec2_in).then_inc(S("vec2_ready"), 16)
            norm("rms1", lambda k: modl[:, 3 * KD + k, 0:1], centred=False, keep=False)

            def move_fin(t, u):
                act.wait_ge(S("slot_done"), STARTS["fin"] + t + 1)
                if t < 8:
                    dst, func = g_hi[:, 2 * t:2 * t + 2, :], ACT.Copy
                else:
                    dst, func = zf[:, 2 * (t - 8):2 * (t - 8) + 2, :], ACT.Silu
                if t == 8:
                    act.wait_ge(S("fin_moved"), 8)
                do(dst, ps[:, u, :].rearrange("p (b j) -> p b j", b=2), func)\
                    .then_inc(S("u_rounded") if t < 8 else S("fin_moved"), 1)

            for t in range(N_FIN):
                hi(STARTS["fin"] + t + 2)
                move_fin(t, t % 4)
                if t == 9:
                    act.wait_ge(S("dft_ready"), 16)
                    do(dft_parts[0], dft[:, :, :], ACT.Copy).then_inc(S("dft_rounded"), 1)
            for g in range(GROUPS):
                if g >= 2:
                    act.wait_ge(S("f_done"), g - 1)
                for n in range(2):
                    act.wait_ge(S("pq_done"), 2 * g + n + 1)
                    do(pq[0][:, g % 2, n, :], ps[:, 2 * (g % 2) + n, 0:DFT_C], ACT.Copy).then_inc(S("pq_rounded"), 1)
            units(N_FOUT, "fout")
            norm("rmsf", None, centred=False)

            act.wait_ge(S("pads_clear"), 4)
            def move_evin(t, u):
                act.wait_ge(S("slot_done"), STARTS["evin"] + t + 1)
                if t < 2:
                    dst = pad_a[:, 2 * t:2 * t + 2, 32:]
                else:
                    dst = U[:, 2 * (t - 2):2 * (t - 2) + 2, :]
                do(dst, ps[:, u, :].rearrange("p (b j) -> p b j", b=2), ACT.Copy)\
                    .then_inc(S("evin_moved"), 1)

            units(N_EVIN, "evin", move_evin)
            units(N_EVOUT, "evout")
            norm("mix0", lambda k: vcol("mix_b0", k))
            act.dma_start(fsel[:, :, :], fsel_in).then_inc(S("fsel_ready"), 16)

            def feed_forward(l):
                def gating(t, u):
                    act.wait_ge(S("slot_done"), t + (STARTS[f"ffi{l}"] + 1))
                    if not isinstance(t, int) or t >= 2:
                        act.wait_ge(S("ffi_moved"), t + (N_FFI * l - 1))
                    do(gate[:, u % 2, :], ps[:, u, 0:SEQ], ACT.Silu).then_inc(S("gate_ready"), 1)
                units(N_FFI, f"ffi{l}", gating)
                units(N_FFO, f"ffo{l}")
                norm(f"ffn{l}", lambda k: vcol(f"ffn_b{l}", k), split=l == 0)

            feed_forward(0)

            def move_odin(t, u):
                act.wait_ge(S("slot_done"), STARTS["odin"] + t + 1)
                if t < 4:
                    if t >= 2:
                        act.wait_ge(S("odin_moved"), t - 1)
                    do(gate[:, t % 2, :], ps[:, t, SEQ:2 * SEQ], ACT.Sigmoid).then_inc(S("glu_ready"), 1)
                    return
                if t == 4:
                    act.wait_ge(S("odin_moved"), 4)
                if t < 8:
                    dst = U[:, 2 * (t - 4):2 * (t - 4) + 2, :]
                else:
                    dst = vtok[:, :, (t - 8) * SEQ:(t - 7) * SEQ]
                do(dst, ps[:, u, :].rearrange("p (b j) -> p b j", b=2), ACT.Copy)\
                    .then_inc(S("odin_moved"), 1)

            for t in range(N_ODIN):
                hi(STARTS["odin"] + t + 2)
                move_odin(t, t % 4)
                if t == 4:
                    softplus_of_minus(frow[:, 0, :], frow[:, 1, :], S("forget_moved"), S("forget_log"))
            for k in range(KH):
                act.wait_ge(S("norm_centred"), since("centred", "conv") + k + 1)
                do(sq[:, k, :], acc31[:, k, :], ACT.Square).then_inc(S("norm_squares"), 1)
            act.wait_ge(S("norm_var"), since("var", "conv") + 1)
            do(rstd[:, 0:SEQ], ps[:, 5, 0:SEQ], ACT.Sqrt, bias=eps[:, 1:2]).then_inc(S("norm_root"), 1)
            for hd in range(FH):
                act.wait_ge(S("max_ready"), hd + 1)
                for t in range(2):
                    a = logit[:, hd, t, :]
                    last = do(a, a, ACT.Exp, scale=FD ** -0.5, bias=stat[:, 1, 2 * hd + t:2 * hd + t + 1],
                              accum_out=stat[:, 2, 2 * hd + t:2 * hd + t + 1])
                    if t == 0:
                        chain.step(last)
                last.then_inc(S("exp_ready"), 1)
                if hd == 1:
                    for k in range(KH):
                        act.wait_ge(S("norm_scaled"), since("scaled", "conv") + k + 1)
                        do(g_hi[:, k, :], acc31[:, k, :], ACT.Silu, bias=vcol("cn_b", k))\
                            .then_inc(S("conv_hi"), 1)
                        do(sq[:, k, :], acc31[:, k, :], ACT.Silu, bias=vcol("cn_b", k))\
                            .then_inc(S("conv_whole"), 1)
            hi(STARTS["odout"] + 2)
            hi(STARTS["odout"] + 3)
            for hd in range(FH):
                act.wait_ge(S("probT_done"), hd + 1)
                if hd >= 2:
                    act.wait_ge(S("attn_done"), hd - 1)
                chain.step(do(probT[:, hd % 2, 0, :], ps[:, hd % 2, 0:SEQ], ACT.Copy))
                do(probT[:, hd % 2, 1, P:SEQ], ps[:, hd % 2, 3 * P:4 * P], ACT.Copy)\
                    .then_inc(S("probT_moved"), 1)
            hi(STARTS["odout"] + 4)
            load_root()
            hi(STARTS["odout"] + 5)
            norm("mix1", lambda k: vcol("mix_b1", k))
            feed_forward(1)

        @block.gpsimd
        def _(pool):
            pair_op = nc.gpsimd.tensor_tensor
            def lo(q):
                for half in range(2):
                    pool.wait_ge(S("hi_ready"), 2 * q + half + 1)
                    part = slice(half * SLOT // 2, (half + 1) * SLOT // 2)
                    pair_op(w_lo[:, q % 2, part], ring[:, q % RING, part], w_hi[:, q % 2, part],
                        ALU.subtract).then_inc(S("lo_ready"), 1)

            pool.wait_ge(S("lo_ready"), 2 * STARTS["xm"])
            for q in range(STARTS["xm"], STARTS["qk"] + 2):
                lo(q)
            pool.wait_ge(S("slot_done"), STARTS["oz"])
            pool.wait_ge(S("vec_ready"), 16)
            for c in range(KE):
                a = xconv[:, c, CTX:TOK]
                nc.gpsimd.tensor_scalar(a, a, vcol("skip", c), None, ALU.mult).then_inc(S("skip_ready"), 1)
            for t in range(N_OZ // 2):
                pool.wait_ge(S("oz_moved"), t + 1)
                for c in (2 * t, 2 * t + 1):
                    nc.gpsimd.tensor_scalar(o_sb[:, c, :], o_sb[:, c, :], vcol("ln_w", c), None, ALU.mult)\
                        .then_inc(S("o_scaled"), 1)
            for t in range(N_OZ // 2):
                pool.wait_ge(S("oz_moved"), N_OZ // 2 + t + 1)
                pool.wait_ge(S("o_scaled"), 2 * t + 2)
                pool.wait_ge(S("skip_ready"), 2 * t + 2)
                c = slice(2 * t, 2 * t + 2)
                for a in (o_sb[:, c, :], xconv[:, c, CTX:TOK]):
                    pair_op(a, a, z_sb[:, c, :], ALU.mult).then_inc(S("z_applied"), 1)
            pool.wait_ge(S("slot_done"), STARTS["ada1"])
            for b in range(2):
                for d, t, j in ((0, 3, 0), (1, 2, P)):
                    nc.gpsimd.memset(wexp[b][:, d, t, j:j + P], 0.0).then_inc(S("wexp_clear"), 1)
            def rest_of_y(hd):
                pool.wait_ge(S("y_rounded"), hd + 1)
                c = slice(HC * hd, HC * hd + HC)
                pair_op(y_lo[:, c, :], work(2 * (hd % 2)), y_hi[:, c, :], ALU.subtract).then_inc(S("y_ready"), 1)

            pool.wait_ge(S("lo_ready"), 2 * (STARTS["ada1"] + 2))
            for n in range(HEADS):
                for t in range(4 * n + 2, 4 * n + 6):
                    lo(STARTS["ada1"] + t)
                if n >= 2:
                    rest_of_y(n - 2)
            for hd in range(2, HEADS):
                rest_of_y(hd)
            for g in range(GROUPS):
                pool.wait_ge(S("fy_rounded"), g + 1)
                c = slice(2 * g, 2 * g + 2)
                pair_op(g_lo[:, c, :], zf[:, c, :], g_hi[:, c, :], ALU.subtract).then_inc(S("fy_split"), 1)
            pool.wait_ge(S("norm_in"), since("in", "rmsf") + KD)
            for a in (pad_a, pad_b, pad_c, pad_d):
                nc.gpsimd.memset(a[:, :, 0:32], 0.0).then_inc(S("pads_clear"), 1)
            for c in range(2 * KH):
                pool.wait_ge(S("evmix_rounded"), c + 1)
                src = U[:, 3 * KH + c if c < KH else c - KH, :]
                pair_op(g_lo[:, c, :], src, g_hi[:, c, :], ALU.subtract).then_inc(S("evmix_split"), 1)

            def feed_forward(l):
                def rest(t, u):
                    pool.wait_ge(S("ffi_rounded"), t + (N_FFI * l + 1))
                    pair_op(g_lo[:, t, :], gated[:, u, :], g_hi[:, t, :], ALU.subtract).then_inc(S("ffi_split"), 1)
                for t in range(4):
                    rest(t, t)
                with pool.Fori(1, N_FFI // 4) as i:
                    for u in range(4):
                        rest(i * 4 + u, u)
                for t in range(N_FFI // 4 * 4, N_FFI):
                    rest(t, t % 4)

            pool.wait_ge(S("norm_in"), since("in", "mix0") + KD)
            nc.gpsimd.memset(logit[:, :, 0, P:SEQ], NEG).then_inc(S("logit_clear"), 1)
            feed_forward(0)
            pool.wait_ge(S("lo_ready"), 2 * (STARTS["odin"] + 2))
            for q in range(STARTS["odin"] + 2, STARTS["odout"] + 2):
                lo(q)
            for c in range(KH):
                pool.wait_ge(S("attn_rounded"), c + 1)
                pair_op(g_lo[:, KH + c, :], gated[:, c, :], g_hi[:, KH + c, :], ALU.subtract)\
                    .then_inc(S("attn_split"), 1)
            feed_forward(1)

        @block.vector
        def _(dve):
            v = nc.vector
            chain = Chain(dve, S("dve_order"))

            def lo(q, i=0, per=0, halves=(0, 1)):
                if isinstance(q, int) and q >= SLOTS:
                    return
                for half in halves:
                    dve.wait_ge(S("hi_ready"), i * (2 * per) + (2 * q + half + 1))
                    part = slice(half * SLOT // 2, (half + 1) * SLOT // 2)
                    v.tensor_tensor(w_lo[:, q % 2, part], ring[:, q % RING, part], w_hi[:, q % 2, part],
                                    ALU.subtract).then_inc(S("lo_ready"), 1)

            def units(n, name, body=None):
                q0 = STARTS[name]
                for t in range(min(n, UNROLL)):
                    lo(q0 + t + 2, halves=() if body is None and t == n - 1 else (0, 1))
                    if body is not None:
                        body(t, t)
                at = UNROLL
                if n // UNROLL > 2:
                    with dve.Fori(1, n // UNROLL - 1) as i:
                        for u in range(UNROLL):
                            lo(q0 + u + 2, i, UNROLL)
                            if body is not None:
                                body(i * UNROLL + u, u)
                    at = (n // UNROLL - 1) * UNROLL
                for t in range(at, n):
                    lo(q0 + t + 2, halves=() if body is None and t == n - 1 else (0, 1))
                    if body is not None:
                        body(t, t % 4)

            chain.step(v.memset(eps[:, 0:1], RMS_EPS))
            chain.step(v.memset(eps[:, 1:2], LN_EPS))
            v.memset(ones_d[:, :], 1.0 / D).then_inc(S("ones_ready"), 1)
            v.memset(ones_h[:, :], 1.0 / HALF).then_inc(S("ones_ready"), 1)
            v.memset(ones[:, :], 1.0).then_inc(S("ones_ready"), 1)
            chain.step(v.memset(ones_row[:, :], 1.0))
            dve.wait_ge(S("silc_rounded"), 1)
            v.tensor_tensor(silc_parts[:, :, 2:4], silc[:, :, :], silc_parts[:, :, 0:2], ALU.subtract)\
                .then_inc(S("silc_split"), 1)
            lo(0)
            lo(1)
            for pair in range(N_ADA0 // 2):
                if pair == 2:
                    dve.wait_ge(S("root_0"), 1)
                    chain.step(v.reciprocal(rstd[:, :], rstd[:, :]))
                for q in (2 * pair + 2, 2 * pair + 3):
                    if q < N_ADA0:
                        lo(q)
                dve.wait_ge(S("slot_done"), 2 * pair + 2)
                if pair >= 2:
                    dve.wait_ge(S("ada_turned"), pair - 1)
                v.tensor_copy(arow[:, pair % 2, :], ps[0:4, 2 + pair % 2, :]).then_inc(S("ada_moved"), 1)
            b_ada = vcol("b_ada", 0, 6 * KD).rearrange("p (m o) -> p m o", o=1).to_broadcast([P, 6 * KD, 2])
            dve.wait_ge(S("vec_ready"), 16)
            dve.wait_ge(S("ada_turned"), N_ADA0 // 2)
            chain.step(v.tensor_tensor(modl[:, 0:2 * KD, :],
                                       ps[:, 4, 0:4 * KD].rearrange("p (m t) -> p m t", t=2),
                                       b_ada[:, 0:2 * KD, :], ALU.add))
            chain.join()
            chain.step(v.scalar_tensor_tensor(scl[:, 0:KD], modl[:, KD:2 * KD, 1], 1.0, vcol("norm_g0", 0, KD),
                                              ALU.add, ALU.mult))
            v.scalar_tensor_tensor(scl[:, KD:2 * KD], modl[:, KD:2 * KD, 0], 1.0, vcol("norm_g0", 0, KD),
                                   ALU.add, ALU.mult).then_inc(S("mod0_ready"), 1)
            chain.join()
            dve.wait_ge(S("mod0_ready"), 1)
            dve.wait_ge(S("x_ready"), 16)
            dve.wait_ge(S("ctx_ready"), 16)
            def rest_of_h(k):
                for t, col, dst in ((0, 1, hc), (1, 0, hl)):
                    dve.wait_ge(S("h_rounded"), 2 * k + t + 1)
                    v.scalar_tensor_tensor(dst[:, 1, k, :], V[:, k, t * CTX:t * CTX + SEQ],
                                           modl[:, k, col:col + 1], dst[:, 0, k, :], ALU.add, ALU.subtract)\
                        .then_inc(S("h_ready"), 1)

            for k in range(KD):
                v.scalar_tensor_tensor(V[:, k, 0:CTX], xconv[:, k, 0:CTX], scl[:, k:k + 1], rstd[:, 0:CTX],
                                       ALU.mult, ALU.mult).then_inc(S("scaled_0"), 1)
                v.scalar_tensor_tensor(V[:, k, CTX:TOK], X[:, k, :], scl[:, KD + k:KD + k + 1],
                                       rstd[:, CTX:TOK], ALU.mult, ALU.mult).then_inc(S("scaled_0"), 1)
                if k:
                    rest_of_h(k - 1)
            rest_of_h(KD - 1)

            def convolve(c):
                tap = lambda b, n: vcol("conv_w", (c + b) * 9 + n)
                src = [V[:, c + (HC + b), :] for b in range(2)]
                dst = [xconv[:, c + b, :] for b in range(2)]
                grid_in, grid_out = [[a[:, CTX:TOK].rearrange("p (y x) -> p y x", x=GRID) for a in s]
                                     for s in (src, dst)]
                for b in range(2):
                    dve.wait_ge(S("xm_moved"), c + (b + 1))
                    chain.step(v.tensor_scalar(dst[b], src[b], tap(b, 4), vcol("conv_b", c + b), ALU.mult, ALU.add))
                for n in (1, 7, 3, 5, 0, 2, 6, 8):
                    dy, dx = n // 3 - 1, n % 3 - 1
                    y0, y1, x0, x1 = max(0, -dy), ROWS - max(0, dy), max(0, -dx), GRID - max(0, dx)
                    for b in range(2):
                        o = grid_out[b][:, y0:y1, x0:x1]
                        chain.join(1)
                        chain.step(v.scalar_tensor_tensor(o, grid_in[b][:, y0 + dy:y1 + dy, x0 + dx:x1 + dx],
                                                          tap(b, n), o, ALU.mult, ALU.add))
                        if n == 3:
                            o = dst[b][:, 1:CTX]
                            chain.step(v.scalar_tensor_tensor(o, src[b][:, 0:CTX - 1], tap(b, 3), o,
                                                              ALU.mult, ALU.add))
                chain.join()
                for b in range(2):
                    o = dst[b][:, 0:CTX - 1]
                    v.scalar_tensor_tensor(o, src[b][:, 1:CTX], tap(b, 5), o, ALU.mult, ALU.add)\
                        .then_inc(S("conv_done"), 1)

            def split_head(hd):
                for k in range(HC):
                    dve.wait_ge(S("xc_rounded"), HC * hd + k + 1)
                    v.tensor_tensor(xsplit[:, 1, k, :], xconv[:, HC * hd + k, :], xsplit[:, 0, k, :],
                                    ALU.subtract).then_inc(S("xc_split"), 1)

            for u in range(2):
                convolve(2 * u)
            with dve.Fori(1, N_XM // 2 - 1) as i:
                chain.enter(i - 1, 40)
                for u in range(2):
                    convolve(i * 4 + 2 * u)
            chain.leave(N_XM // 2 - 2)
            split_head(0)
            for c in range(KE - 4, KE, 2):
                convolve(c)
            dve.wait_ge(S("lo_ready"), 2 * (STARTS["qk"] + 2))

            for hd in range(HEADS):
                for r in range(2 * HC):
                    dve.wait_ge(S("qk_rounded"), 2 * HC * hd + r + 1)
                    v.scalar_tensor_tensor(qk_lo[:, r, :], ps[:, r % 4, :], 1.0 if r < 4 else DH ** -0.5,
                                           qk_hi[:, r, :], ALU.mult, ALU.subtract).then_inc(S("qk_split"), 1)
                    if r == 3:
                        dve.wait_ge(S("gate_rounded"), hd + 1)
                        parts = gate_parts[:, hd % 2].rearrange("p (a e) g -> p a e g", a=2)
                        v.tensor_tensor(parts[:, :, :, 16:32],
                                        gate_w[:, 0:2 * KE, :].rearrange("p (a h e) g -> p h a e g", a=2,
                                                                         h=HEADS)[:, hd],
                                        parts[:, :, :, 0:16], ALU.subtract).then_inc(S("gate_split"), 1)
                    if r % 4 == 3:
                        lo(STARTS["qk"] + 2 * hd + r // 4 + 2)
                if hd < HEADS - 1:
                    split_head(hd + 1)
                else:
                    dve.wait_ge(S("gates_done"), HEADS)
                    v.tensor_copy(gates, ps[0:32, 7, :]).then_inc(S("gates_moved"), 1)
                dve.wait_ge(S("scores_done"), hd + 1)
                v.tensor_copy(scores[:, hd, :, :],
                              ps[:, 4:6, :].rearrange("p b (t j) -> p (b t) j", t=2)).then_inc(S("scores_moved"), 1)

            dve.wait_ge(S("grow_done"), 1)
            dve.wait_ge(S("rows_ready"), 16)
            for g, a in ((0, 0), (2, 1), (1, 2), (3, 3)):
                ins = v.tensor_scalar(grow(a)[:, 0], ps[0:HEADS, (6, 7, 4, 5)[g], :].rearrange("p (t j) -> p t j", t=2),
                                      rows[0:HEADS, g:g + 1], None, ALU.add)
                if a < 3:
                    chain.step(ins)
            ins.then_inc(S("grow_moved"), 1)
            rows2 = lambda a: grow(a, 2).rearrange("p r t j -> p (r t) j")
            dve.wait_ge(S("grow_log"), 1)
            chain.step(v.scalar_tensor_tensor(rows2(2), rows2(2), 0.0, rows2(4), ALU.min, ALU.subtract))
            chain.join()

            def scan(dst, src, first, op0, op1, weight=None):
                for half in range(2):
                    for d in range(2):
                        o, a = grow(dst + d)[:, 0, half], grow(src + d)[:, 0, half]
                        prev = grow(dst + d)[:, 0, 0]
                        w = a if weight is None else weight
                        if d:
                            o, a, w = o[:, ::-1], a[:, ::-1], w[:, ::-1]
                        start = first if half == 0 else (prev[:, 0:1] if d else prev[:, CTX - 1:CTX])
                        chain.step(v.tensor_tensor_scan(o, w, a, start, op0, op1))
                    chain.join()

            scan(6, 2, 0.0, ALU.mult, ALU.add, ones_row[:, :])
            lo(STARTS["oz"] + 2)
            v.tensor_tensor(rows2(0), rows2(0), rows2(6), ALU.subtract).then_inc(S("g_ready"), 1)
            dve.wait_ge(S("g_ready"), 1)
            scan(4, 0, 0.0, ALU.max, ALU.max)
            lo(STARTS["oz"] + 3)
            lat = lambda a: grow(a, 2)[:, :, 1, :]
            chain.step(v.tensor_tensor(grow(3)[:, 0], lat(4), lat(6), ALU.add))
            chain.step(v.tensor_scalar(grow(2)[:, 0], lat(4), -1.0, None, ALU.mult))
            chain.join()
            v.tensor_scalar(grow(3)[:, 0], grow(3)[:, 0], -88.0, None, ALU.max).then_inc(S("m_ready"), 1)
            for t in range(2, N_OZ):
                lo(STARTS["oz"] + t + 2)
            dve.wait_ge(S("gcol_done"), 1)
            v.tensor_copy(gcol[:, :, :, :].rearrange("p d t h -> p (d t h)"), ps[:, 4, 0:32])\
                .then_inc(S("gcol_ready"), 1)
            dve.wait_ge(S("gcol_ready"), 1)

            def mask_diagonals(hd):
                dve.wait_ge(S("spread_done"), hd + 1)
                if hd >= 2:
                    dve.wait_ge(S("den_done"), hd - 1)
                else:
                    dve.wait_ge(S("slot_done"), STARTS["ada1"])
                for n, (d, t, lo) in enumerate(((0, 2, 0), (0, 3, P), (1, 2, 0), (1, 3, P))):
                    ins = v.scalar_tensor_tensor(wexp[hd % 2][:, d, t, lo:lo + P], ps[:, 0, d * SEQ + lo:d * SEQ + lo + P],
                                                 gcol[:, d, t, hd:hd + 1], cc("mask_b" if d else "mask_f"),
                                                 ALU.add, ALU.add)
                    if n < 3:
                        chain.step(ins)
                ins.then_inc(S("diag_ready"), 1)

            def normalise(hd):
                w = wexp[hd % 2]
                dve.wait_ge(S("den_done"), hd + 1)
                r = em[hd % 2]
                chain.join()
                den = ps[:, 2, :].rearrange("p (d j) -> p d j", d=2)
                chain.step(v.scalar_tensor_tensor(r, den, -1.0, r, ALU.mult, ALU.max))
                chain.join()
                chain.step(v.tensor_tensor(r, den, r, ALU.max))
                chain.join()
                chain.step(v.reciprocal(r, r))
                chain.join()
                for d in range(2):
                    chain.step(v.tensor_tensor(w[:, d], w[:, d], wide(r[:, d, :], 4), ALU.mult))
                chain.join()
                v.tensor_tensor(scores[:, hd], w[:, 0], w[:, 1], ALU.add).then_inc(S("probs_ready"), 1)

            def centre(hd):
                dve.wait_ge(S("head_mean"), hd + 1)
                a = work(2 * (hd % 2))
                v.tensor_tensor(a, a, wide(ps[:, 3, 0:SEQ], HC), ALU.subtract).then_inc(S("head_centred"), 1)

            def weigh_scores(hd):
                dve.wait_ge(S("wexp_ready"), hd + 1)
                w = wexp[hd % 2]
                chain.step(v.tensor_tensor(w[:, 0], w[:, 0], scores[:, hd], ALU.mult))
                v.tensor_tensor(w[:, 1], w[:, 1], scores[:, hd], ALU.mult).then_inc(S("weighted_ready"), 1)
                dve.wait_ge(S("weighted_ready"), hd + 1)

            def finish_head(hd):
                a = work(2 * (hd % 2))
                c = slice(HC * hd, HC * hd + HC)
                dve.wait_ge(S("z_applied"), 4 * (hd + 1))
                dve.wait_ge(S("head_root"), hd + 1)
                chain.step(v.reciprocal(rstd[:, 0:SEQ], rstd[:, 0:SEQ]))
                chain.join()
                chain.step(v.tensor_tensor(a, a, wide(rstd[:, 0:SEQ], HC), ALU.mult))
                chain.join()
                chain.step(v.tensor_tensor(a, a, o_sb[:, c, :], ALU.mult))
                chain.join()
                chain.step(v.tensor_tensor(a, a, xconv[:, c, CTX:TOK], ALU.add))
                chain.join()
                v.tensor_copy(y_hi[:, c, :], a).then_inc(S("y_rounded"), 1)

            def rest_of_modulation():
                dve.wait_ge(S("ada_turned"), (N_ADA0 + N_ADA1) // 2)
                chain.step(v.tensor_tensor(modl[:, 2 * KD:6 * KD, :],
                                           ps[:, 7, 0:8 * KD].rearrange("p (m t) -> p m t", t=2),
                                           b_ada[:, 2 * KD:6 * KD, :], ALU.add))
                chain.join()
                v.scalar_tensor_tensor(scl[:, 2 * KD:3 * KD], modl[:, 4 * KD:5 * KD, 0], 1.0,
                                       vcol("norm_g1", 0, KD), ALU.add, ALU.mult).then_inc(S("mod1_ready"), 1)

            for n in range(HEADS):
                if n >= 1:
                    normalise(n - 1)
                mask_diagonals(n)
                if n >= 2:
                    centre(n - 2)
                weigh_scores(n)
                if n >= 2:
                    finish_head(n - 2)
            rest_of_modulation()
            normalise(HEADS - 1)
            centre(HEADS - 2)
            dve.wait_ge(S("lo_ready"), 2 * (STARTS["mout"] + 2))
            lo(STARTS["mout"] + 2)
            finish_head(HEADS - 2)
            centre(HEADS - 1)
            lo(STARTS["mout"] + 3)
            lo(STARTS["mout"] + 4)
            finish_head(HEADS - 1)
            lo(STARTS["mout"] + 5)
            for t in range(6, N_MOUT + 1):
                lo(STARTS["mout"] + t)

            def norm(name, gain, centred, n=KD, src=X, bias=None, split=True, late=None):
                dst = sq if src is X else src
                if centred:
                    dve.wait_ge(S("norm_mean"), since("mean", name) + 1)
                    for k in range(n):
                        v.tensor_tensor(src[:, k, :], src[:, k, :], mean_ps, ALU.subtract)\
                            .then_inc(S("norm_centred"), 1)
                if late is not None:
                    lo(late, halves=(1,))
                if centred:
                    dve.wait_ge(S("norm_centred"), since("centred", name) + n)
                dve.wait_ge(S("norm_root"), since("root", name) + 1)
                chain.step(v.reciprocal(rstd[:, 0:SEQ], rstd[:, 0:SEQ]))
                chain.join()
                for k in range(n + split):
                    if k < n:
                        v.scalar_tensor_tensor(dst[:, k, :], src[:, k, :], gain(k), rstd[:, 0:SEQ],
                                               ALU.mult, ALU.mult).then_inc(S("norm_scaled"), 1)
                    if split and k >= 1:
                        k -= 1
                        dve.wait_ge(S("norm_hi"), since("hi", name) + k + 1)
                        v.scalar_tensor_tensor(x_lo[:, k, :], sq[:, k, :], 0.0 if bias is None else bias(k),
                                               x_hi[:, k, :], ALU.add, ALU.subtract)\
                            .then_inc(S("norm_split"), 1)

            def residual(name, stage, index, term):
                for m in range(KD):
                    if m % 2 == 0:
                        if m < KD - 2:
                            dve.wait_ge(S("bank_summed"), 3 * index + m // 2 + 1)
                        else:
                            dve.wait_ge(S("slot_done"), STARTS[after[stage]])
                    term(m).then_inc(S("norm_in"), 1)
                lo(STARTS[after[stage]] + 1, halves=(0,))
                dve.wait_ge(S("norm_in"), since("in", name) + KD)

            def gated_term(block_at):
                return lambda m: v.scalar_tensor_tensor(X[:, m, :], acc[:, m, :],
                                                        modl[:, block_at + m, 0:1], X[:, m, :], ALU.mult, ALU.add)

            def scaled_term(m):
                return v.scalar_tensor_tensor(X[:, m, :], X[:, m, :], ALPHA, acc[:, m, :], ALU.mult, ALU.add)

            after = {"mout": "fin", "fout": "evin", "evout": "ffi0", "ffo0": "odin", "odout": "ffi1",
                     "ffo1": "end"}
            dve.wait_ge(S("mod1_ready"), 1)
            residual("rms1", "mout", 0, gated_term(2 * KD))
            norm("rms1", lambda k: scl[:, 2 * KD + k:2 * KD + k + 1], False,
                 bias=lambda k: modl[:, 3 * KD + k, 0:1], late=STARTS["fin"] + 1)
            for t in range(N_FIN):
                lo(STARTS["fin"] + t + 2)
                if t < 8:
                    dve.wait_ge(S("u_rounded"), t + 1)
                    v.tensor_tensor(g_lo[:, 2 * t:2 * t + 2, :], ps[:, t % 4, :].rearrange("p (b j) -> p b j", b=2),
                                    g_hi[:, 2 * t:2 * t + 2, :], ALU.subtract).then_inc(S("fin_moved"), 1)
                if t == 10:
                    dve.wait_ge(S("dft_rounded"), 1)
                    v.tensor_tensor(dft_parts[1], dft[:, :, :], dft_parts[0], ALU.subtract)\
                        .then_inc(S("dft_split"), 1)
            dve.wait_ge(S("fin_moved"), N_FIN)

            def rest_of_pq(g):
                for n in range(2):
                    dve.wait_ge(S("pq_rounded"), 2 * g + n + 1)
                    v.tensor_tensor(pq[1][:, g % 2, n, :], ps[:, 2 * (g % 2) + n, 0:DFT_C], pq[0][:, g % 2, n, :],
                                    ALU.subtract).then_inc(S("pq_moved"), 1)

            rest_of_pq(0)
            for g in range(GROUPS):
                if g + 1 < GROUPS:
                    rest_of_pq(g + 1)
                dve.wait_ge(S("f_done"), g + 1)
                a = zf[:, 2 * g:2 * g + 2, :]
                v.tensor_tensor(a, ps[:, 4 + g % 4, :].rearrange("p (c j) -> p c j", c=2), a, ALU.mult)\
                    .then_inc(S("f_moved"), 1)
                dve.wait_ge(S("f_moved"), g + 1)
                v.tensor_copy(g_hi[:, 2 * g:2 * g + 2, :], a).then_inc(S("fy_rounded"), 1)
            units(N_FOUT, "fout")
            residual("rmsf", "fout", 1, gated_term(5 * KD))
            norm("rmsf", lambda k: vcol("norm_f", k), False, late=STARTS["evin"] + 1)

            dve.wait_ge(S("vec2_ready"), 16)
            def sums(steps):
                for n in steps:
                    a, b = (pad_a, pad_b, pad_c, pad_b)[n], (pad_b, pad_c, pad_b, pad_c)[n]
                    chain.join()
                    chain.step(v.tensor_tensor(b[:, n:, 32:], a[:, n:, 32:],
                                               a[:, n:, 32 - (1 << n):32 - (1 << n) + SEQ], ALU.add))

            def pooled(groups):
                for g in groups:
                    w, b = WINDOWS[g], (pad_b, pad_c)[g % 2]
                    chain.step(v.scalar_tensor_tensor(h2[:, g, :], b[:, g, 32:], 1.0 / w, pad_a[:, g, 32:],
                                                      ALU.mult, ALU.subtract))
                chain.join()
                for g in groups:
                    w, b = WINDOWS[g], (pad_b, pad_c)[g % 2]
                    chain.step(v.tensor_tensor(h2[:, g, 0:w], b[:, g, 32:32 + w], cc("count", 16 * g, 16 * g + w),
                                               ALU.mult))
                for g in groups:
                    w = WINDOWS[g]
                    chain.join()
                    v.tensor_tensor(h2[:, g, 0:w], h2[:, g, 0:w], pad_a[:, g, 32:32 + w], ALU.subtract)\
                        .then_inc(S("pooled_ready"), 1)

            def convolve(t):
                dve.wait_ge(S("evin_moved"), t + 3)
                chain.step(v.tensor_tensor(pad_d[:, t, 32:], U[:, 2 * t, :], U[:, 2 * t + 1, :], ALU.mult))

            def taps():
                chain.join()
                for t in range(KH):
                    chain.step(v.tensor_scalar(U[:, t, :], pad_d[:, t, 30:30 + SEQ], vcol("ev_conv", 3 * t), None,
                                               ALU.mult))
                for k in (1, 2):
                    for t in range(KH):
                        chain.join(KH - 1)
                        chain.step(v.scalar_tensor_tensor(U[:, t, :], pad_d[:, t, 30 + k:30 + k + SEQ],
                                                          vcol("ev_conv", 3 * t + k), U[:, t, :],
                                                          ALU.mult, ALU.add))

            def pool_out():
                dve.wait_ge(S("pool_done"), 1)
                for g in range(KH):
                    chain.step(v.tensor_scalar(U[:, 3 * KH + g, :],
                                               ps[:, 4 + g // 2, (g % 2) * SEQ:(g % 2 + 1) * SEQ],
                                               vcol("pool_s", g), None, ALU.mult))
                    chain.join()
                    v.tensor_copy(g_hi[:, g, :], U[:, 3 * KH + g, :]).then_inc(S("evmix_rounded"), 1)

            for t in range(N_EVIN):
                if t == N_EVIN - 1:
                    pool_out()
                lo(STARTS["evin"] + t + 2)
                if t == 2:
                    dve.wait_ge(S("pads_clear"), 4)
                    dve.wait_ge(S("evin_moved"), 2)
                    sums((0, 1))
                if t == 3:
                    sums((2, 3))
                if t == 4:
                    chain.join()
                    pooled((0, 1))
                    convolve(0)
                if t == 5:
                    pooled((2, 3))
                    convolve(1)
                if t == 6:
                    convolve(2)
                    convolve(3)
            taps()
            dve.wait_ge(S("evin_moved"), N_EVIN)
            for t in range(KH):
                chain.join(KH - 1)
                chain.step(v.tensor_tensor(U[:, t, :], U[:, t, :], U[:, 2 * KH + t, :], ALU.mult))
            for t in range(KH):
                chain.join(KH - 1 - t)
                v.tensor_copy(g_hi[:, KH + t, :], U[:, t, :]).then_inc(S("evmix_rounded"), 1)
            units(N_EVOUT, "evout")
            residual("mix0", "evout", 2, scaled_term)
            norm("mix0", lambda k: vcol("mix_g0", k), True, bias=lambda k: vcol("mix_b0", k),
                 late=STARTS["ffi0"] + 1)

            def feed_forward(l):
                def gating(t, u):
                    dve.wait_ge(S("gate_ready"), t + (N_FFI * l + 1))
                    if not isinstance(t, int) or t >= 4:
                        dve.wait_ge(S("ffi_split"), t + (N_FFI * l - 3))
                    v.tensor_tensor(gated[:, u, :], gate[:, u % 2, :], ps[:, u, SEQ:2 * SEQ], ALU.mult)\
                        .then_inc(S("ffi_moved"), 1)
                    dve.wait_ge(S("ffi_moved"), t + (N_FFI * l + 1))
                    v.tensor_copy(g_hi[:, t, :], gated[:, u, :]).then_inc(S("ffi_rounded"), 1)
                units(N_FFI, f"ffi{l}", gating)
                units(N_FFO, f"ffo{l}")
                residual(f"ffn{l}", f"ffo{l}", 3 + 2 * l, scaled_term)
                norm(f"ffn{l}", lambda k: vcol(f"ffn_g{l}", k), True, bias=lambda k: vcol(f"ffn_b{l}", k),
                     split=l == 0, late=STARTS[after[f"ffo{l}"]] + 1)

            feed_forward(0)

            chain.step(v.memset(frow[:, 4, :], 1.0))

            def gated_unit(t):
                dve.wait_ge(S("glu_ready"), t + 1)
                v.tensor_tensor(pad_a[:, t, 32:], gate[:, t % 2, :], ps[:, t, 0:SEQ], ALU.mult)\
                    .then_inc(S("odin_moved"), 1)

            def taps(k, pair):
                for t in pair:
                    chain.join(1)
                    chain.step(v.scalar_tensor_tensor(acc31[:, t, :], pad_a[:, t, bass.ds(k + 2, SEQ)],
                                                      vcol("dw_w", k * KH + t), acc31[:, t, :],
                                                      ALU.mult, ALU.add))

            def looped_taps(k0, pair):
                with dve.Fori(0, 2) as i:
                    chain.enter(i, 2 * 7)
                    for k in range(7):
                        taps(i * 7 + (k0 + k), pair)
                chain.leave(2)

            for pair in ((0, 1), (2, 3)):
                for t in pair:
                    if t < 2:
                        gated_unit(t)
                    dve.wait_ge(S("odin_moved"), t + 1)
                    chain.step(v.tensor_scalar(acc31[:, t, :], pad_a[:, t, 2:2 + SEQ], vcol("dw_w", t),
                                               vcol("dw_b", t), ALU.mult, ALU.add))
                looped_taps(1, pair)
                if pair[0] == 0:
                    gated_unit(2)
                    gated_unit(3)
                    dve.wait_ge(S("forget_done"), 1)
                    v.tensor_scalar(frow[:, 0, :], ps[0:FH, 4, 0:SEQ], rows[0:FH, 4:5], None, ALU.add)\
                        .then_inc(S("forget_moved"), 1)
                looped_taps(15, pair)
                taps(TAPS - 2, pair)
                chain.join()
                for t in pair:
                    v.scalar_tensor_tensor(acc31[:, t, :], pad_a[:, t, TAPS + 1:TAPS + 1 + SEQ],
                                           vcol("dw_w", (TAPS - 1) * KH + t), acc31[:, t, :],
                                           ALU.mult, ALU.add).then_inc(S("norm_in"), 1)
                if pair[0] == 0:
                    dve.wait_ge(S("forget_log"), 1)
                    chain.step(v.scalar_tensor_tensor(frow[:, 0, :], frow[:, 0, :], 0.0, frow[:, 1, :],
                                                      ALU.min, ALU.subtract))
                    chain.join()
                    chain.step(v.tensor_tensor_scan(frow[:, 2, :], frow[:, 4, :], frow[:, 0, :], 0.0,
                                                    ALU.mult, ALU.add))
                    chain.join()
                    v.tensor_scalar(frow[:, 3, :], frow[:, 2, :], -float(FD) ** 0.5, None, ALU.mult)\
                        .then_inc(S("cum_ready"), 1)

            dve.wait_ge(S("norm_mean"), since("mean", "conv") + 1)
            for k in range(KH):
                v.tensor_tensor(acc31[:, k, :], acc31[:, k, :], ps[:, 4, 0:SEQ], ALU.subtract)\
                    .then_inc(S("norm_centred"), 1)
            dve.wait_ge(S("norm_centred"), since("centred", "conv") + KH)

            def masked(hd):
                dve.wait_ge(S("logits_done"), hd + 1)
                a = ps[:, (hd + 2) % 4, :]
                chain.step(v.tensor_tensor(logit[:, hd, 0, 0:P], a[:, 0:P], cc("mask_b"), ALU.add))
                chain.step(v.tensor_tensor(logit[:, hd, 1, P:SEQ], a[:, 3 * P:4 * P], cc("mask_b"), ALU.add))
                v.tensor_copy(logit[:, hd, 1, 0:P], a[:, 2 * P:3 * P]).then_inc(S("logits_moved"), 1)

            def maximum(hd):
                dve.wait_ge(S("logits_moved"), hd + 1)
                chain.step(v.tensor_reduce(stat[:, 0, 2 * hd:2 * hd + 2], logit[:, hd, :, :], AX.X, ALU.max))
                chain.join()
                v.tensor_scalar(stat[:, 1, 2 * hd:2 * hd + 2], stat[:, 0, 2 * hd:2 * hd + 2], -FD ** -0.5, None,
                                ALU.mult).then_inc(S("max_ready"), 1)

            dve.wait_ge(S("logit_clear"), 1)
            chain.join()
            for hd in range(FH):
                masked(hd)
                if hd >= 1:
                    chain.join()
                    maximum(hd - 1)
                if hd == 2:
                    dve.wait_ge(S("norm_root"), since("root", "conv") + 1)
                    chain.step(v.reciprocal(rstd[:, 0:SEQ], rstd[:, 0:SEQ]))
                    chain.join()
                    for k in range(KH):
                        v.scalar_tensor_tensor(acc31[:, k, :], acc31[:, k, :], vcol("cn_g", k), rstd[:, 0:SEQ],
                                               ALU.mult, ALU.mult).then_inc(S("norm_scaled"), 1)
                if hd == 6:
                    for k in range(KH):
                        dve.wait_ge(S("conv_hi"), k + 1)
                        dve.wait_ge(S("conv_whole"), k + 1)
                        v.tensor_tensor(g_lo[:, k, :], sq[:, k, :], g_hi[:, k, :], ALU.subtract)\
                            .then_inc(S("conv_split"), 1)
            chain.join()
            maximum(FH - 1)
            for hd in range(FH):
                dve.wait_ge(S("exp_ready"), hd + 1)
                r = stat[:, 2, 2 * hd:2 * hd + 2]
                chain.step(v.reciprocal(r, r))
                chain.join()
                chain.step(v.tensor_scalar(logit[:, hd, 0, :], logit[:, hd, 0, :], r[:, 0:1], None, ALU.mult))
                v.tensor_scalar(logit[:, hd, 1, :], logit[:, hd, 1, :], r[:, 1:2], None, ALU.mult)\
                    .then_inc(S("prob_ready"), 1)
            dve.wait_ge(S("lo_ready"), 2 * (STARTS["odout"] + 2))
            lo(STARTS["odout"] + 2)
            lo(STARTS["odout"] + 3)
            for c in range(KH):
                dve.wait_ge(S("attn_done"), 2 * c + 2)
                v.tensor_copy(gated[:, c, :], ps[:, 2 + c % 2, 0:SEQ]).then_inc(S("attn_moved"), 1)
                dve.wait_ge(S("attn_moved"), c + 1)
                v.tensor_copy(g_hi[:, KH + c, :], gated[:, c, :]).then_inc(S("attn_rounded"), 1)
            lo(STARTS["ffi1"])
            residual("mix1", "odout", 4, scaled_term)
            norm("mix1", lambda k: vcol("mix_g1", k), True, bias=lambda k: vcol("mix_b1", k),
                 late=STARTS["ffi1"] + 1)
            feed_forward(1)


def _columns(a):
    a = np.asarray(a)
    return np.moveaxis(a.reshape(*a.shape[:-1], -1, P), -1, 0)


def _wide_slots(w, order=None):
    blocks = w.reshape(KD, P, -1, P)
    if order is not None:
        blocks = blocks[:, :, order]
    k, p, n, c = blocks.shape
    return blocks.reshape(k, p, n // 2, 2 * c).transpose(2, 1, 0, 3).reshape(n // 2, P, SLOT)


def _deep_slots(w):
    n = w.shape[0] // (2 * P)
    return w.reshape(n, 2, P, D).transpose(0, 2, 1, 3).reshape(n, P, SLOT)


def _by_feature(x):
    return np.ascontiguousarray(x[0].T.reshape(KD, P, -1).transpose(1, 0, 2))


def _stream(a):
    order = np.concatenate([np.arange(P), np.arange(GD - 1, P - 1, -1)])
    order = (np.arange(GROUPS)[:, None] * GD + order).reshape(-1)
    f_in = a["f_w_in"][0][:, np.concatenate([np.arange(E), E + order])]
    pairs = lambda n: [b for t in range(n) for b in (t, n + t)]
    ada = [_wide_slots(a["w_ada"][l]) for l in range(2)]
    w_in = _wide_slots(a["m_w_in"][0])
    heads = np.stack([a["m_w_q"][0], a["m_w_k"][0]], axis=1).reshape(2 * HEADS, HC, P, DH)
    od = a["od_w_in_2"][0]
    od_cols = np.concatenate([od[:, 3 * HALF + FH:], od[:, :3 * HALF]], axis=1)
    parts = [ada[0][:8], w_in[:8], heads.transpose(0, 2, 1, 3).reshape(-1, P, SLOT), w_in[8:], ada[0][8:],
             ada[1], _deep_slots(a["m_w_out"][0]), _wide_slots(f_in), _deep_slots(a["f_w_out"][0][order]),
             _wide_slots(a["ev_w_in_2"][0], [12, 13, 14, 15, 4, 8, 5, 9, 6, 10, 7, 11, 0, 1, 2, 3]),
             _deep_slots(np.roll(a["ev_w_out_2"][0], HALF, axis=0)),
             _wide_slots(a["ffn_w_in_2"][0], pairs(KF)), _deep_slots(a["ffn_w_out_2"][0]),
             _wide_slots(od_cols, pairs(KH) + list(range(2 * KH, 5 * KH))), _deep_slots(np.roll(a["od_w_out_2"][0], HALF, axis=0)),
             _wide_slots(a["ffn_w_in_2"][1], pairs(KF)), _deep_slots(a["ffn_w_out_2"][1])]
    return np.concatenate(parts)


def _vectors(a):
    od = a["od_w_in_2"][0]
    parts = {
        "c": np.stack([_columns(a["c"][0]), _columns(a["c_ctx"])], axis=-1),
        "norm_g0": _columns(a["norm_g"][0]), "norm_g1": _columns(a["norm_g"][1]),
        "norm_f": _columns(a["norm_f"]), "b_ada": _columns(a["b_ada"]),
        "conv_w": _columns(a["m_conv_w"][0, :, :, 0].reshape(9, E)).transpose(0, 2, 1),
        "conv_b": _columns(a["m_conv_b"][0]), "ln_w": _columns(a["m_ln_w"][0]),
        "skip": _columns(a["m_skip"][0]),
        "gate_w": a["m_w_if"][0].transpose(1, 2, 0, 3).reshape(3 * KE, P, 16).transpose(1, 0, 2),
        "ev_conv": _columns(a["ev_conv_w_2"][0]).transpose(0, 2, 1),
        "pool_s": _columns(a["ev_pool_scale_2"][0]), "pool_w": a["ev_pool_w_2"][0].transpose(1, 0, 2),
        "dw_w": _columns(a["od_dw_w_2"][0]), "dw_b": _columns(a["od_dw_b_2"][0]),
        "cn_g": _columns(a["od_cn_g_2"][0]), "cn_b": _columns(a["od_cn_b_2"][0]),
        "forget_w": od[:, 3 * HALF:3 * HALF + FH].reshape(KD, P, FH).transpose(1, 0, 2),
    }
    for l in range(2):
        for k, n in (("mix", "ln_mix"), ("ffn", "ln_ffn")):
            parts[f"{k}_g{l}"] = _columns(a[f"{n}_g_2"][l])
            parts[f"{k}_b{l}"] = _columns(a[f"{n}_b_2"][l])
    return [np.concatenate([parts[k].reshape(P, table[k][1]) for k in table], axis=1) for table in (VEC, VEC2)]


def _constants():
    c = np.zeros((P, CSTS), np.float32)
    i, j = np.arange(P)[:, None], np.arange(P)[None, :]

    def put(name, value, rows=P):
        a, n = CST[name]
        c[:rows, a:a + n] = value
    put("ident", i == j)
    put("mask_f", np.where(i <= j, 0.0, NEG))
    put("mask_b", np.where(i >= j, 0.0, NEG))
    put("count", np.concatenate([1.0 / np.minimum(np.arange(16) + 1, w) for w in WINDOWS])[None])
    put("fold", np.tile(np.eye(2), (2, 1)), 4)
    put("fold_gates", np.tile(np.eye(16), (2, 1)), 32)
    put("select", np.repeat(np.eye(HEADS), P, axis=1), HEADS)
    return c


def _dft():
    a = 2 * np.pi * (np.outer(np.arange(SEQ), np.arange(SEQ)) % SEQ) / SEQ
    t = np.concatenate([np.cos(a[:, :DFT_H]), -np.sin(a[:, :DFT_H]), np.cos(a), -np.sin(a), np.sin(a)], axis=1) / 16
    return np.ascontiguousarray(t.reshape(2, P, -1).transpose(1, 0, 2), np.float32)


def kernel(**inputs):
    import concourse.bacc as bacc
    from concourse.bass_utils import run_bass_kernel_spmd

    a = {k: np.asarray(v) for k, v in inputs.items()}
    rows = np.zeros((FH, 8), np.float32)
    rows[:HEADS, 0:4] = np.stack([a["m_b_i"][0, 0], a["m_b_f"][0, 0], a["m_b_i"][0, 1], a["m_b_f"][0, 1]], axis=1)
    rows[:, 4] = a["od_forget_b_2"][0]
    vectors, vectors2 = _vectors(a)
    select = np.repeat(np.eye(FH, dtype=np.float32), P, axis=1).reshape(FH, FH, P)
    arrays = {"weights": _stream(a), "x": _by_feature(a["x"]), "ctx": _by_feature(a["ctx"]),
              "vectors": vectors, "vectors2": vectors2, "constants": _constants(), "dft": _dft(),
              "select": select, "rows": rows}
    nc = bacc.Bacc("TRN2", target_bir_lowering=False, num_devices=1)
    args = [nc.dram_tensor(f"in_{k}", v.shape, F32, kind="ExternalInput").ap() for k, v in arrays.items()]
    result = nc.dram_tensor("result", (P, KD, SEQ), F32, kind="ExternalOutput").ap()
    program(nc, *args, result)
    r = run_bass_kernel_spmd(nc, [{f"in_{k}": np.ascontiguousarray(v) for k, v in arrays.items()}], core_ids=[0])
    y = np.asarray(r.results[0]["result"])
    return np.ascontiguousarray(y.transpose(2, 1, 0).reshape(1, SEQ, D))
```
